# Optimizing a Trainium2 kernel written in Bass

```python
import jax, jax.numpy as jnp
from jax import lax
import numpy as np

D_MODEL = 1024
BATCH = 1
SEQ = 2048
DEPTH = 1

MEM_LEN = 256
GLA_HEADS = 4
GLA_DK = D_MODEL // 16
GLA_DV = D_MODEL // 8
GLA_KW = GLA_HEADS * GLA_DK
GLA_WIDTH = GLA_HEADS * GLA_DV
GLA_GATE_RANK = 16
GLA_TAU = 16.0
GLA_CHUNK = 64
CONV_CH = D_MODEL // 4
CONV_WIDTH = 3
XA_HEADS = 4
XA_DH = D_MODEL // 16
XA_WIDTH = XA_HEADS * XA_DH
MIX_WIDTH = GLA_WIDTH + CONV_CH + XA_WIDTH
IN_SIZES = (GLA_KW, GLA_KW, GLA_WIDTH, GLA_WIDTH, GLA_GATE_RANK,
            CONV_CH, CONV_CH, CONV_CH, XA_WIDTH)
IN_COLS = sum(IN_SIZES)
D_FF = 4 * D_MODEL
LN_EPS = 1e-5
RMS_EPS = 1e-6

kernel_name = "hybrid_gla_shortconv_memxattn_deepnorm"

def layer_norm(x, g, b):
    xf = x.astype(jnp.float32)
    mu = jnp.mean(xf, axis=-1, keepdims=True)
    var = jnp.mean(jnp.square(xf - mu), axis=-1, keepdims=True)
    y = (xf - mu) * lax.rsqrt(var + LN_EPS)
    return (y * g.astype(jnp.float32) + b.astype(jnp.float32)).astype(x.dtype)

def rms_norm(x, g):
    xf = x.astype(jnp.float32)
    y = xf * lax.rsqrt(jnp.mean(jnp.square(xf), axis=-1, keepdims=True) + RMS_EPS)
    return y * g.astype(jnp.float32)

def gla_chunked(q, k, v, log_a):
    B, S, H, dk = q.shape
    dv = v.shape[-1]
    C = GLA_CHUNK
    N = S // C

    def to_chunks(t):
        return t.astype(jnp.float32).reshape(B, N, C, H, t.shape[-1]).transpose(1, 0, 3, 2, 4)

    qc, kc, vc, ac = to_chunks(q), to_chunks(k), to_chunks(v), to_chunks(log_a)
    causal = jnp.tril(jnp.ones((C, C), dtype=bool))

    def step(state, inp):
        q_, k_, v_, a_ = inp
        b = jnp.cumsum(a_, axis=2)
        o_inter = jnp.einsum('bhck,bhkv->bhcv', q_ * jnp.exp(b), state)
        diff = b[:, :, :, None, :] - b[:, :, None, :, :]
        decay = jnp.exp(jnp.where(causal[:, :, None], diff, -jnp.inf))
        scores = jnp.einsum('bhik,bhjk,bhijk->bhij', q_, k_, decay)
        o_intra = jnp.einsum('bhij,bhjv->bhiv', scores, v_)
        b_last = b[:, :, -1:, :]
        k_dec = k_ * jnp.exp(b_last - b)
        state = (jnp.exp(b_last[:, :, 0, :])[..., None] * state
                 + jnp.einsum('bhck,bhcv->bhkv', k_dec, v_))
        return state, o_inter + o_intra

    s0 = jnp.zeros((B, H, dk, dv), jnp.float32)
    _, o = lax.scan(step, s0, (qc, kc, vc, ac))
    return o.transpose(1, 0, 3, 2, 4).reshape(B, S, H, dv)

def causal_short_conv(u, w):
    width = w.shape[0]
    S = u.shape[1]
    up = jnp.pad(u, ((0, 0), (width - 1, 0), (0, 0)))
    return sum(up[:, i:i + S, :] * w[i] for i in range(width))

def memory_cross_attention(q, mk, mv):
    s = jnp.einsum('bshd,bmhd->bhsm', q, mk).astype(jnp.float32) * (q.shape[-1] ** -0.5)
    p = jax.nn.softmax(s, axis=-1).astype(mv.dtype)
    return jnp.einsum('bhsm,bmhd->bshd', p, mv)

def hybrid_mixer(h, mem, w_in, w_gate_up, b_gate, conv_w, gla_norm_g, w_mem_kv, w_out):
    B, S, _ = h.shape
    z = h @ w_in
    offsets = [int(o) for o in np.cumsum(IN_SIZES)[:-1]]
    q, k, v, g, a_low, c_b, c_c, c_h, xq = jnp.split(z, offsets, axis=-1)

    q = q.reshape(B, S, GLA_HEADS, GLA_DK) * (GLA_DK ** -0.5)
    k = k.reshape(B, S, GLA_HEADS, GLA_DK)
    v = v.reshape(B, S, GLA_HEADS, GLA_DV)
    log_a = jax.nn.log_sigmoid((a_low @ w_gate_up + b_gate).astype(jnp.float32)) / GLA_TAU
    log_a = log_a.reshape(B, S, GLA_HEADS, GLA_DK)
    o = gla_chunked(q, k, v, log_a)
    o = rms_norm(o, gla_norm_g).astype(h.dtype)
    y_gla = (o * jax.nn.silu(g.reshape(B, S, GLA_HEADS, GLA_DV))).reshape(B, S, GLA_WIDTH)

    y_conv = c_b * causal_short_conv(c_c * c_h, conv_w)

    M = mem.shape[1]
    mk, mv = jnp.split(mem @ w_mem_kv, 2, axis=-1)
    y_xa = memory_cross_attention(xq.reshape(B, S, XA_HEADS, XA_DH),
                                  mk.reshape(B, M, XA_HEADS, XA_DH),
                                  mv.reshape(B, M, XA_HEADS, XA_DH)).reshape(B, S, XA_WIDTH)

    return jnp.concatenate([y_gla, y_conv, y_xa], axis=-1) @ w_out

def setup_inputs(seed: int = 0) -> dict:
    key = jax.random.key(seed)
    ks = jax.random.split(key, 20)
    f32 = jnp.float32
    beta = (8.0 * DEPTH) ** -0.25

    def nrm(k, shape, scale):
        return jax.random.normal(k, shape, f32) * scale

    L = DEPTH
    return {
        "x": jax.random.normal(ks[0], (BATCH, SEQ, D_MODEL), f32),
        "mem": jax.random.normal(ks[1], (BATCH, MEM_LEN, D_MODEL), f32),
        "w_in": nrm(ks[2], (L, D_MODEL, IN_COLS), D_MODEL ** -0.5),
        "w_gate_up": nrm(ks[3], (L, GLA_GATE_RANK, GLA_KW), GLA_GATE_RANK ** -0.5),
        "b_gate": nrm(ks[4], (L, GLA_KW), 0.1),
        "conv_w": nrm(ks[5], (L, CONV_WIDTH, CONV_CH), CONV_WIDTH ** -0.5),
        "gla_norm_g": 1.0 + nrm(ks[6], (L, GLA_DV), 0.02),
        "w_mem_kv": nrm(ks[7], (L, D_MODEL, 2 * XA_WIDTH), D_MODEL ** -0.5),
        "w_out": nrm(ks[8], (L, MIX_WIDTH, D_MODEL), beta * MIX_WIDTH ** -0.5),
        "ln1_g": 1.0 + nrm(ks[9], (L, D_MODEL), 0.02),
        "ln1_b": nrm(ks[10], (L, D_MODEL), 0.02),
        "w_ff1": nrm(ks[11], (L, D_MODEL, D_FF), D_MODEL ** -0.5),
        "w_ff2": nrm(ks[12], (L, D_FF, D_MODEL), beta * D_FF ** -0.5),
        "ln2_g": 1.0 + nrm(ks[13], (L, D_MODEL), 0.02),
        "ln2_b": nrm(ks[14], (L, D_MODEL), 0.02),
    }

def reference(x, mem, w_in, w_gate_up, b_gate, conv_w, gla_norm_g, w_mem_kv, w_out,
              ln1_g, ln1_b, w_ff1, w_ff2, ln2_g, ln2_b):
    alpha = (2.0 * DEPTH) ** 0.25
    for l in range(DEPTH):
        mix = hybrid_mixer(x, mem, w_in[l], w_gate_up[l], b_gate[l], conv_w[l],
                           gla_norm_g[l], w_mem_kv[l], w_out[l])
        x = layer_norm(alpha * x + mix, ln1_g[l], ln1_b[l])
        ff = jnp.square(jax.nn.relu(x @ w_ff1[l])) @ w_ff2[l]
        x = layer_norm(alpha * x + ff, ln2_g[l], ln2_b[l])
    return x


_drawn_inputs = setup_inputs


def setup_inputs(seed=0):
    import zlib

    import numpy as np

    out = dict(_drawn_inputs(seed))
    spreads = {}
    factors = {'b_gate': 6.1,
     'gla_norm_g': 22.899,
     'ln1_g': 2.734,
     'ln1_b': 2.766,
     'ln2_g': 7.522,
     'ln2_b': 7.883,
     'mem': 3.957,
     'w_mem_kv': 3.886}
    for name, (base, spread) in spreads.items():
        noise = np.random.default_rng([zlib.crc32(name.encode()), seed]).standard_normal(out[name].shape)
        drawn = base * np.exp(spread * noise) if base else spread * noise
        out[name] = __import__('jax').numpy.asarray(drawn.astype(out[name].dtype))
    for name, factor in factors.items():
        out[name] = (out[name] * factor).astype(out[name].dtype)
    return out
```

```python
from contextlib import ExitStack

import concourse.bass as bass
from concourse import mybir

F32 = mybir.dt.float32
F32R = mybir.dt.float32r
U8 = mybir.dt.uint8
ALU = mybir.AluOpType
ACT = mybir.ActivationFunctionType
AX_X = mybir.AxisListType.X

P = 128
BLK = 512
CH = 128
NCH = BLK // CH
LEVELS = [1, 2, 4, 8, 16, 32, 64]
DK, DV, HEADS = 64, 128, 4
RANK = 16
LN_EPS, RMS_EPS = 1e-5, 1e-6
ALPHA = 2.0 ** 0.25
TAU = 16.0
RAW = 2
RING = 4

J_OUT, J_Q, J_V, J_XQ = 0, 8, 12, 16
J_C0, J_H0, J_G0, J_G1, J_B0, J_C1, J_H1, J_B1, J_G2, J_G3 = range(18, 28)
GATE_TILE = [J_G0, J_G1, J_G2, J_G3]
SC_USES, OB_USES, AUX_USES = 20, 12, 23
ACT_STEPS_FIRST, ACT_STEPS = 4, 8
DVE_STEPS_FIRST, DVE_STEPS = 154, 162
K_ORDER = [0, 2, 3, 1]


def three_products(pe):
    def three(dst, a_hi, a_lo, b_hi, b_lo, first, last):
        pe.matmul(dst, a_hi, b_lo, start=first, stop=False)
        pe.matmul(dst, a_lo, b_hi, start=False, stop=False)
        return pe.matmul(dst, a_hi, b_hi, start=False, stop=last)
    return three


def hybrid_layer(nc, x, mem, w_in, w_gate_up, b_gate, conv_w, gla_norm_g, w_mem_kv, w_out,
                 ln1_g, ln1_b, w_ff1, w_ff2, ln2_g, ln2_b, normed, out):
    S, D = x.shape[1], x.shape[2]
    KT = D // P
    NBLK = S // BLK
    DFF = w_ff1.shape[2]
    M = mem.shape[1]
    HALF = S // 2
    NT = HALF // P
    NFB = DFF // (2 * P)
    assert (KT, NBLK, M) == (8, 4, 256)

    x_rows = x[0]
    out_rows = out[0]
    win_v = w_in[0].rearrange("(k p) n -> p k n", p=P)
    wout_v = w_out[0].rearrange("(k p) n -> p k n", p=P)
    wkv_v = w_mem_kv[0].rearrange("(k p) n -> p k n", p=P)
    w1_v = w_ff1[0].rearrange("(k p) n -> p k n", p=P)
    w2_rows = w_ff2[0]
    COL_Q, COL_V, COL_G = 0, 512, 1024
    COL_LOW = 1536
    COL_B, COL_C, COL_H, COL_XQ = 1552, 1808, 2064, 2320
    SLOT_COL = {J_Q: 0, J_Q + 1: 128, J_Q + 2: 256, J_Q + 3: 384, J_XQ: COL_XQ, J_XQ + 1: COL_XQ + 128,
                J_C0: COL_C, J_H0: COL_H, J_B0: COL_B, J_C1: COL_C + 128, J_H1: COL_H + 128, J_B1: COL_B + 128,
                J_G0: COL_G, J_G1: COL_G + 128, J_G2: COL_G + 256, J_G3: COL_G + 384}

    def slot_source(j):
        if j < J_Q:
            k = 2 * K_ORDER[j % 4]
            return wout_v[:, k:k + 2, 512 * (j // 4):512 * (j // 4) + 512]
        if J_V <= j < J_XQ:
            return win_v[:, 2 * (j - J_V):2 * (j - J_V) + 2, COL_V:COL_V + 512]
        return win_v[:, :, SLOT_COL[j]:SLOT_COL[j] + P]

    with ExitStack() as ctx:
        def sb(name, shape, dt=F32):
            return ctx.enter_context(nc.sbuf_tensor(name, shape, dt))

        def sem(name):
            return ctx.enter_context(nc.semaphore(name))

        raw = sb("raw", [P, RAW, 1024])
        w_hi = sb("w_hi", [P, RING, 1024], F32R)
        w_lo = sb("w_lo", [P, RING, 1024], F32R)
        rows = sb("rows", [P, 4, D])
        xT_hi = sb("xT_hi", [P, KT, BLK], F32R)
        xT_lo = sb("xT_lo", [P, KT, BLK], F32R)
        y_hi = sb("y_hi", [P, KT, BLK], F32R)
        y_lo = sb("y_lo", [P, KT, BLK], F32R)
        qT = sb("qT", [P, 2, BLK])
        kT = sb("kT", [P, 2, BLK])
        v_rows = sb("v_rows", [P, NCH, HEADS * DV])
        xqT = sb("xqT", [P, 2, BLK])
        u = sb("u", [P, 2, BLK + 2])
        gate = sb("gate", [P, 2, BLK])
        k_dec = sb("k_dec", [P, BLK])
        b_last = sb("b_last", [P, NCH])
        decay_last = sb("decay_last", [P, NCH])
        k_lev = sb("k_lev", [P, 5, BLK])
        k_top = sb("k_top", [P, NCH, 64])
        q_lev = sb("q_lev", [P, 7, BLK // 2])
        q_dec = sb("q_dec", [P, BLK])
        probs = sb("probs", [P, 2, CH])
        k_dec_rows = sb("k_dec_rows", [P, P])
        state = sb("state", [P, 2, 2, DV])
        oT = sb("oT", [P, 2, BLK])
        rr = sb("rr", [P, 2, BLK])
        gin = sb("gin", [P, 2, BLK])
        y_raw = sb("y_raw", [P, 2, BLK])
        xp = sb("xp", [P, 4, M])
        xpT = sb("xpT", [P, 2, 4 * P])
        mkT = sb("mkT", [P, 2, M])
        mv = sb("mv", [P, 2, 256])
        masks = sb("masks", [P, 6, 64], U8)
        ident = sb("ident", [P, P])
        ones = sb("ones", [P, P])
        mean_w = sb("mean_w", [P, P])
        low_hi = sb("low_hi", [P, KT, RANK], F32R)
        low_lo = sb("low_lo", [P, KT, RANK], F32R)
        w_gate = sb("w_gate", [RANK, 256])
        gate_bias = sb("gate_bias", [P, 2])
        rms_g = sb("rms_g", [P, 1])
        taps = sb("taps", [P, 2, 3])
        eps_rms = sb("eps_rms", [P, 1])
        eps_ln = sb("eps_ln", [P, 1])
        stats = sb("stats", [P, 4, 2, 6])
        mvar = sb("mvar", [P, 4, 2])
        rstd = sb("rstd", [P, 4])
        xmax = sb("xmax", [P, 4])
        xnmax = sb("xnmax", [P, 4])
        xsum = sb("xsum", [P, 4])
        xrec = sb("xrec", [P, 4])
        lowT = y_raw[0:RANK, 1, :]
        low_raw = gin[:, 0, 0:KT * RANK].rearrange("p (k n) -> p k n", k=KT)
        mask_f = gin[:, 1, 0:384].rearrange("p (l n) -> p l n", l=6)

        main = [ctx.enter_context(nc.psum_tensor(f"main{i}", [P, 512], F32)) for i in range(RING)]
        sc = [ctx.enter_context(nc.psum_tensor(f"sc{i}", [P, 512], F32)) for i in range(2)]
        ob = ctx.enter_context(nc.psum_tensor("ob", [P, 512], F32))
        aux = ctx.enter_context(nc.psum_tensor("aux", [P, 512], F32))

        raw_landed = [sem(f"raw_landed{i}") for i in range(RAW)]
        hi_done, lo_done, row_used = sem("hi_done"), sem("lo_done"), sem("row_used")
        main_done = sem("main_done")
        main_free = [sem(f"main_free{i}") for i in range(RING)]
        sc_done = [sem(f"sc_done{i}") for i in range(2)]
        sc_free = [sem(f"sc_free{i}") for i in range(2)]
        ob_done, ob_free = sem("ob_done"), sem("ob_free")
        aux_done, aux_free = sem("aux_done"), sem("aux_free")
        x_landed = [sem(f"x_landed{i}") for i in range(4)]
        res_landed = [sem(f"res_landed{i}") for i in range(4)]
        stored = [sem(f"stored{i}") for i in range(4)]
        small_landed, const_done, const_step = sem("small_landed"), sem("const_done"), sem("const_step")
        xt_hi_done = sem("xt_hi_done")
        low_hi_done, low_split = sem("low_hi_done"), sem("low_split")
        ln_stats, ln_rstd, ln_out = sem("ln_stats"), sem("ln_rstd"), sem("ln_out")
        soft_ready = sem("soft_ready")
        expo_ready, exp_ready, prep_ready = sem("expo_ready"), sem("exp_ready"), sem("prep_ready")
        sq_ready, rms_ready, on_ready = sem("sq_ready"), sem("rms_ready"), sem("on_ready")
        gin_ready, yraw_ready, yhi_ready, y_ready = sem("gin_ready"), sem("yraw_ready"), sem("yhi_ready"), sem("y_ready")
        xmax_ready, xp_ready, xy_hi_ready = sem("xmax_ready"), sem("xp_ready"), sem("xy_hi_ready")
        act_step, dve_step = sem("act_step"), sem("dve_step")
        block = ctx.enter_context(nc.Block())

        def slot_n(t, j):
            return 28 * t - 4 + j

        def turn(t, j):
            return 7 * t - 1 + j // 4

        def raw_turn(t, j):
            return (4 // RAW) * (7 * t - 1) + j // RAW

        def level_view(tile, s):
            return tile.rearrange("p (n w) -> p n w", w=2 * s)

        class Steps:

            def __init__(self, eng, semaphore, base):
                self.eng, self.semaphore, self.base, self.count = eng, semaphore, base, 0

            def mark(self, ins):
                ins.then_inc(self.semaphore, 1)
                self.count += 1

            def settle(self):
                self.eng.wait_ge(self.semaphore, self.base + self.count)

        @block.sync
        def _(sp):
            def load(t, j, source):
                if not (isinstance(t, int) and slot_n(t, j) < RAW):
                    sp.wait_ge(lo_done, slot_n(t, j) - RAW + 1)
                shape = source.shape
                dst = raw[:, j % RAW, :].rearrange("p (k n) -> p k n", k=shape[1])
                sp.dma_start(dst, source).then_inc(raw_landed[j % RAW], 16)

            for i in range(4):
                src = wkv_v[:, :, P * i:P * i + P] if i < 2 else wkv_v[:, 4 * (i - 2):4 * (i - 2) + 4, 256:512]
                load(0, 4 + i, src)
            for j in range(J_Q, 28):
                load(0, j, slot_source(j))
            with sp.Fori(1, NBLK) as t:
                for j in range(28):
                    load(t, j, slot_source(j))
            for j in range(J_Q):
                load(NBLK, j, slot_source(j))

        @block.gpsimd
        def _(pool):
            for m in range(2):
                pool.dma_start(rows[:, m, :], mem[0, P * m:P * m + P, :]).then_inc(small_landed, 16)
            for dst, src in ((low_raw, win_v[:, :, COL_LOW:COL_LOW + RANK]),
                             (w_gate[:, :], w_gate_up[0]),
                             (gate_bias[:, :], b_gate[0].rearrange("(c p) -> p c", p=P)),
                             (rms_g[:, :], gla_norm_g[0].rearrange("(c p) -> p c", p=P))):
                with nc.allow_non_contiguous_dma(reason="a few short rows, once"):
                    pool.dma_start(dst, src).then_inc(small_landed, 16)
            for c in range(2):
                with nc.allow_non_contiguous_dma(reason="a few short rows, once"):
                    pool.dma_start(taps[:, c, :], conv_w[0, :, P * c:P * c + P].rearrange("w p -> p w")).then_inc(
                        small_landed, 16)
            pool.memset(ident[:, :], 0.0).then_inc(const_step, 1)
            pool.memset(ones[:, :], 1.0).then_inc(const_step, 1)
            pool.memset(mask_f, 1.0).then_inc(const_step, 1)
            pool.wait_ge(const_step, 3)
            pool.affine_select(out=ident[:, :], in_=ident[:, :], compare_op=ALU.not_equal, fill=1.0, base=0,
                               pattern=[[-1, P]], channel_multiplier=1).then_inc(const_done, 1)
            for l, s in enumerate(LEVELS[:6]):
                m = mask_f[:, l, :].rearrange("p (n w) -> p n w", w=s)
                pool.affine_select(out=m, in_=m, compare_op=ALU.is_ge, fill=0.0, base=0,
                                   pattern=[[-2 * s, 64 // s], [0, s]], channel_multiplier=1).then_inc(const_step, 1)
            pool.wait_ge(const_step, 9)
            for l, s in enumerate(LEVELS[:6]):
                m = mask_f[:, l, :].rearrange("p (n w) -> p n w", w=s)
                pool.affine_select(out=m, in_=m, compare_op=ALU.is_ge, fill=0.0, base=s - 1,
                                   pattern=[[2 * s, 64 // s], [0, s]], channel_multiplier=-1).then_inc(const_step, 1)
            pool.wait_ge(const_step, 15)
            pool.tensor_copy(masks[:, :, :], mask_f).then_inc(const_done, 1)
            pool.memset(mean_w[:, :], 1.0 / DV).then_inc(const_done, 1)
            pool.memset(k_lev[:, :, :], 0.0).then_inc(const_done, 1)
            pool.memset(state[:, :, :, :], 0.0).then_inc(const_done, 1)
            pool.memset(u[:, :, :], 0.0).then_inc(const_done, 1)
            pool.memset(eps_rms[:, :], RMS_EPS).then_inc(const_done, 1)
            pool.memset(eps_ln[:, :], LN_EPS).then_inc(const_done, 1)

            def load_x(t, j):
                pool.nop(nofuse=True)
                pool.dma_start(rows[:, j, :], x_rows[bass.ds(BLK * t + P * j, P), :]).then_inc(x_landed[j], 16)

            def load_residual(t, j):
                pool.wait_ge(sc_done[0], SC_USES * t + 2 + j + 1)
                pool.wait_ge(sc_done[1], SC_USES * t + 2 + j + 1)
                pool.nop(nofuse=True)
                pool.dma_start(rows[:, j, :], x_rows[bass.ds(BLK * (t - 1) + P * j, P), :]).then_inc(
                    res_landed[j], 16)

            def store_normed(t, j):
                pool.wait_ge(ln_out, 4 * (t - 1) + j + 1)
                pool.nop(nofuse=True)
                pool.dma_start(normed[bass.ds(BLK * (t - 1) + P * j, P), :], rows[:, j, :]).then_inc(stored[j], 16)

            pool.wait_ge(sc_done[0], 2)
            pool.wait_ge(sc_done[1], 2)
            for j in range(4):
                load_x(0, j)
            def token_rows(t):
                for j in range(4):
                    pool.wait_ge(sc_done[0], SC_USES * (t - 1) + 2 + j + 1)
                    pool.wait_ge(sc_done[1], SC_USES * (t - 1) + 2 + j + 1)
                    pool.wait_ge(stored[j], 16 * (t - 1))
                    load_x(t, j)
                for j in range(4):
                    load_residual(t, j)
                for j in range(4):
                    store_normed(t, j)

            token_rows(1)
            with pool.Fori(2, NBLK) as t:
                token_rows(t)
            for j in range(4):
                pool.wait_ge(stored[j], 16 * (NBLK - 1))
                pool.dma_start(rows[:, j, :], x_rows[BLK * (NBLK - 1) + P * j:BLK * (NBLK - 1) + P * j + P, :]
                               ).then_inc(res_landed[j], 16)
            for j in range(4):
                store_normed(NBLK, j)
            for j in range(4):
                pool.wait_ge(stored[j], 16 * NBLK)

        @block.tensor
        def _(pe):
            three = three_products(pe)

            def transposes(u_sc, j):
                for b in range(2):
                    pe.wait_ge(sc_free[b], u_sc)
                    for k in range(4):
                        src = rows[:, j, P * (4 * b + k):P * (4 * b + k) + P]
                        ins = pe.transpose(sc[b][:, P * k:P * k + P], src, ident[:, :])
                    ins.then_inc(sc_done[b], 1)

            def column_quarter(t, j, q):
                if q == 0:
                    pe.wait_ge(lo_done, slot_n(t, j) + 1)
                    pe.wait_ge(main_free[j % 4], turn(t, j))
                hi = w_hi[:, j % RING, :].rearrange("p (k n) -> p k n", k=KT)
                lo = w_lo[:, j % RING, :].rearrange("p (k n) -> p k n", k=KT)
                for k in (2 * q, 2 * q + 1):
                    ins = three(main[j % 4][:, :], hi[:, k, :], lo[:, k, :], xT_hi[:, k, :], xT_lo[:, k, :],
                                k == 0, k == KT - 1)
                if q == 3:
                    ins.then_inc(main_done, 1)

            def column_tile(t, j):
                for q in range(4):
                    column_quarter(t, j, q)

            def row_slot(t, j0, i, a_hi, a_lo, kt0):
                j = j0 + i
                pe.wait_ge(lo_done, slot_n(t, j) + 1)
                hi = w_hi[:, j % RING, :].rearrange("p (k n) -> p k n", k=2)
                lo = w_lo[:, j % RING, :].rearrange("p (k n) -> p k n", k=2)
                for c in range(4):
                    if i == 0:
                        pe.wait_ge(main_free[c], turn(t, j0))
                    tok = slice(P * c, P * c + P)
                    for k in range(2):
                        ins = three(main[c][:, :], a_hi[:, kt0 + k, tok], a_lo[:, kt0 + k, tok], hi[:, k, :],
                                    lo[:, k, :], i == 0 and k == 0, i == 3 and k == 1)
                    if i == 3:
                        ins.then_inc(main_done, 1)
                if i < 3:
                    ins.then_inc(row_used, 1)

            def output_projection(t):
                for half in range(2):
                    for i in range(4):
                        pe.wait_ge(y_ready, 6 * (t - 1) + [2, 4, 4, 6][i])
                        row_slot(t, 4 * half, i, y_hi, y_lo, 2 * K_ORDER[i])

            def aux_turn(t, use):
                pe.wait_ge(aux_free, AUX_USES * t + use)

            def score(t, hp, c):
                tok = slice(CH * c, CH * c + CH)
                if c == 0:
                    pe.wait_ge(prep_ready, 2 * t + hp + 1)
                aux_turn(t, 3 + 10 * hp + 2 * c)
                pe.transpose(aux[:, 0:P], k_dec[:, tok], ident[:, :]).then_inc(aux_done, 1)
                for e in range(2):
                    pe.wait_ge(sc_free[e], SC_USES * t + 2 + (4 if hp == 0 else 16) + c)
                    r = slice(64 * e, 64 * e + 64)
                    for l in range(7):
                        if l == 0:
                            k_side = kT[r, hp, tok]
                        elif l < 6:
                            k_side = k_lev[r, l - 1, tok]
                        else:
                            k_side = k_top[r, c, :]
                        rows_out = P if l < 6 else 64
                        pe.matmul(sc[e][0:rows_out, 64 * l:64 * l + 64], k_side, q_lev[r, l, 64 * c:64 * c + 64],
                                  start=True, stop=True)
                    pe.matmul(sc[e][:, 448:449], gate[r, hp, tok], ones[r, 0:1], start=True, stop=True
                              ).then_inc(sc_done[e], 1)

            def attend(t, hp, c):
                tok = slice(CH * c, CH * c + CH)
                for e in range(2):
                    pe.wait_ge(sc_free[e], SC_USES * t + 2 + (4 if hp == 0 else 16) + c + 1)
                pe.wait_ge(ob_free, OB_USES * t + (0 if hp == 0 else 8) + c)
                aux_turn(t, 3 + 10 * hp + 2 * c + 1)
                if hp == 0:
                    pe.wait_ge(main_free[c], turn(t, J_V) + 1)
                for e in range(2):
                    vh = v_rows[:, c, DV * (2 * hp + e):DV * (2 * hp + e) + DV]
                    pe.matmul(ob[:, DV * e:DV * e + CH], vh, probs[:, e, :], start=True, stop=False)
                    ins = pe.matmul(ob[:, DV * e:DV * e + CH], state[:, hp, e, :], q_dec[:, tok],
                                    start=False, stop=True)
                ins.then_inc(ob_done, 1)
                for e in range(2):
                    vh = v_rows[:, c, DV * (2 * hp + e):DV * (2 * hp + e) + DV]
                    ins = pe.matmul(aux[:, DV * e:DV * e + DV], k_dec_rows[:, :], vh, start=True, stop=True)
                ins.then_inc(aux_done, 1)

            def mean_square(t, hp):
                for e in range(2):
                    aux_turn(t, 3 + 10 * hp + 8 + e)
                    pe.wait_ge(sq_ready, 4 * t + 2 * hp + e + 1)
                    pe.matmul(aux[:, :], mean_w[:, :], rr[:, e, :], start=True, stop=True).then_inc(aux_done, 1)

            def xattn_score(t, j):
                if j == 0:
                    for i in range(2):
                        pe.wait_ge(main_free[i], turn(t, J_XQ) + 1)
                for e in range(2):
                    pe.wait_ge(sc_free[e], SC_USES * t + 2 + 8 + 2 * j)
                    for i in range(2):
                        ins = pe.matmul(sc[e][:, M * i:M * i + M], xqT[64 * e:64 * e + 64, i, P * j:P * j + P],
                                        mkT[64 * e:64 * e + 64, i, :], start=True, stop=True)
                    ins.then_inc(sc_done[e], 1)

            def xattn_transpose(t, j):
                pe.wait_ge(xp_ready, 4 * t + j + 1)
                for m in range(2):
                    pe.wait_ge(sc_free[m], SC_USES * t + 2 + 9 + 2 * j)
                    for h in range(4):
                        ins = pe.transpose(sc[m][:, P * h:P * h + P], xp[:, h, P * m:P * m + P], ident[:, :])
                    ins.then_inc(sc_done[m], 1)

            def xattn_attend(t, j):
                pe.wait_ge(sc_free[0], SC_USES * t + 2 + 10 + 2 * j)
                pe.wait_ge(sc_free[1], SC_USES * t + 2 + 10 + 2 * j)
                pe.wait_ge(ob_free, OB_USES * t + 4 + j)
                for h in range(4):
                    for m in range(2):
                        ins = pe.matmul(ob[:, P * h:P * h + P], mv[:, m, P * (h // 2):P * (h // 2) + P],
                                        xpT[:, m, P * h:P * h + P], start=(m == 0), stop=(m == 1))
                ins.then_inc(ob_done, 1)

            def mixer_block(t, with_out):
                for j in range(4):
                    pe.wait_ge(x_landed[j], 16 * (t + 1))
                    transposes(SC_USES * t + 2 + j, j)
                if with_out:
                    output_projection(t)
                pe.wait_ge(sc_free[0], SC_USES * t + 2 + 4)
                pe.wait_ge(sc_free[1], SC_USES * t + 2 + 4)
                aux_turn(t, 0)
                for k in range(KT):
                    ins = three(aux[0:RANK, :], low_hi[:, k, :], low_lo[:, k, :], xT_hi[:, k, :], xT_lo[:, k, :],
                                k == 0, k == KT - 1)
                ins.then_inc(aux_done, 1)
                for i in range(2):
                    column_tile(t, J_Q + 2 * i)
                    aux_turn(t, 1 + i)
                    pe.matmul(aux[:, :], w_gate[:, P * i:P * i + P], lowT, start=True, stop=True
                              ).then_inc(aux_done, 1)
                    column_tile(t, J_Q + 2 * i + 1)
                for i in range(4):
                    row_slot(t, J_V, i, xT_hi, xT_lo, 2 * i)
                column_tile(t, J_XQ)
                column_tile(t, J_XQ + 1)
                for c in range(NCH):
                    score(t, 0, c)
                    column_quarter(t, J_C0 + c // 2, 2 * (c % 2))
                    column_quarter(t, J_C0 + c // 2, 2 * (c % 2) + 1)
                    attend(t, 0, c)
                for j in range(4):
                    xattn_score(t, j)
                    if j == 0:
                        mean_square(t, 0)
                    column_quarter(t, J_G0 + j // 2, 2 * (j % 2))
                    xattn_transpose(t, j)
                    column_quarter(t, J_G0 + j // 2, 2 * (j % 2) + 1)
                    xattn_attend(t, j)
                for c in range(NCH):
                    score(t, 1, c)
                    for q in range(4):
                        column_quarter(t, J_B0 + c, q)
                    attend(t, 1, c)
                column_tile(t, J_G2)
                mean_square(t, 1)
                column_tile(t, J_G3)

            pe.wait_ge(const_done, 1)
            pe.wait_ge(small_landed, 16 * 8)
            transposes(0, 0)
            transposes(1, 1)
            pe.wait_ge(sc_free[0], 2)
            pe.wait_ge(sc_free[1], 2)
            for i in range(2):
                pe.wait_ge(lo_done, i + 1)
                for k in range(KT):
                    hi = w_hi[:, i, P * k:P * k + P]
                    lo = w_lo[:, i, P * k:P * k + P]
                    ins = three(main[i][:, 0:M], hi, lo, xT_hi[:, k, 0:M], xT_lo[:, k, 0:M], k == 0, k == KT - 1)
                ins.then_inc(main_done, 1)
            for i in range(2):
                pe.wait_ge(lo_done, 3 + i)
                for m in range(2):
                    for k in range(4):
                        tok = slice(P * m, P * m + P)
                        ins = three(main[2 + m][:, 0:256], xT_hi[:, 4 * i + k, tok], xT_lo[:, 4 * i + k, tok],
                                    w_hi[:, 2 + i, 256 * k:256 * k + 256], w_lo[:, 2 + i, 256 * k:256 * k + 256],
                                    i == 0 and k == 0, i == 1 and k == 3)
                    if i == 1:
                        ins.then_inc(main_done, 1)
            pe.wait_ge(const_done, 8)
            pe.wait_ge(low_split, 1)
            mixer_block(0, False)
            with pe.Fori(1, NBLK) as t:
                mixer_block(t, True)
            output_projection(NBLK)

        def reuse(eng, t, j):
            if isinstance(t, int) and t == 0 and j < 12:
                if j >= 8:
                    eng.wait_ge(main_done, 4)
                return
            p = j - 4
            group = {0: 0, 4: 1, 12: 2}.get(p - p % 4)
            if p < 0 or group is None or p % 4 == 3:
                eng.wait_ge(main_done, slot_n(t, p) + 1)
            else:
                eng.wait_ge(row_used, 9 * t - 6 + 3 * group + p % 4 + 1)

        @block.scalar
        def _(act):
            def split(t, j):
                act.wait_ge(raw_landed[j % RAW], 16 * (raw_turn(t, j) + 1))
                reuse(act, t, j)
                act.activation(w_hi[:, j % RING, :], raw[:, j % RAW, :], ACT.Copy).then_inc(hi_done, 1)

            def next_split(t, j):
                if j + 4 < 28:
                    split(t, j + 4)
                else:
                    split(t + 1, j + 4 - 28)

            def tile_done(t, j):
                act.wait_ge(main_done, slot_n(t, j) + 1)

            def xT_part(n, uses, b, j):
                act.wait_ge(sc_done[b], uses + 1)
                act.activation(xT_hi[:, 4 * b:4 * b + 4, P * j:P * j + P],
                               sc[b][:, :].rearrange("p (k n) -> p k n", k=4), ACT.Copy).then_inc(xt_hi_done, 1)

            def gate_in(t, i):
                if i < 2 and isinstance(t, int) and t == 0:
                    return
                if i in (2, 5):
                    j = J_H0 if i == 2 else J_H1
                    act.wait_ge(main_free[j % 4], turn(t, j) + 1)
                else:
                    act.wait_ge(yraw_ready, 6 * t + {0: -1, 1: 0, 3: 1, 4: 2}[i])

            def y_part(t, i, kt):
                act.wait_ge(yraw_ready, 6 * t + i + 1)
                act.activation(y_hi[:, kt, :], y_raw[:, i % 2, :], ACT.Copy).then_inc(yhi_ready, 1)

            def exponentials(t, hp):
                act.wait_ge(expo_ready, 2 * t + hp + 1)
                act.activation(q_lev[:, :, :], q_lev[:, :, :], ACT.Exp, scale=1.0 / TAU)
                for l in range(1, 6):
                    view = level_view(k_lev[:, l - 1, :], LEVELS[l])[:, :, 0:LEVELS[l]]
                    act.activation(view, view, ACT.Exp, scale=1.0 / TAU)
                act.activation(k_top[:, :, :], k_top[:, :, :], ACT.Exp, scale=1.0 / TAU)
                act.activation(q_dec[:, :], q_dec[:, :], ACT.Exp, scale=1.0 / TAU)
                act.activation(k_dec[:, :], k_dec[:, :], ACT.Exp, scale=1.0 / TAU)
                act.activation(decay_last[:, :], b_last[:, :], ACT.Exp, scale=1.0 / TAU).then_inc(exp_ready, 1)

            def copy_k_dec(t, hp, c):
                act.wait_ge(aux_done, AUX_USES * t + 3 + 10 * hp + 2 * c + 1)
                act.activation(k_dec_rows[:, :], aux[:, 0:P], ACT.Copy).then_inc(aux_free, 1)

            def copy_o(t, hp, c):
                act.wait_ge(ob_done, OB_USES * t + (0 if hp == 0 else 8) + c + 1)
                if c == 0:
                    act.wait_ge(yraw_ready, 6 * t + 2 * hp)
                act.activation(oT[:, :, CH * c:CH * c + CH], ob[:, 0:2 * CH].rearrange("p (e n) -> p e n", e=2),
                               ACT.Copy).then_inc(ob_free, 1)

            def square(t, hp):
                act.wait_ge(on_ready, 4 * t + 2 * hp)
                act.wait_ge(ob_free, OB_USES * t + (0 if hp == 0 else 8) + 4)
                for e in range(2):
                    act.activation(rr[:, e, :], oT[:, e, :], ACT.Square).then_inc(sq_ready, 1)

            def inverse_rms(t, hp, steps):
                for e in range(2):
                    act.wait_ge(aux_done, AUX_USES * t + 3 + 10 * hp + 8 + e + 1)
                    act.activation(rr[:, e, :], aux[:, :], ACT.Ln, bias=eps_rms[:, :]).then_inc(aux_free, 1)
                    act.wait_ge(aux_free, AUX_USES * t + 3 + 10 * hp + 8 + e + 1)
                    act.activation(rr[:, e, :], rr[:, e, :], ACT.Exp, scale=-0.5).then_inc(rms_ready, 1)

            def mixer_block(t, with_out, steps):
                for j in range(4):
                    for b in range(2):
                        xT_part(8 * t + 4 + 2 * j + b, SC_USES * t + 2 + j, b, j)
                if with_out:
                    output_part(t, steps)
                act.wait_ge(aux_done, AUX_USES * t + 1)
                act.wait_ge(y_ready, 6 * t)
                act.activation(lowT, aux[0:RANK, :], ACT.Copy).then_inc(aux_free, 1)
                for i in range(4):
                    tile_done(t, J_Q + i)
                    dst = qT if i < 2 else kT
                    act.activation(dst[:, i % 2, :], main[(J_Q + i) % 4][:, :], ACT.Copy,
                                   scale=(DK ** -0.5 if i < 2 else 1.0)).then_inc(main_free[(J_Q + i) % 4], 1)
                    next_split(t, J_Q + i)
                    if i in (0, 2):
                        h = i // 2
                        act.wait_ge(aux_done, AUX_USES * t + 2 + h)
                        act.activation(gate[:, h, :], aux[:, :], ACT.Identity, bias=gate_bias[:, h:h + 1]
                                       ).then_inc(aux_free, 1)
                for h in range(2):
                    act.wait_ge(aux_free, AUX_USES * t + 2 + h)
                    act.wait_ge(on_ready, 4 * t)
                    steps.mark(act.activation(rr[:, h, :], gate[:, h, :], ACT.Abs))
                    steps.settle()
                    steps.mark(act.activation(rr[:, h, :], rr[:, h, :], ACT.Exp, scale=-1.0))
                    steps.settle()
                    act.activation(rr[:, h, :], rr[:, h, :], ACT.Ln, bias=ones[:, 0:1]).then_inc(soft_ready, 1)
                next_split(t, J_V)
                exponentials(t, 0)
                for i in range(1, 4):
                    next_split(t, J_V + i)
                for i in range(4):
                    tile_done(t, J_V + i)
                    act.activation(v_rows[:, i, :], main[i][:, :], ACT.Copy).then_inc(main_free[i], 1)
                for i in range(2):
                    tile_done(t, J_XQ + i)
                    act.activation(xqT[:, i, :], main[i][:, :], ACT.Copy, scale=DK ** -0.5).then_inc(main_free[i], 1)
                    next_split(t, J_XQ + i)
                for c in range(NCH):
                    copy_k_dec(t, 0, c)
                    if c == 1:
                        tile_done(t, J_C0)
                        gate_in(t, 0)
                        act.activation(gin[:, 0, :], main[J_C0 % 4][:, :], ACT.Copy).then_inc(main_free[J_C0 % 4], 1)
                        next_split(t, J_C0)
                    if c == 3:
                        next_split(t, J_H0)
                    copy_o(t, 0, c)
                square(t, 0)
                for j in range(4):
                    act.wait_ge(xmax_ready, 4 * t + j + 1)
                    for e in range(2):
                        act.wait_ge(sc_done[e], SC_USES * t + 2 + 8 + 2 * j + 1)
                        for i in range(2):
                            ins = act.activation(xp[:, 2 * i + e, :], sc[e][:, M * i:M * i + M], ACT.Exp,
                                                 bias=xnmax[:, 2 * e + i:2 * e + i + 1],
                                                 accum_out=xsum[:, 2 * i + e:2 * i + e + 1])
                        ins.then_inc(sc_free[e], 1)
                    if j == 0:
                        inverse_rms(t, 0, steps)
                    act.wait_ge(sc_done[0], SC_USES * t + 2 + 9 + 2 * j + 1)
                    act.activation(xpT[:, 0, :], sc[0][:, :], ACT.Copy).then_inc(sc_free[0], 1)
                    if j == 1:
                        exp_gate(t, 0, J_G0)
                        next_split(t, J_G0)
                    if j == 3:
                        y_part(t, 0, 0)
                        exp_gate(t, 1, J_G1)
                        next_split(t, J_G1)
                    act.wait_ge(ob_done, OB_USES * t + 4 + j + 1)
                    for e in range(2):
                        r = slice(64 * e, 64 * e + 64)
                        src = ob[r, :].rearrange("p (i e n) -> p i e n", i=2, e=2)[:, :, e, :]
                        act.activation(y_hi[r, 6:8, P * j:P * j + P], src, ACT.Copy).then_inc(xy_hi_ready, 1)
                    if j == 2:
                        exponentials(t, 1)
                for c in range(NCH):
                    copy_k_dec(t, 1, c)
                    if c == 0:
                        y_part(t, 1, 1)
                    if c == 1:
                        tile_done(t, J_C1)
                        gate_in(t, 3)
                        act.activation(gin[:, 1, :], main[J_C1 % 4][:, :], ACT.Copy).then_inc(main_free[J_C1 % 4], 1)
                        y_part(t, 2, 4)
                    next_split(t, J_B0 + c)
                    copy_o(t, 1, c)
                square(t, 1)
                y_part(t, 3, 5)
                exp_gate(t, 2, J_G2)
                next_split(t, J_G2)
                inverse_rms(t, 1, steps)
                exp_gate(t, 3, J_G3)
                next_split(t, J_G3)
                y_part(t, 4, 2)
                y_part(t, 5, 3)

            def exp_gate(t, g, j):
                tile_done(t, j)
                use = (1, 2, 4, 5)[g]
                gate_in(t, use)
                act.activation(gin[:, use % 2, :], main[j % 4][:, :], ACT.Exp, scale=-1.0).then_inc(gin_ready, 1)

            def output_part(t, steps):
                for j in range(8):
                    if slot_exists(t, j + 4):
                        next_split(t, j)
                for c in range(4):
                    act.wait_ge(ln_stats, 4 * (t - 1) + c + 1)
                    steps.mark(act.activation(rstd[:, c:c + 1], mvar[:, c, 1:2], ACT.Ln, bias=eps_ln[:, :]))
                    steps.settle()
                    act.activation(rstd[:, c:c + 1], rstd[:, c:c + 1], ACT.Exp, scale=-0.5).then_inc(ln_rstd, 1)

            def slot_exists(t, j):
                return not (isinstance(t, int) and t == NBLK and j >= 8)

            nc.scalar.preload_act_table_set("natural_log_exp_and_others")
            for i in range(4):
                split(0, 4 + i)
            for m in range(2):
                for b in range(2):
                    xT_part(0, m, b, m)
            act.wait_ge(small_landed, 16 * 8)
            act.wait_ge(const_done, 2)
            act.activation(low_hi[:, :, :], low_raw, ACT.Copy).then_inc(low_hi_done, 1)
            for i in range(4):
                act.wait_ge(main_done, i + 1)
                if i < 2:
                    act.activation(mkT[:, i, :], main[i][:, 0:M], ACT.Copy).then_inc(main_free[i], 1)
                else:
                    act.activation(mv[:, i - 2, :], main[i][:, 0:256], ACT.Copy).then_inc(main_free[i], 1)
            for i in range(4):
                split(0, 8 + i)
            act.wait_ge(const_done, 8)
            steps = Steps(act, act_step, 0)
            mixer_block(0, False, steps)
            assert steps.count == ACT_STEPS_FIRST, steps.count
            with act.Fori(1, NBLK) as t:
                steps = Steps(act, act_step, ACT_STEPS_FIRST + ACT_STEPS * (t - 1))
                mixer_block(t, True, steps)
                assert steps.count == ACT_STEPS, steps.count
            steps = Steps(act, act_step, ACT_STEPS_FIRST + ACT_STEPS * (NBLK - 1))
            output_part(NBLK, steps)

        @block.vector
        def _(dve):
            def split(t, j):
                dve.wait_ge(hi_done, slot_n(t, j) + 1)
                dve.tensor_tensor(w_lo[:, j % RING, :], raw[:, j % RAW, :], w_hi[:, j % RING, :].bitcast(F32),
                                  ALU.subtract).then_inc(lo_done, 1)

            def next_split(t, j):
                if j + 4 < 28:
                    split(t, j + 4)
                else:
                    split(t + 1, j + 4 - 28)

            def tile_done(t, j):
                dve.wait_ge(main_done, slot_n(t, j) + 1)

            def xT_part(n, b, j):
                dve.wait_ge(xt_hi_done, n + 1)
                dst = (slice(None), slice(4 * b, 4 * b + 4), slice(P * j, P * j + P))
                dve.tensor_tensor(xT_lo[dst], sc[b][:, :].rearrange("p (k n) -> p k n", k=4), xT_hi[dst].bitcast(F32),
                                  ALU.subtract).then_inc(sc_free[b], 1)

            def log_gates(t, steps):
                for hp in range(2):
                    dve.wait_ge(soft_ready, 2 * t + hp + 1)
                    steps.mark(dve.scalar_tensor_tensor(out=gate[:, hp, :], in0=gate[:, hp, :], scalar=0.0,
                                                        in1=rr[:, hp, :], op0=ALU.min, op1=ALU.subtract))
                for i in range(4):
                    dve.wait_ge(main_free[(J_Q + i) % 4], turn(t, J_Q + i) + 1)

            def cumulate(t, hp, steps):
                if hp == 1:
                    dve.wait_ge(ob_done, OB_USES * t + 4)
                steps.settle()
                for c in range(NCH):
                    steps.mark(dve.tensor_tensor_scan(q_dec[:, CH * c:CH * c + CH], ones[:, :],
                                                      gate[:, hp, CH * c:CH * c + CH], 0.0, ALU.mult, ALU.add))
                steps.settle()
                steps.mark(dve.tensor_copy(b_last[:, :], q_dec[:, CH - 1:BLK:CH]))
                steps.mark(dve.tensor_tensor(gate[:, hp, :], qT[:, hp, :], kT[:, hp, :], ALU.mult))
                steps.settle()

            def exponents_q(t, hp):
                for l, s in enumerate(LEVELS):
                    b = level_view(q_dec[:, :], s)
                    ref = b[:, :, s - 1:s].to_broadcast([P, BLK // (2 * s), s])
                    dve.tensor_tensor(q_lev[:, l, :].rearrange("p (n w) -> p n w", w=s), b[:, :, s:2 * s], ref,
                                      ALU.subtract)

            def k_side(l):
                s = LEVELS[l]
                return k_top[:, :, :] if l == 6 else level_view(k_lev[:, l - 1, :], s)[:, :, 0:s]

            def exponents_k(t, hp):
                for l in range(1, 7):
                    s = LEVELS[l]
                    b = level_view(q_dec[:, :], s)
                    ref = b[:, :, s - 1:s].to_broadcast([P, BLK // (2 * s), s])
                    dve.tensor_tensor(k_side(l), ref, b[:, :, 0:s], ALU.subtract)
                dve.tensor_tensor(k_dec[:, :].rearrange("p (c w) -> p c w", w=CH),
                                  b_last[:, :].unsqueeze(2).to_broadcast([P, NCH, CH]),
                                  q_dec[:, :].rearrange("p (c w) -> p c w", w=CH), ALU.subtract
                                  ).then_inc(expo_ready, 1)

            def decayed(t, hp):
                dve.wait_ge(exp_ready, 2 * t + hp + 1)
                for l, s in enumerate(LEVELS):
                    dst = q_lev[:, l, :].rearrange("p (n w) -> p n w", w=s)
                    dve.tensor_tensor(dst, dst, level_view(qT[:, hp, :], s)[:, :, s:2 * s], ALU.mult)
                    if l > 0:
                        dve.tensor_tensor(k_side(l), k_side(l), level_view(kT[:, hp, :], s)[:, :, 0:s], ALU.mult)
                dve.tensor_tensor(q_dec[:, :], q_dec[:, :], qT[:, hp, :], ALU.mult)
                dve.tensor_tensor(k_dec[:, :], k_dec[:, :], kT[:, hp, :], ALU.mult).then_inc(prep_ready, 1)

            def mask_scores(t, hp, c, steps):
                for e in range(2):
                    dve.wait_ge(sc_done[e], SC_USES * t + 2 + (4 if hp == 0 else 16) + c + 1)
                    steps.mark(dve.tensor_scalar(probs[:, e, :], ident[:, :], sc[e][:, 448:449], None, ALU.mult))
                steps.settle()
                for e in range(2):
                    steps.mark(dve.tensor_copy(probs[0:64, e, 64:128], sc[e][0:64, 384:448]))
                for l, s in enumerate(LEVELS[:6]):
                    steps.settle()
                    dve.nop(nofuse=True)
                    for e in range(2):
                        ins = dve.copy_predicated(level_view(probs[:, e, :], s)[:, :, s:2 * s],
                                                  masks[:, l, :].rearrange("p (n w) -> p n w", w=s),
                                                  sc[e][:, 64 * l:64 * l + 64].rearrange("p (n w) -> p n w", w=s))
                        if l == 5:
                            ins.then_inc(sc_free[e], 1)
                        else:
                            steps.mark(ins)

            def update_state(t, hp, c):
                dve.wait_ge(aux_done, AUX_USES * t + 3 + 10 * hp + 2 * c + 2)
                for e in range(2):
                    r = slice(64 * e, 64 * e + 64)
                    ins = dve.scalar_tensor_tensor(out=state[r, hp, e, :], in0=state[r, hp, e, :],
                                                   scalar=decay_last[r, c:c + 1], in1=aux[r, DV * e:DV * e + DV],
                                                   op0=ALU.mult, op1=ALU.add)
                ins.then_inc(aux_free, 1)

            def normalise_o(t, hp):
                for e in range(2):
                    dve.wait_ge(rms_ready, 4 * t + 2 * hp + e + 1)
                    dve.scalar_tensor_tensor(out=oT[:, e, :], in0=oT[:, e, :], scalar=rms_g[:, 0:1], in1=rr[:, e, :],
                                             op0=ALU.mult, op1=ALU.mult).then_inc(on_ready, 1)

            def silu(t, g, j, steps):
                use = (1, 2, 4, 5)[g]
                buf = gin[:, use % 2, :]
                dve.wait_ge(gin_ready, 4 * t + g + 1)
                steps.mark(dve.tensor_scalar(buf, buf, 1.0, None, ALU.add))
                steps.settle()
                steps.mark(dve.reciprocal(buf, buf))
                steps.settle()
                dve.tensor_tensor(buf, buf, main[j % 4][:, :], ALU.mult).then_inc(main_free[j % 4], 1)

            def gated(t, g, j):
                use, i = ((1, 0), (2, 1), (4, 4), (5, 5))[g]
                dve.wait_ge(on_ready, 4 * t + g + 1)
                dve.wait_ge(main_free[j % 4], turn(t, j) + 1)
                dve.tensor_tensor(y_raw[:, i % 2, :], oT[:, g % 2, :], gin[:, use % 2, :], ALU.mult
                                  ).then_inc(yraw_ready, 1)

            def y_part(t, i, kt):
                dve.wait_ge(yhi_ready, 6 * t + i + 1)
                dve.tensor_tensor(y_lo[:, kt, :], y_raw[:, i % 2, :], y_hi[:, kt, :].bitcast(F32), ALU.subtract
                                  ).then_inc(y_ready, 1)

            def conv_input(t, ch, j, steps):
                steps.mark(dve.tensor_copy(u[:, ch, 0:2], u[:, ch, BLK:BLK + 2]))
                steps.settle()
                tile_done(t, j)
                c_tile = J_C0 if ch == 0 else J_C1
                dve.wait_ge(main_free[c_tile % 4], turn(t, c_tile) + 1)
                dve.tensor_tensor(u[:, ch, 2:BLK + 2], gin[:, ch, :], main[j % 4][:, :], ALU.mult
                                  ).then_inc(main_free[j % 4], 1)

            def conv(t, ch, j, steps):
                acc = y_raw[:, ch, :]
                h_tile = J_H0 if ch == 0 else J_H1
                dve.wait_ge(main_free[h_tile % 4], turn(t, h_tile) + 1)
                steps.mark(dve.tensor_scalar(acc, u[:, ch, 0:BLK], taps[:, ch, 0:1], None, ALU.mult))
                for w in (1, 2):
                    steps.settle()
                    steps.mark(dve.scalar_tensor_tensor(out=acc, in0=u[:, ch, w:w + BLK], scalar=taps[:, ch, w:w + 1],
                                                        in1=acc, op0=ALU.mult, op1=ALU.add))
                steps.settle()
                tile_done(t, j)
                dve.tensor_tensor(acc, acc, main[j % 4][:, :], ALU.mult).then_inc(yraw_ready, 1)
                dve.wait_ge(yraw_ready, 6 * t + 3 + ch)
                dve.tensor_copy(xmax[:, 0:1], main[j % 4][:, 0:1]).then_inc(main_free[j % 4], 1)

            def output_part(t, steps):
                for half in range(2):
                    for c in range(4):
                        if not (isinstance(t, int) and t == NBLK and half == 1):
                            next_split(t, 4 * half + c)
                    for c in range(4):
                        tile_done(t, 4 * half + c)
                        if half == 0:
                            dve.wait_ge(res_landed[c], 16 * t)
                        dst = rows[:, c, 512 * half:512 * half + 512]
                        dve.scalar_tensor_tensor(out=dst, in0=dst, scalar=ALPHA, in1=main[c][:, :],
                                                 op0=ALU.mult, op1=ALU.add).then_inc(main_free[c], 1)
                        if half == 1:
                            dve.wait_ge(main_free[c], turn(t, 4) + 1)
                            for i in range(2):
                                steps.mark(dve.bn_stats(stats[:, c, i, :], rows[:, c, 512 * i:512 * i + 512]))
                            steps.settle()
                            dve.nop(nofuse=True)
                            dve.bn_aggr(mvar[:, c, :], stats[:, c, :, :]).then_inc(ln_stats, 1)
                for c in range(4):
                    dve.wait_ge(ln_rstd, 4 * (t - 1) + c + 1)
                    dve.tensor_scalar(rows[:, c, :], rows[:, c, :], mvar[:, c, 0:1], rstd[:, c:c + 1],
                                      ALU.subtract, ALU.mult).then_inc(ln_out, 1)

            def softmax_max(t, j, steps):
                for e in range(2):
                    dve.wait_ge(sc_done[e], SC_USES * t + 2 + 8 + 2 * j + 1)
                    steps.mark(dve.tensor_reduce(xmax[:, 2 * e:2 * e + 2],
                                                 sc[e][:, :].rearrange("p (i m) -> p i m", i=2), AX_X, ALU.max))
                steps.settle()
                dve.tensor_scalar(xnmax[:, :], xmax[:, :], -1.0, None, ALU.mult).then_inc(xmax_ready, 1)

            def softmax_norm(t, j, steps):
                for e in range(2):
                    dve.wait_ge(sc_free[e], SC_USES * t + 2 + 8 + 2 * j + 1)
                steps.mark(dve.reciprocal(xrec[:, :], xsum[:, :]))
                steps.settle()
                for h in range(4):
                    ins = dve.tensor_scalar(xp[:, h, :], xp[:, h, :], xrec[:, h:h + 1], None, ALU.mult)
                ins.then_inc(xp_ready, 1)

            def mixer_block(t, with_out, steps):
                for j in range(4):
                    for b in range(2):
                        xT_part(8 * t + 4 + 2 * j + b, b, j)
                if with_out:
                    output_part(t, steps)
                for i in range(4):
                    next_split(t, J_Q + i)
                log_gates(t, steps)
                cumulate(t, 0, steps)
                exponents_q(t, 0)
                exponents_k(t, 0)
                next_split(t, J_V)
                decayed(t, 0)
                for i in range(1, 4):
                    next_split(t, J_V + i)
                next_split(t, J_XQ)
                next_split(t, J_XQ + 1)
                for c in range(NCH):
                    mask_scores(t, 0, c, steps)
                    if c == 1:
                        next_split(t, J_C0)
                    if c == 3:
                        conv_input(t, 0, J_H0, steps)
                        next_split(t, J_H0)
                    update_state(t, 0, c)
                for j in range(4):
                    softmax_max(t, j, steps)
                    if j == 0:
                        cumulate(t, 1, steps)
                        exponents_q(t, 1)
                    if j == 1:
                        exponents_k(t, 1)
                    softmax_norm(t, j, steps)
                    if j == 0:
                        normalise_o(t, 0)
                    dve.wait_ge(sc_done[1], SC_USES * t + 2 + 9 + 2 * j + 1)
                    dve.tensor_copy(xpT[:, 1, :], sc[1][:, :]).then_inc(sc_free[1], 1)
                    if j in (1, 3):
                        g = j // 2
                        silu(t, g, GATE_TILE[g], steps)
                        gated(t, g, GATE_TILE[g])
                        next_split(t, GATE_TILE[g])
                    if j == 3:
                        y_part(t, 0, 0)
                    for e in range(2):
                        dve.wait_ge(xy_hi_ready, 8 * t + 2 * j + e + 1)
                        r = slice(64 * e, 64 * e + 64)
                        src = ob[r, :].rearrange("p (i e n) -> p i e n", i=2, e=2)[:, :, e, :]
                        ins = dve.tensor_tensor(y_lo[r, 6:8, P * j:P * j + P], src,
                                                y_hi[r, 6:8, P * j:P * j + P].bitcast(F32), ALU.subtract)
                    ins.then_inc(ob_free, 1)
                decayed(t, 1)
                for c in range(NCH):
                    mask_scores(t, 1, c, steps)
                    if c == 0:
                        y_part(t, 1, 1)
                        conv(t, 0, J_B0, steps)
                    if c == 1:
                        y_part(t, 2, 4)
                    if c == 2:
                        conv_input(t, 1, J_H1, steps)
                    if c == 3:
                        conv(t, 1, J_B1, steps)
                    next_split(t, J_B0 + c)
                    update_state(t, 1, c)
                y_part(t, 3, 5)
                silu(t, 2, J_G2, steps)
                next_split(t, J_G2)
                normalise_o(t, 1)
                gated(t, 2, J_G2)
                silu(t, 3, J_G3, steps)
                gated(t, 3, J_G3)
                next_split(t, J_G3)
                y_part(t, 4, 2)
                y_part(t, 5, 3)

            def first_split(j):
                split(0, j)

            for i in range(4):
                first_split(4 + i)
            for m in range(2):
                for b in range(2):
                    xT_part(2 * m + b, b, m)
            dve.wait_ge(low_hi_done, 1)
            dve.tensor_tensor(low_lo[:, :, :], low_raw, low_hi[:, :, :].bitcast(F32), ALU.subtract
                              ).then_inc(low_split, 1)
            for i in range(4):
                first_split(8 + i)
            dve.wait_ge(const_done, 8)
            steps = Steps(dve, dve_step, 0)
            mixer_block(0, False, steps)
            assert steps.count == DVE_STEPS_FIRST, steps.count
            with dve.Fori(1, NBLK) as t:
                steps = Steps(dve, dve_step, DVE_STEPS_FIRST + DVE_STEPS * (t - 1))
                mixer_block(t, True, steps)
                assert steps.count == DVE_STEPS, steps.count
            steps = Steps(dve, dve_step, DVE_STEPS_FIRST + DVE_STEPS * (NBLK - 1))
            output_part(NBLK, steps)

    feed_forward(nc, normed, ln1_g, ln1_b, w1_v, w2_rows, ln2_g, ln2_b, out_rows, KT, HALF, NT, NFB)


def feed_forward(nc, normed, ln1_g, ln1_b, w1_v, w2_rows, ln2_g, ln2_b, out_rows, KT, HALF, NT, NFB):
    D = KT * P
    with ExitStack() as ctx:
        def sb(name, shape, dt=F32):
            return ctx.enter_context(nc.sbuf_tensor(name, shape, dt))

        def sem(name):
            return ctx.enter_context(nc.semaphore(name))

        raw = sb("f_raw", [P, 2, 1024])
        w_hi = sb("f_w_hi", [P, 4, 1024], F32R)
        w_lo = sb("f_w_lo", [P, 4, 1024], F32R)
        xT_hi = sb("f_xT_hi", [P, KT, HALF], F32R)
        xT_lo = sb("f_xT_lo", [P, KT, HALF], F32R)
        h_hi = sb("h_hi", [P, 2, HALF], F32R)
        h_lo = sb("h_lo", [P, 2, HALF], F32R)
        acc = sb("acc", [P, 2, NT, D])
        relu = sb("relu", [P, 2, 512])
        h_raw = sb("h_raw", [P, 2, 512])
        g1_row = sb("g1_row", [P, D])
        b1_row = sb("b1_row", [P, D])
        g2_row = sb("g2_row", [P, D])
        b2_row = sb("b2_row", [P, D])
        g1_col = sb("g1_col", [P, KT])
        b1_col = sb("b1_col", [P, KT])
        ident = sb("f_ident", [P, P])
        eps_ln = sb("f_eps_ln", [P, 1])
        stats = sb("f_stats", [P, NT, 2, 6])
        mvar = sb("f_mvar", [P, NT, 2])
        rstd = sb("f_rstd", [P, NT])
        nmean = sb("f_nmean", [P, NT])
        fm = [ctx.enter_context(nc.psum_tensor(f"fm{i}", [P, 512], F32)) for i in range(4)]
        fo = [ctx.enter_context(nc.psum_tensor(f"fo{i}", [P, 512], F32)) for i in range(4)]

        raw_landed = [sem(f"f_raw_landed{i}") for i in range(2)]
        hi_done, lo_done = sem("f_hi_done"), sem("f_lo_done")
        fm_done, fo_done = sem("fm_done"), sem("fo_done")
        fm_free = [sem(f"fm_free{i}") for i in range(4)]
        fo_free = [sem(f"fo_free{i}") for i in range(4)]
        n_landed = [[sem(f"n_landed{hf}_{c}") for c in range(NT)] for hf in range(2)]
        out_stored = [sem(f"out_stored{c}") for c in range(NT)]
        col_landed, row_landed = sem("col_landed"), sem("row_landed")
        const_step, const_done = sem("f_const_step"), sem("f_const_done")
        x_hi_ready, x_lo_ready = sem("x_hi_ready"), sem("x_lo_ready")
        init_step, init_done = sem("init_step"), sem("init_done")
        relu_ready, hraw_ready, h_hi_ready, h_lo_ready = (
            sem("relu_ready"), sem("hraw_ready"), sem("h_hi_ready"), sem("h_lo_ready"))
        stats_step, ln_stats, ln_step, ln_rstd, ln_out = (
            sem("f_stats_step"), sem("f_ln_stats"), sem("f_ln_step"), sem("f_ln_rstd"), sem("f_ln_out"))
        scale_step, out_ready = sem("scale_step"), sem("out_ready")
        tail_step, tail_ready, tail_stored = sem("tail_step"), sem("tail_ready"), sem("tail_stored")
        block = ctx.enter_context(nc.Block())

        def slot_n(hf, fb, s):
            return 4 * NFB * hf + 4 * fb + s

        def fm_turn(hf, fb):
            return (4 + NFB) * hf + 4 + fb

        def fm_n(hf, fb, i):
            return 4 * fm_turn(hf, fb) + i

        def fo_n(hf, fb, i):
            return 16 * NFB * hf + 16 * fb + i

        def h_n(hf, fb, i):
            return 4 * NFB * hf + 4 * fb + i

        POOL_TAIL = 5

        @block.sync
        def _(sp):
            def load(hf, fb, first=False):
                for s in range(4):
                    if not (first and s < 2):
                        sp.wait_ge(lo_done, slot_n(hf, fb, s) - 1)
                    if s < 2:
                        src = w1_v[:, :, bass.ds(2 * P * fb + P * s, P)]
                        dst = raw[:, s, :].rearrange("p (k n) -> p k n", k=KT)
                    else:
                        src = w2_rows[bass.ds(2 * P * fb + P * (s - 2), P), :]
                        dst = raw[:, s - 2, :]
                    sp.dma_start(dst, src).then_inc(raw_landed[s % 2], 16)

            load(0, 0, True)
            with sp.Fori(1, NFB) as fb:
                load(0, fb)
            with sp.Fori(0, NFB) as fb:
                load(1, fb)
            for i, c in enumerate(range(POOL_TAIL, NT)):
                sp.wait_ge(tail_ready, i + 1)
                sp.dma_start(out_rows[HALF + P * c:HALF + P * c + P, :], acc[:, 1, c, :]).then_inc(tail_stored, 16)
            sp.wait_ge(tail_stored, 16 * (NT - POOL_TAIL))

        @block.gpsimd
        def _(pool):
            for c in range(NT):
                pool.dma_start(acc[:, 0, c, :], normed[P * c:P * c + P, :]).then_inc(n_landed[0][c], 16)
            for dst, src in ((g1_col, ln1_g), (b1_col, ln1_b)):
                with nc.allow_non_contiguous_dma(reason="one value a partition, once"):
                    pool.dma_start(dst[:, :], src[0].rearrange("(k p) -> p k", p=P)).then_inc(col_landed, 16)
            pool.memset(ident[:, :], 0.0).then_inc(const_step, 1)
            pool.wait_ge(const_step, 1)
            pool.affine_select(out=ident[:, :], in_=ident[:, :], compare_op=ALU.not_equal, fill=1.0, base=0,
                               pattern=[[-1, P]], channel_multiplier=1).then_inc(const_done, 1)
            pool.memset(eps_ln[:, :], LN_EPS).then_inc(const_done, 1)
            for dst, src in ((g1_row, ln1_g), (b1_row, ln1_b), (g2_row, ln2_g), (b2_row, ln2_b)):
                pool.dma_start(dst[:, :], src.to_broadcast([P, D])).then_inc(row_landed, 16)
            for c in range(NT):
                pool.dma_start(acc[:, 1, c, :], normed[HALF + P * c:HALF + P * c + P, :]).then_inc(n_landed[1][c], 16)
            pool.wait_ge(row_landed, 16 * 4)
            pool.tensor_scalar(g1_row[:, :], g1_row[:, :], ALPHA, None, ALU.mult).then_inc(init_step, 1)
            pool.tensor_scalar(b1_row[:, :], b1_row[:, :], ALPHA, None, ALU.mult).then_inc(init_step, 1)
            for hf in range(2):
                for c in range(NT):
                    pool.wait_ge(fm_done, fm_n(hf, -4, 8 * (c // 4) + 8))
                    pool.wait_ge(init_step, 2 + NT * hf + c)
                    pool.tensor_tensor(acc[:, hf, c, :], acc[:, hf, c, :], g1_row[:, :], ALU.mult
                                       ).then_inc(init_step, 1)
                    pool.wait_ge(init_step, 2 + NT * hf + c + 1)
                    pool.tensor_tensor(acc[:, hf, c, :], acc[:, hf, c, :], b1_row[:, :], ALU.add
                                       ).then_inc(init_done, 1)
            for hf in range(2):
                for c in range(NT if hf == 0 else POOL_TAIL):
                    pool.wait_ge(ln_out, NT * hf + c + 1)
                    pool.tensor_tensor(acc[:, hf, c, :], acc[:, hf, c, :], g2_row[:, :], ALU.mult
                                       ).then_inc(scale_step, 1)
                    pool.wait_ge(scale_step, NT * hf + c + 1)
                    pool.tensor_tensor(acc[:, hf, c, :], acc[:, hf, c, :], b2_row[:, :], ALU.add
                                       ).then_inc(out_ready, 1)
                    pool.wait_ge(out_ready, NT * hf + c + 1)
                    pool.dma_start(out_rows[HALF * hf + P * c:HALF * hf + P * c + P, :], acc[:, hf, c, :]
                                   ).then_inc(out_stored[c], 16)
            for c in range(NT):
                pool.wait_ge(out_stored[c], 32 if c < POOL_TAIL else 16)

        @block.tensor
        def _(pe):
            three = three_products(pe)

            def hidden(hf, fb):
                for i in range(4):
                    f, sb_ = i % 2, i // 2
                    if i < 2:
                        pe.wait_ge(lo_done, slot_n(hf, fb, f) + 1)
                    pe.wait_ge(hraw_ready, h_n(hf, fb, 0))
                    tok = slice(512 * sb_, 512 * sb_ + 512)
                    for k in range(KT):
                        col = slice(P * k, P * k + P)
                        ins = three(fm[i][:, :], w_hi[:, f, col], w_lo[:, f, col], xT_hi[:, k, tok], xT_lo[:, k, tok],
                                    k == 0, k == KT - 1)
                    ins.then_inc(fm_done, 1)

            def project(hf, fb, i):
                c, d = i // 2, i % 2
                if i == 0:
                    pe.wait_ge(lo_done, slot_n(hf, fb, 3) + 1)
                if i % 8 == 0:
                    pe.wait_ge(h_lo_ready, h_n(hf, fb, 2 + i // 4))
                pe.wait_ge(fo_free[i % 4], 4 * NFB * hf + 4 * fb + i // 4)
                tok = slice(P * c, P * c + P)
                for f in range(2):
                    ins = three(fo[i % 4][:, :], h_hi[:, f, tok], h_lo[:, f, tok],
                                w_hi[:, 2 + f, 512 * d:512 * d + 512], w_lo[:, 2 + f, 512 * d:512 * d + 512],
                                f == 0, f == 1)
                ins.then_inc(fo_done, 1)

            def transposes(hf, i):
                sb_, k = i // 8, i % 8
                pe.wait_ge(fm_free[i % 4], 4 * hf + i // 4)
                if hf == 1 and i == 0:
                    pe.wait_ge(hraw_ready, h_n(1, 0, 0))
                for c in range(4):
                    if k == 0:
                        pe.wait_ge(n_landed[hf][4 * sb_ + c], 16)
                    ins = pe.transpose(fm[i % 4][:, P * c:P * c + P], acc[:, hf, 4 * sb_ + c, P * k:P * k + P],
                                       ident[:, :])
                ins.then_inc(fm_done, 1)

            def both(hf, fb):
                hidden(hf, fb)
                for i in range(16):
                    project(hf, fb, i)

            pe.wait_ge(const_done, 1)
            for i in range(16):
                transposes(0, i)
            pe.wait_ge(x_lo_ready, 16)
            both(0, 0)
            with pe.Fori(1, NFB - 1) as fb:
                both(0, fb)
            hidden(0, NFB - 1)
            for i in range(16):
                project(0, NFB - 1, i)
                transposes(1, i)
            pe.wait_ge(x_lo_ready, 32)
            both(1, 0)
            with pe.Fori(1, NFB) as fb:
                both(1, fb)

        @block.scalar
        def _(act):
            def split(hf, fb, s):
                act.wait_ge(raw_landed[s % 2], 16 * (2 * NFB * hf + 2 * fb + s // 2 + 1))
                first = isinstance(fb, int) and hf == 0 and fb == 0
                if s < 2 and isinstance(fb, int) and fb == 0:
                    if hf == 1:
                        act.wait_ge(fm_done, fm_n(0, NFB - 1, s + 3))
                elif s < 2:
                    act.wait_ge(fm_done, fm_n(hf, fb - 1, s + 3))
                elif not first:
                    act.wait_ge(fo_done, fo_n(hf, fb, 0))
                act.activation(w_hi[:, s, :], raw[:, s % 2, :], ACT.Copy).then_inc(hi_done, 1)

            def hidden(hf, fb):
                for i in range(4):
                    f, sb_ = i % 2, i // 2
                    act.wait_ge(fm_done, fm_n(hf, fb, i) + 1)
                    act.activation(relu[:, i % 2, :], fm[i][:, :], ACT.Relu).then_inc(relu_ready, 1)
                    act.wait_ge(hraw_ready, h_n(hf, fb, i) + 1)
                    act.activation(h_hi[:, f, 512 * sb_:512 * sb_ + 512], h_raw[:, i % 2, :], ACT.Copy
                                   ).then_inc(h_hi_ready, 1)

            def x_part(hf, i):
                sb_, k = i // 8, i % 8
                act.wait_ge(fm_done, fm_n(hf, -4, i) + 1)
                if i >= 2:
                    act.wait_ge(x_lo_ready, 16 * hf + i - 1)
                elif hf == 1:
                    act.wait_ge(hraw_ready, h_n(1, 0, 0))
                act.activation(relu[:, i % 2, :], fm[i % 4][:, :], ACT.Identity, scale=g1_col[:, k:k + 1],
                               bias=b1_col[:, k:k + 1]).then_inc(fm_free[i % 4], 1)
                act.wait_ge(fm_free[i % 4], 4 * hf + i // 4 + 1)
                act.activation(xT_hi[:, k, 512 * sb_:512 * sb_ + 512], relu[:, i % 2, :], ACT.Copy
                               ).then_inc(x_hi_ready, 1)

            def normalise(hf, c):
                act.wait_ge(ln_stats, NT * hf + c + 1)
                act.activation(rstd[:, c:c + 1], mvar[:, c, 1:2], ACT.Ln, bias=eps_ln[:, :]).then_inc(ln_step, 1)
                act.wait_ge(ln_step, 3 * (NT * hf + c) + 1)
                act.activation(rstd[:, c:c + 1], rstd[:, c:c + 1], ACT.Exp, scale=-0.5).then_inc(ln_step, 1)
                act.wait_ge(ln_step, 3 * (NT * hf + c) + 2)
                act.activation(nmean[:, c:c + 1], nmean[:, c:c + 1], ACT.Copy, scale=rstd[:, c:c + 1]
                               ).then_inc(ln_step, 1)
                act.wait_ge(ln_step, 3 * (NT * hf + c) + 3)
                act.activation(acc[:, hf, c, :], acc[:, hf, c, :], ACT.Identity, scale=rstd[:, c:c + 1],
                               bias=nmean[:, c:c + 1]).then_inc(ln_out, 1)

            def block_but_last(hf, fb):
                split(hf, fb, 2)
                split(hf, fb, 3)
                hidden(hf, fb)
                split(hf, fb + 1, 0)
                split(hf, fb + 1, 1)

            act.wait_ge(col_landed, 32)
            act.wait_ge(const_done, 2)
            split(0, 0, 0)
            split(0, 0, 1)
            for i in range(16):
                x_part(0, i)
            for hf in range(2):
                block_but_last(hf, 0)
                if hf == 1:
                    for c in range(NT):
                        normalise(0, c)
                with act.Fori(1, NFB - 1) as fb:
                    block_but_last(hf, fb)
                split(hf, NFB - 1, 2)
                split(hf, NFB - 1, 3)
                hidden(hf, NFB - 1)
                if hf == 0:
                    split(1, 0, 0)
                    split(1, 0, 1)
                    for i in range(16):
                        x_part(1, i)
            for c in range(NT):
                normalise(1, c)

        @block.vector
        def _(dve):
            def split(hf, fb, s):
                dve.wait_ge(hi_done, slot_n(hf, fb, s) + 1)
                dve.tensor_tensor(w_lo[:, s, :], raw[:, s % 2, :], w_hi[:, s, :].bitcast(F32), ALU.subtract
                                  ).then_inc(lo_done, 1)

            def hidden_tile(hf, fb, i):
                f, sb_ = i % 2, i // 2
                tok = slice(512 * sb_, 512 * sb_ + 512)
                dve.wait_ge(relu_ready, h_n(hf, fb, i) + 1)
                if not (isinstance(fb, int) and hf == 0 and fb == 0 and i < 2):
                    dve.wait_ge(h_lo_ready, h_n(hf, fb, i) - 1)
                dve.scalar_tensor_tensor(out=h_raw[:, i % 2, :], in0=fm[i][:, :], scalar=0.0,
                                         in1=relu[:, i % 2, :], op0=ALU.max, op1=ALU.mult
                                         ).then_inc(hraw_ready, 1)
                dve.wait_ge(h_hi_ready, h_n(hf, fb, i) + 1)
                dve.tensor_tensor(h_lo[:, f, tok], h_raw[:, i % 2, :], h_hi[:, f, tok].bitcast(F32),
                                  ALU.subtract).then_inc(h_lo_ready, 1)

            def add(hf, fb, i):
                c, d = i // 2, i % 2
                dve.wait_ge(fo_done, fo_n(hf, fb, i) + 1)
                if isinstance(fb, int) and fb == 0 and d == 0:
                    dve.wait_ge(init_done, NT * hf + c + 1)
                dst = acc[:, hf, c, 512 * d:512 * d + 512]
                dve.tensor_tensor(dst, dst, fo[i % 4][:, :], ALU.add).then_inc(fo_free[i % 4], 1)

            def x_part(hf, i):
                sb_, k = i // 8, i % 8
                tok = slice(512 * sb_, 512 * sb_ + 512)
                dve.wait_ge(x_hi_ready, 16 * hf + i + 1)
                dve.tensor_tensor(xT_lo[:, k, tok], relu[:, i % 2, :], xT_hi[:, k, tok].bitcast(F32), ALU.subtract
                                  ).then_inc(x_lo_ready, 1)

            def statistics(hf, c):
                for d in range(2):
                    i = 2 * c + d
                    dve.wait_ge(fo_free[i % 4], 4 * NFB * (hf + 1) - 4 + i // 4 + 1)
                    dve.bn_stats(stats[:, c, d, :], acc[:, hf, c, 512 * d:512 * d + 512]).then_inc(stats_step, 1)
                dve.wait_ge(stats_step, 3 * (NT * hf + c) + 2)
                dve.bn_aggr(mvar[:, c, :], stats[:, c, :, :]).then_inc(stats_step, 1)
                dve.wait_ge(stats_step, 3 * (NT * hf + c) + 3)
                dve.tensor_scalar(nmean[:, c:c + 1], mvar[:, c, 0:1], -1.0, None, ALU.mult).then_inc(ln_stats, 1)

            def block_but_last(hf, fb):
                split(hf, fb, 2)
                split(hf, fb, 3)
                for i in range(4):
                    hidden_tile(hf, fb, i)
                    if hf == 1 and isinstance(fb, int):
                        statistics(0, 2 * i)
                        statistics(0, 2 * i + 1)
                for i in range(16):
                    add(hf, fb, i)
                    if i == 3:
                        split(hf, fb + 1, 0)
                    if i == 5:
                        split(hf, fb + 1, 1)

            split(0, 0, 0)
            split(0, 0, 1)
            for i in range(16):
                x_part(0, i)
            for hf in range(2):
                block_but_last(hf, 0)
                with dve.Fori(1, NFB - 1) as fb:
                    block_but_last(hf, fb)
                split(hf, NFB - 1, 2)
                split(hf, NFB - 1, 3)
                for i in range(4):
                    hidden_tile(hf, NFB - 1, i)
                if hf == 0:
                    split(1, 0, 0)
                    split(1, 0, 1)
                    for i in range(16):
                        add(0, NFB - 1, i)
                        x_part(1, i)
            for c in range(NT):
                add(1, NFB - 1, 2 * c)
                add(1, NFB - 1, 2 * c + 1)
                statistics(1, c)
            dve.wait_ge(row_landed, 16 * 4)
            for i, c in enumerate(range(POOL_TAIL, NT)):
                dve.wait_ge(ln_out, NT + c + 1)
                dve.tensor_tensor(acc[:, 1, c, :], acc[:, 1, c, :], g2_row[:, :], ALU.mult).then_inc(tail_step, 1)
                dve.wait_ge(tail_step, i + 1)
                dve.tensor_tensor(acc[:, 1, c, :], acc[:, 1, c, :], b2_row[:, :], ALU.add).then_inc(tail_ready, 1)


_INS = ["x", "mem", "w_in", "w_gate_up", "b_gate", "conv_w", "gla_norm_g", "w_mem_kv", "w_out",
        "ln1_g", "ln1_b", "w_ff1", "w_ff2", "ln2_g", "ln2_b"]


def kernel(**inputs):
    import numpy as _np
    import concourse.bacc as _bacc
    from concourse import mybir as _mybir
    from concourse.bass_utils import run_bass_kernel_spmd as _run

    nc = _bacc.Bacc("TRN2", target_bir_lowering=False, num_devices=1,
                    dynamic_dma_scratch_size=8192)
    arrays, args = {}, []
    for name in _INS:
        a = _np.ascontiguousarray(inputs[name])
        arrays[f"in_{name}_dram"] = a
        args.append(nc.dram_tensor(f"in_{name}_dram", a.shape, _mybir.dt.from_np(a.dtype), kind="ExternalInput").ap())
    B, S, D = inputs["x"].shape
    args.append(nc.dram_tensor("normed_dram", (S, D), _mybir.dt.float32, kind="Internal").ap())
    args.append(nc.dram_tensor("out_0_dram", (B, S, D), _mybir.dt.float32, kind="ExternalOutput").ap())
    hybrid_layer(nc, *args)
    r = _run(nc, [arrays], core_ids=[0])
    return r.results[0]["out_0_dram"]
```

```python
from contextlib import ExitStack

import concourse.bass as bass
from concourse import mybir

F32 = mybir.dt.float32
F32R = mybir.dt.float32r
U8 = mybir.dt.uint8
ALU = mybir.AluOpType
ACT = mybir.ActivationFunctionType
AX_X = mybir.AxisListType.X

P = 128
BLK = 512
CH = 128
NCH = BLK // CH
LEVELS = [1, 2, 4, 8, 16, 32, 64]
DK, DV, HEADS = 64, 128, 4
RANK = 16
LN_EPS, RMS_EPS = 1e-5, 1e-6
ALPHA = 2.0 ** 0.25
TAU = 16.0
RAW = 2
RING = 4

J_OUT_A, J_XQ, J_Q, J_OUT_B, J_K, J_C0, J_H0, J_V = 0, 4, 6, 8, 12, 14, 15, 16
J_B0, J_G0, J_G1, J_C1, J_H1, J_B1, J_G2, J_G3 = range(20, 28)
GATE_TILE = [J_G0, J_G1, J_G2, J_G3]
SC_XT, SC_XA, SC_GLA, SC_USES = 0, 4, 12, 20
OB_XA, OB_GLA, OB_USES = 0, 4, 12
AUX_LOW, AUX_GATE, AUX_GLA, AUX_PAIR, AUX_USES = 0, 1, 3, 7, 17
ACT_STEPS_FIRST, ACT_STEPS = 12, 24
DVE_STEPS_FIRST, DVE_STEPS = 144, 156
K_ORDER = [3, 0, 2, 1]
K_READY = [2, 5, 6, 8]
Y_TILE = [6, 7, 4, 0, 1, 5, 2, 3]


def three_products(pe):
    def three(dst, a_hi, a_lo, b_hi, b_lo, first, last):
        pe.matmul(dst, a_hi, b_lo, start=first, stop=False)
        pe.matmul(dst, a_lo, b_hi, start=False, stop=False)
        return pe.matmul(dst, a_hi, b_hi, start=False, stop=last)
    return three


def hybrid_layer(nc, x, mem, w_in, w_gate_up, b_gate, conv_w, gla_norm_g, w_mem_kv, w_out,
                 ln1_g, ln1_b, w_ff1, w_ff2, ln2_g, ln2_b, normed, out):
    S, D = x.shape[1], x.shape[2]
    KT = D // P
    NBLK = S // BLK
    DFF = w_ff1.shape[2]
    M = mem.shape[1]
    HALF = S // 2
    NT = HALF // P
    NFB = DFF // (2 * P)
    assert (KT, NBLK, M) == (8, 4, 256)

    x_rows = x[0]
    out_rows = out[0]
    win_v = w_in[0].rearrange("(k p) n -> p k n", p=P)
    wout_v = w_out[0].rearrange("(k p) n -> p k n", p=P)
    wkv_v = w_mem_kv[0].rearrange("(k p) n -> p k n", p=P)
    w1_v = w_ff1[0].rearrange("(k p) n -> p k n", p=P)
    w2_rows = w_ff2[0]
    COL_Q, COL_V, COL_G = 0, 512, 1024
    COL_LOW = 1536
    COL_B, COL_C, COL_H, COL_XQ = 1552, 1808, 2064, 2320
    SLOT_COL = {J_Q: 0, J_Q + 1: 128, J_K: 256, J_K + 1: 384, J_XQ: COL_XQ, J_XQ + 1: COL_XQ + 128,
                J_C0: COL_C, J_H0: COL_H, J_B0: COL_B, J_C1: COL_C + 128, J_H1: COL_H + 128, J_B1: COL_B + 128,
                J_G0: COL_G, J_G1: COL_G + 128, J_G2: COL_G + 256, J_G3: COL_G + 384}

    def slot_source(j):
        for half, j0 in ((0, J_OUT_A), (1, J_OUT_B)):
            if j0 <= j < j0 + 4:
                k = 2 * K_ORDER[j - j0]
                return wout_v[:, k:k + 2, 512 * half:512 * half + 512]
        if J_V <= j < J_V + 4:
            return win_v[:, 2 * (j - J_V):2 * (j - J_V) + 2, COL_V:COL_V + 512]
        return win_v[:, :, SLOT_COL[j]:SLOT_COL[j] + P]

    with ExitStack() as ctx:
        def sb(name, shape, dt=F32):
            return ctx.enter_context(nc.sbuf_tensor(name, shape, dt))

        def sem(name):
            return ctx.enter_context(nc.semaphore(name))

        raw = sb("raw", [P, RAW, 1024])
        w_hi = sb("w_hi", [P, RING, 1024], F32R)
        w_lo = sb("w_lo", [P, RING, 1024], F32R)
        rows = sb("rows", [P, 4, D])
        xT_hi = sb("xT_hi", [P, KT, BLK], F32R)
        xT_lo = sb("xT_lo", [P, KT, BLK], F32R)
        y_hi = sb("y_hi", [P, KT, BLK], F32R)
        y_lo = sb("y_lo", [P, KT, BLK], F32R)
        qT = sb("qT", [P, 2, BLK])
        kT = sb("kT", [P, 2, BLK])
        v_rows = sb("v_rows", [P, NCH, HEADS * DV])
        xqT = sb("xqT", [P, 2, BLK])
        u = sb("u", [P, 2, BLK + 2])
        gate = sb("gate", [P, 2, BLK])
        k_dec = sb("k_dec", [P, BLK])
        b_last = sb("b_last", [P, 2, NCH])
        decay_last = sb("decay_last", [P, NCH])
        k_lev = sb("k_lev", [P, 5, BLK])
        k_top = sb("k_top", [P, NCH, 64])
        q_lev = sb("q_lev", [P, 7, BLK // 2])
        q_dec = sb("q_dec", [P, BLK])
        probs = sb("probs", [P, 2, CH])
        k_dec_rows = sb("k_dec_rows", [P, NCH, P])
        state = sb("state", [P, 2, 2, DV])
        oT = sb("oT", [P, 2, BLK])
        rr = sb("rr", [P, 2, BLK])
        gin = sb("gin", [P, 2, BLK])
        y_raw = sb("y_raw", [P, 2, BLK])
        xy_raw = sb("xy_raw", [P, 2, BLK])
        xp = sb("xp", [P, 4, M])
        xpT = sb("xpT", [P, 2, 4 * P])
        mkT = sb("mkT", [P, 2, M])
        mv = sb("mv", [P, 2, 256])
        masks = sb("masks", [P, 6, 64], U8)
        ident = sb("ident", [P, P])
        ones = sb("ones", [P, P])
        mean_w = sb("mean_w", [P, P])
        low_hi = sb("low_hi", [P, KT, RANK], F32R)
        low_lo = sb("low_lo", [P, KT, RANK], F32R)
        w_gate = sb("w_gate", [RANK, 256])
        gate_bias = sb("gate_bias", [P, 2])
        rms_g = sb("rms_g", [P, 1])
        taps = sb("taps", [P, 2, 3])
        eps_rms = sb("eps_rms", [P, 1])
        eps_ln = sb("eps_ln", [P, 1])
        stats = sb("stats", [P, 4, 2, 6])
        mvar = sb("mvar", [P, 4, 2])
        rstd = sb("rstd", [P, 4])
        nmean = sb("nmean", [P, 4])
        xmax = sb("xmax", [P, 4])
        xnmax = sb("xnmax", [P, 4])
        xsum = sb("xsum", [P, 4])
        xrec = sb("xrec", [P, 4])
        lowT = y_raw[0:RANK, 1, :]
        low_raw = gin[:, 0, 0:KT * RANK].rearrange("p (k n) -> p k n", k=KT)
        mask_f = gin[:, 1, 0:384].rearrange("p (l n) -> p l n", l=6)

        main = [ctx.enter_context(nc.psum_tensor(f"main{i}", [P, 512], F32)) for i in range(RING)]
        sc = [ctx.enter_context(nc.psum_tensor(f"sc{i}", [P, 512], F32)) for i in range(2)]
        ob = ctx.enter_context(nc.psum_tensor("ob", [P, 512], F32))
        aux = ctx.enter_context(nc.psum_tensor("aux", [P, 512], F32))

        raw_landed = [sem(f"raw_landed{i}") for i in range(RAW)]
        hi_done, lo_done, row_used = sem("hi_done"), sem("lo_done"), sem("row_used")
        main_done = sem("main_done")
        main_free = [sem(f"main_free{i}") for i in range(RING)]
        sc_done = [sem(f"sc_done{i}") for i in range(2)]
        sc_free = [sem(f"sc_free{i}") for i in range(2)]
        ob_done, ob_free = sem("ob_done"), sem("ob_free")
        aux_done, aux_free = sem("aux_done"), sem("aux_free")
        x_landed = [sem(f"x_landed{i}") for i in range(4)]
        res_landed = [sem(f"res_landed{i}") for i in range(4)]
        stored = [sem(f"stored{i}") for i in range(4)]
        mem_landed = [sem(f"mem_landed{i}") for i in range(2)]
        small_landed, const_done, const_step = sem("small_landed"), sem("const_done"), sem("const_step")
        xt_hi_done = sem("xt_hi_done")
        low_hi_done, low_split = sem("low_hi_done"), sem("low_split")
        ln_stats, ln_rstd, ln_out = sem("ln_stats"), sem("ln_rstd"), sem("ln_out")
        soft_ready = sem("soft_ready")
        expo_ready, exp_ready, prep_ready = sem("expo_ready"), sem("exp_ready"), sem("prep_ready")
        sq_ready, rms_ready, on_ready = sem("sq_ready"), sem("rms_ready"), sem("on_ready")
        gin_ready, yraw_ready, yhi_ready, y_ready = sem("gin_ready"), sem("yraw_ready"), sem("yhi_ready"), sem("y_ready")
        xmax_ready, xp_ready = sem("xmax_ready"), sem("xp_ready")
        act_step, dve_step, xy_copied = sem("act_step"), sem("dve_step"), sem("xy_copied")
        block = ctx.enter_context(nc.Block())

        def slot_n(t, j):
            if isinstance(t, int) and t == 0 and j < 8:
                return j
            return 28 * t - 4 + j

        def turn(t, j):
            if isinstance(t, int) and t == 0 and j < 8:
                return j // 4
            return 7 * t - 1 + j // 4

        def raw_turn(t, j):
            if isinstance(t, int) and t == 0 and j < 8:
                return j // RAW
            return (4 // RAW) * (7 * t - 1) + j // RAW

        def following(t, j):
            if isinstance(t, int) and t == 0 and j < 8:
                return 0, j + 8
            return (t, j + 4) if j + 4 < 28 else (t + 1, j + 4 - 28)

        def level_view(tile, s):
            return tile.rearrange("p (n w) -> p n w", w=2 * s)

        class Steps:

            def __init__(self, eng, semaphore, base):
                self.eng, self.semaphore, self.base, self.count = eng, semaphore, base, 0

            def mark(self, ins):
                ins.then_inc(self.semaphore, 1)
                self.count += 1

            def settle(self):
                self.eng.wait_ge(self.semaphore, self.base + self.count)

        @block.sync
        def _(sp):
            def load(t, j, source):
                if not (isinstance(t, int) and slot_n(t, j) < RAW):
                    sp.wait_ge(lo_done, slot_n(t, j) - RAW + 1)
                shape = source.shape
                dst = raw[:, j % RAW, :].rearrange("p (k n) -> p k n", k=shape[1])
                sp.dma_start(dst, source).then_inc(raw_landed[j % RAW], 16)

            for i in range(4):
                src = wkv_v[:, :, P * i:P * i + P] if i < 2 else wkv_v[:, 4 * (i - 2):4 * (i - 2) + 4, 256:512]
                load(0, i, src)
            for j in range(J_XQ, 28):
                if not J_OUT_B <= j < J_OUT_B + 4:
                    load(0, j, slot_source(j))
            with sp.Fori(1, NBLK) as t:
                for j in range(28):
                    load(t, j, slot_source(j))
            for i in range(4):
                load(NBLK, i, slot_source(J_OUT_A + i))
            for i in range(4):
                load(NBLK, 4 + i, slot_source(J_OUT_B + i))

        @block.gpsimd
        def _(pool):
            pool.memset(ident[:, :], 0.0).then_inc(const_step, 1)
            pool.dma_start(rows[:, 2, :], mem[0, 0:P, :]).then_inc(mem_landed[0], 16)
            pool.wait_ge(const_step, 1)
            pool.affine_select(out=ident[:, :], in_=ident[:, :], compare_op=ALU.not_equal, fill=1.0, base=0,
                               pattern=[[-1, P]], channel_multiplier=1).then_inc(const_done, 1)
            pool.dma_start(rows[:, 3, :], mem[0, P:2 * P, :]).then_inc(mem_landed[1], 16)
            for j in range(2):
                pool.dma_start(rows[:, j, :], x_rows[P * j:P * j + P, :]).then_inc(x_landed[j], 16)
            for dst, src in ((low_raw, win_v[:, :, COL_LOW:COL_LOW + RANK]),
                             (w_gate[:, :], w_gate_up[0]),
                             (gate_bias[:, :], b_gate[0].rearrange("(c p) -> p c", p=P)),
                             (rms_g[:, :], gla_norm_g[0].rearrange("(c p) -> p c", p=P))):
                with nc.allow_non_contiguous_dma(reason="a few short rows, once"):
                    pool.dma_start(dst, src).then_inc(small_landed, 16)
            for c in range(2):
                with nc.allow_non_contiguous_dma(reason="a few short rows, once"):
                    pool.dma_start(taps[:, c, :], conv_w[0, :, P * c:P * c + P].rearrange("w p -> p w")).then_inc(
                        small_landed, 16)
            pool.memset(ones[:, :], 1.0).then_inc(const_step, 1)
            pool.memset(mask_f, 1.0).then_inc(const_step, 1)
            for m in range(2):
                pool.wait_ge(sc_done[0], m + 1)
                pool.wait_ge(sc_done[1], m + 1)
                pool.dma_start(rows[:, 2 + m, :], x_rows[P * (2 + m):P * (3 + m), :]).then_inc(x_landed[2 + m], 16)
            pool.wait_ge(const_step, 3)
            for l, s in enumerate(LEVELS[:6]):
                m = mask_f[:, l, :].rearrange("p (n w) -> p n w", w=s)
                pool.affine_select(out=m, in_=m, compare_op=ALU.is_ge, fill=0.0, base=0,
                                   pattern=[[-2 * s, 64 // s], [0, s]], channel_multiplier=1).then_inc(const_step, 1)
            pool.wait_ge(const_step, 9)
            for l, s in enumerate(LEVELS[:6]):
                m = mask_f[:, l, :].rearrange("p (n w) -> p n w", w=s)
                pool.affine_select(out=m, in_=m, compare_op=ALU.is_ge, fill=0.0, base=s - 1,
                                   pattern=[[2 * s, 64 // s], [0, s]], channel_multiplier=-1).then_inc(const_step, 1)
            pool.wait_ge(const_step, 15)
            pool.tensor_copy(masks[:, :, :], mask_f).then_inc(const_done, 1)
            pool.memset(mean_w[:, :], 1.0 / DV).then_inc(const_done, 1)
            pool.memset(k_lev[:, :, :], 0.0).then_inc(const_done, 1)
            pool.memset(state[:, :, :, :], 0.0).then_inc(const_done, 1)
            pool.memset(u[:, :, :], 0.0).then_inc(const_done, 1)
            pool.memset(eps_rms[:, :], RMS_EPS).then_inc(const_done, 1)
            pool.memset(eps_ln[:, :], LN_EPS).then_inc(const_done, 1)

            def load_rows(t, j, landed):
                pool.nop(nofuse=True)
                pool.dma_start(rows[:, j, :], x_rows[bass.ds(BLK * t + P * j, P), :]).then_inc(landed[j], 16)

            def transposed(t, j):
                pool.wait_ge(sc_done[0], SC_USES * t + 2 + SC_XT + j + 1)
                pool.wait_ge(sc_done[1], SC_USES * t + 2 + SC_XT + j + 1)

            def store_normed(t, j):
                pool.wait_ge(ln_out, 4 * (t - 1) + j + 1)
                pool.nop(nofuse=True)
                pool.dma_start(normed[bass.ds(BLK * (t - 1) + P * j, P), :], rows[:, j, :]).then_inc(stored[j], 16)

            def y_low(t, i):
                src = xy_raw[:, i, :] if i < 2 else y_raw[:, i % 2, :]
                pool.wait_ge(yhi_ready, 8 * t + i + 1)
                pool.nop(nofuse=True)
                pool.tensor_tensor(y_lo[:, Y_TILE[i], :], src, y_hi[:, Y_TILE[i], :].bitcast(F32), ALU.subtract
                                   ).then_inc(y_ready, 1)

            for j in range(4):
                transposed(0, j)
                load_rows(1, j, x_landed)
            for i in range(8):
                y_low(0, i)

            def mixer_block(t, next_t, landed):
                for j in range(4):
                    transposed(t, j)
                    load_rows(t - 1, j, res_landed)
                y_low(t, 0)
                y_low(t, 1)
                for j in range(4):
                    store_normed(t, j)
                for j in range(4):
                    pool.wait_ge(stored[j], 16 * t)
                    load_rows(next_t, j, landed)
                for i in range(2, 8):
                    y_low(t, i)

            with pool.Fori(1, NBLK - 1) as t:
                mixer_block(t, t + 1, x_landed)
            mixer_block(NBLK - 1, NBLK - 1, res_landed)
            for j in range(4):
                store_normed(NBLK, j)
            for j in range(4):
                pool.wait_ge(stored[j], 16 * NBLK)

        @block.tensor
        def _(pe):
            three = three_products(pe)

            def transposes(u_sc, j):
                for b in range(2):
                    pe.wait_ge(sc_free[b], u_sc)
                    for k in range(4):
                        src = rows[:, j, P * (4 * b + k):P * (4 * b + k) + P]
                        ins = pe.transpose(sc[b][:, P * k:P * k + P], src, ident[:, :])
                    ins.then_inc(sc_done[b], 1)

            def column_quarter(t, j, q):
                if q == 0:
                    pe.wait_ge(lo_done, slot_n(t, j) + 1)
                    pe.wait_ge(main_free[j % 4], turn(t, j))
                hi = w_hi[:, j % RING, :].rearrange("p (k n) -> p k n", k=KT)
                lo = w_lo[:, j % RING, :].rearrange("p (k n) -> p k n", k=KT)
                for k in (2 * q, 2 * q + 1):
                    ins = three(main[j % 4][:, :], hi[:, k, :], lo[:, k, :], xT_hi[:, k, :], xT_lo[:, k, :],
                                k == 0, k == KT - 1)
                if q == 3:
                    ins.then_inc(main_done, 1)

            def column_tile(t, j):
                for q in range(4):
                    column_quarter(t, j, q)

            def row_piece(t, j0, i, c, a_hi, a_lo, kt0):
                j = j0 + i
                if c == 0:
                    pe.wait_ge(lo_done, slot_n(t, j) + 1)
                if i == 0:
                    pe.wait_ge(main_free[c], turn(t, j0))
                hi = w_hi[:, j % RING, :].rearrange("p (k n) -> p k n", k=2)
                lo = w_lo[:, j % RING, :].rearrange("p (k n) -> p k n", k=2)
                tok = slice(P * c, P * c + P)
                for k in range(2):
                    ins = three(main[c][:, :], a_hi[:, kt0 + k, tok], a_lo[:, kt0 + k, tok], hi[:, k, :],
                                lo[:, k, :], i == 0 and k == 0, i == 3 and k == 1)
                if i == 3:
                    ins.then_inc(main_done, 1)
                elif c == 3:
                    ins.then_inc(row_used, 1)

            def output_piece(t, j0, i, c):
                if j0 == J_OUT_A and c == 0:
                    pe.wait_ge(y_ready, 8 * (t - 1) + K_READY[i])
                row_piece(t, j0, i, c, y_hi, y_lo, 2 * K_ORDER[i])

            def aux_turn(t, use):
                pe.wait_ge(aux_free, AUX_USES * t + use)

            def transpose_k(t, hp):
                pe.wait_ge(prep_ready, 2 * t + hp + 1)
                aux_turn(t, AUX_GLA + AUX_PAIR * hp)
                for c in range(NCH):
                    ins = pe.transpose(aux[:, P * c:P * c + P], k_dec[:, CH * c:CH * c + CH], ident[:, :])
                ins.then_inc(aux_done, 1)

            def score(t, hp, c):
                tok = slice(CH * c, CH * c + CH)
                if c == 0:
                    pe.wait_ge(prep_ready, 2 * t + hp + 1)
                for e in range(2):
                    pe.wait_ge(sc_free[e], SC_USES * t + 2 + SC_GLA + 4 * hp + c)
                    r = slice(64 * e, 64 * e + 64)
                    for l in range(7):
                        if l == 0:
                            k_side = kT[r, hp, tok]
                        elif l < 6:
                            k_side = k_lev[r, l - 1, tok]
                        else:
                            k_side = k_top[r, c, :]
                        rows_out = P if l < 6 else 64
                        pe.matmul(sc[e][0:rows_out, 64 * l:64 * l + 64], k_side, q_lev[r, l, 64 * c:64 * c + 64],
                                  start=True, stop=True)
                    pe.matmul(sc[e][:, 448:449], gate[r, hp, tok], ones[r, 0:1], start=True, stop=True
                              ).then_inc(sc_done[e], 1)

            def attend(t, hp, c):
                tok = slice(CH * c, CH * c + CH)
                for e in range(2):
                    pe.wait_ge(sc_free[e], SC_USES * t + 2 + SC_GLA + 4 * hp + c + 1)
                pe.wait_ge(ob_free, OB_USES * t + OB_GLA + 4 * hp + c)
                aux_turn(t, AUX_GLA + AUX_PAIR * hp + 1 + c)
                if hp == 0:
                    pe.wait_ge(main_free[c], turn(t, J_V) + 1)
                for e in range(2):
                    vh = v_rows[:, c, DV * (2 * hp + e):DV * (2 * hp + e) + DV]
                    pe.matmul(ob[:, DV * e:DV * e + CH], vh, probs[:, e, :], start=True, stop=False)
                    ins = pe.matmul(ob[:, DV * e:DV * e + CH], state[:, hp, e, :], q_dec[:, tok],
                                    start=False, stop=True)
                ins.then_inc(ob_done, 1)
                for e in range(2):
                    vh = v_rows[:, c, DV * (2 * hp + e):DV * (2 * hp + e) + DV]
                    ins = pe.matmul(aux[:, DV * e:DV * e + DV], k_dec_rows[:, c, :], vh, start=True, stop=True)
                ins.then_inc(aux_done, 1)

            def mean_square(t, hp, e):
                aux_turn(t, AUX_GLA + AUX_PAIR * hp + 5 + e)
                pe.wait_ge(sq_ready, 4 * t + 2 * hp + e + 1)
                pe.matmul(aux[:, :], mean_w[:, :], rr[:, e, :], start=True, stop=True).then_inc(aux_done, 1)

            def xattn_score(t, j):
                if j == 0:
                    for i in range(2):
                        pe.wait_ge(main_free[i], turn(t, J_XQ) + 1)
                for e in range(2):
                    pe.wait_ge(sc_free[e], SC_USES * t + 2 + SC_XA + 2 * j)
                    for i in range(2):
                        ins = pe.matmul(sc[e][:, M * i:M * i + M], xqT[64 * e:64 * e + 64, i, P * j:P * j + P],
                                        mkT[64 * e:64 * e + 64, i, :], start=True, stop=True)
                    ins.then_inc(sc_done[e], 1)

            def xattn_transpose(t, j):
                pe.wait_ge(xp_ready, 4 * t + j + 1)
                for m in range(2):
                    pe.wait_ge(sc_free[m], SC_USES * t + 2 + SC_XA + 2 * j + 1)
                    for h in range(4):
                        ins = pe.transpose(sc[m][:, P * h:P * h + P], xp[:, h, P * m:P * m + P], ident[:, :])
                    ins.then_inc(sc_done[m], 1)

            def xattn_attend(t, j):
                pe.wait_ge(sc_free[0], SC_USES * t + 2 + SC_XA + 2 * j + 2)
                pe.wait_ge(sc_free[1], SC_USES * t + 2 + SC_XA + 2 * j + 2)
                pe.wait_ge(ob_free, OB_USES * t + OB_XA + j)
                for h in range(4):
                    for m in range(2):
                        ins = pe.matmul(ob[:, P * h:P * h + P], mv[:, m, P * (h // 2):P * (h // 2) + P],
                                        xpT[:, m, P * h:P * h + P], start=(m == 0), stop=(m == 1))
                ins.then_inc(ob_done, 1)

            def mixer_block(t, with_out):
                def x_transposes(j):
                    pe.wait_ge(x_landed[j], 16 * (t + 1))
                    transposes(SC_USES * t + 2 + SC_XT + j, j)

                for j in range(4):
                    x_transposes(j)
                    if with_out:
                        for c in range(4):
                            output_piece(t, J_OUT_A, j, c)
                pe.wait_ge(sc_free[0], SC_USES * t + 2 + 4)
                pe.wait_ge(sc_free[1], SC_USES * t + 2 + 4)
                aux_turn(t, AUX_LOW)
                for k in range(KT):
                    ins = three(aux[0:RANK, :], low_hi[:, k, :], low_lo[:, k, :], xT_hi[:, k, :], xT_lo[:, k, :],
                                k == 0, k == KT - 1)
                ins.then_inc(aux_done, 1)
                for i in range(2):
                    column_tile(t, J_XQ + i)
                    aux_turn(t, AUX_GATE + i)
                    pe.matmul(aux[:, :], w_gate[:, P * i:P * i + P], lowT, start=True, stop=True
                              ).then_inc(aux_done, 1)
                column_tile(t, J_Q)

                q_fill = [lambda q=q: column_quarter(t, J_Q + 1, q) for q in range(4)]
                out_fill = [lambda i=i, c=c: output_piece(t, J_OUT_B, i, c) for i in range(4) for c in range(4)]
                k_fill = [lambda q=q: column_quarter(t, J_K, q) for q in range(4)]
                if with_out:
                    fill = q_fill + out_fill + k_fill
                    parts = [(fill[6 * j:6 * j + 4], fill[6 * j + 4:6 * j + 6]) for j in range(4)]
                else:
                    fill = q_fill + k_fill + [lambda j=j, q=q: column_quarter(t, j, q)
                                              for j in (J_K + 1, J_C0) for q in range(4)]
                    parts = [(fill[4 * j:4 * j + 3], fill[4 * j + 3:4 * j + 4]) for j in range(4)]
                for j in range(4):
                    xattn_score(t, j)
                    for piece in parts[j][0]:
                        piece()
                    xattn_transpose(t, j)
                    for piece in parts[j][1]:
                        piece()
                    xattn_attend(t, j)

                for j in (J_K + 1, J_C0, J_H0) if with_out else (J_H0,):
                    column_tile(t, j)
                for i in range(4):
                    for c in range(4):
                        row_piece(t, J_V, i, c, xT_hi, xT_lo, 2 * i)
                    if i == 0:
                        transpose_k(t, 0)
                    if i == 2:
                        score(t, 0, 0)
                attend(t, 0, 0)

                done = 0

                def quarters(n):
                    nonlocal done
                    for i in range(done, done + n):
                        column_quarter(t, J_B0 + i // 4, i % 4)
                    done += n

                for c in range(1, NCH):
                    score(t, 0, c)
                    quarters(3)
                    attend(t, 0, c)
                quarters(2)
                mean_square(t, 0, 0)
                quarters(6)
                mean_square(t, 0, 1)
                quarters(1)
                for c in range(NCH):
                    score(t, 1, c)
                    if c == 0:
                        transpose_k(t, 1)
                    quarters(3)
                    attend(t, 1, c)
                quarters(1)
                mean_square(t, 1, 0)
                quarters(1)
                mean_square(t, 1, 1)
                assert done == 32

            pe.wait_ge(const_done, 1)
            for m in range(2):
                pe.wait_ge(mem_landed[m], 16)
                transposes(m, 2 + m)
            pe.wait_ge(sc_free[0], 2)
            pe.wait_ge(sc_free[1], 2)
            for i in range(2):
                pe.wait_ge(lo_done, i + 1)
                for k in range(KT):
                    hi = w_hi[:, i, P * k:P * k + P]
                    lo = w_lo[:, i, P * k:P * k + P]
                    ins = three(main[i][:, 0:M], hi, lo, xT_hi[:, k, 0:M], xT_lo[:, k, 0:M], k == 0, k == KT - 1)
                ins.then_inc(main_done, 1)
            for i in range(2):
                pe.wait_ge(lo_done, 3 + i)
                for m in range(2):
                    for k in range(4):
                        tok = slice(P * m, P * m + P)
                        ins = three(main[2 + m][:, 0:256], xT_hi[:, 4 * i + k, tok], xT_lo[:, 4 * i + k, tok],
                                    w_hi[:, 2 + i, 256 * k:256 * k + 256], w_lo[:, 2 + i, 256 * k:256 * k + 256],
                                    i == 0 and k == 0, i == 1 and k == 3)
                    if i == 1:
                        ins.then_inc(main_done, 1)
            pe.wait_ge(const_done, 8)
            pe.wait_ge(low_split, 1)
            mixer_block(0, False)
            with pe.Fori(1, NBLK) as t:
                mixer_block(t, True)
            for j0, yj in ((0, J_OUT_A), (4, J_OUT_B)):
                for i in range(4):
                    if j0 == 0:
                        pe.wait_ge(y_ready, 8 * (NBLK - 1) + K_READY[i])
                    for c in range(4):
                        row_piece(NBLK, j0, i, c, y_hi, y_lo, 2 * K_ORDER[i])

        def reuse(eng, t, j):
            if isinstance(t, int) and t == 0 and j < 16:
                if 4 <= j < 8:
                    eng.wait_ge(main_done, 4)
                elif j >= 12:
                    eng.wait_ge(main_done, slot_n(0, j - 8) + 1)
                return
            p = j - 4
            group = {0: 0, 8: 1, 16: 2}.get(p - p % 4)
            if isinstance(t, int) and t == NBLK and p >= 4:
                group = 1
            if p < 0 or group is None or p % 4 == 3:
                eng.wait_ge(main_done, slot_n(t, p) + 1)
            else:
                eng.wait_ge(row_used, 9 * t - 6 + 3 * group + p % 4 + 1)

        @block.scalar
        def _(act):
            def split(t, j):
                act.wait_ge(raw_landed[j % RAW], 16 * (raw_turn(t, j) + 1))
                reuse(act, t, j)
                act.activation(w_hi[:, j % RING, :], raw[:, j % RAW, :], ACT.Copy).then_inc(hi_done, 1)

            def next_split(t, j):
                split(*following(t, j))

            def tile_done(t, j):
                act.wait_ge(main_done, slot_n(t, j) + 1)

            def xT_part(n, uses, b, j):
                act.wait_ge(sc_done[b], uses + 1)
                act.activation(xT_hi[:, 4 * b:4 * b + 4, P * j:P * j + P],
                               sc[b][:, :].rearrange("p (k n) -> p k n", k=4), ACT.Copy).then_inc(xt_hi_done, 1)

            def gate_in(t, i):
                if i < 2 and isinstance(t, int) and t == 0:
                    return
                if i in (2, 5):
                    j = J_H0 if i == 2 else J_H1
                    act.wait_ge(main_free[j % 4], turn(t, j) + 1)
                else:
                    act.wait_ge(yraw_ready, 6 * t + {0: -1, 1: 0, 3: 2, 4: 3}[i])

            def y_part(t, i):
                if i < 2:
                    if not (isinstance(t, int) and t == 0):
                        tile_done(t, J_OUT_B + 3)
                    src = xy_raw[:, i, :]
                    act.wait_ge(xy_copied, 4 * t + 4)
                    act.wait_ge(ob_free, OB_USES * t + OB_XA + 4)
                else:
                    act.wait_ge(yraw_ready, 6 * t + i - 2 + 1)
                    src = y_raw[:, i % 2, :]
                act.activation(y_hi[:, Y_TILE[i], :], src, ACT.Copy).then_inc(yhi_ready, 1)

            def gate_copy(t, h, steps):
                act.wait_ge(aux_done, AUX_USES * t + AUX_GATE + h + 1)
                act.activation(gate[:, h, :], aux[:, :], ACT.Identity, bias=gate_bias[:, h:h + 1]
                               ).then_inc(aux_free, 1)
                act.wait_ge(aux_free, AUX_USES * t + AUX_GATE + h + 1)
                act.wait_ge(on_ready, 4 * t)
                steps.mark(act.activation(rr[:, h, :], gate[:, h, :], ACT.Abs))
                steps.settle()
                steps.mark(act.activation(rr[:, h, :], rr[:, h, :], ACT.Exp, scale=-1.0))
                steps.settle()
                act.activation(rr[:, h, :], rr[:, h, :], ACT.Ln, bias=ones[:, 0:1]).then_inc(soft_ready, 1)

            def exponentials(t, hp):
                act.wait_ge(expo_ready, 4 * t + 2 * hp + 1)
                act.activation(q_lev[:, :, :], q_lev[:, :, :], ACT.Exp, scale=1.0 / TAU).then_inc(exp_ready, 1)
                act.wait_ge(expo_ready, 4 * t + 2 * hp + 2)
                for l in range(1, 6):
                    view = level_view(k_lev[:, l - 1, :], LEVELS[l])[:, :, 0:LEVELS[l]]
                    act.activation(view, view, ACT.Exp, scale=1.0 / TAU)
                act.activation(k_top[:, :, :], k_top[:, :, :], ACT.Exp, scale=1.0 / TAU)
                act.activation(k_dec[:, :], k_dec[:, :], ACT.Exp, scale=1.0 / TAU)
                if hp == 1:
                    act.wait_ge(ob_done, OB_USES * t + OB_GLA + 4)
                act.activation(q_dec[:, :], gate[:, hp, :], ACT.Exp, scale=1.0 / TAU)
                act.activation(decay_last[:, :], b_last[:, hp, :], ACT.Exp, scale=1.0 / TAU).then_inc(exp_ready, 1)

            def copy_k_dec(t, hp):
                act.wait_ge(aux_done, AUX_USES * t + AUX_GLA + AUX_PAIR * hp + 1)
                act.activation(k_dec_rows[:, :, :], aux[:, :].rearrange("p (c n) -> p c n", c=NCH), ACT.Copy
                               ).then_inc(aux_free, 1)

            def copy_o(t, hp, c):
                act.wait_ge(ob_done, OB_USES * t + OB_GLA + 4 * hp + c + 1)
                if c == 0:
                    act.wait_ge(yraw_ready, 6 * t + 3 * hp)
                act.activation(oT[:, :, CH * c:CH * c + CH], ob[:, 0:2 * CH].rearrange("p (e n) -> p e n", e=2),
                               ACT.Copy).then_inc(ob_free, 1)

            def square(t, hp):
                act.wait_ge(on_ready, 4 * t + 2 * hp)
                act.wait_ge(ob_free, OB_USES * t + OB_GLA + 4 * hp + 4)
                for e in range(2):
                    act.activation(rr[:, e, :], oT[:, e, :], ACT.Square).then_inc(sq_ready, 1)

            def inverse_rms(t, hp, e):
                use = AUX_USES * t + AUX_GLA + AUX_PAIR * hp + 5 + e
                act.wait_ge(aux_done, use + 1)
                act.activation(rr[:, e, :], aux[:, :], ACT.Ln, bias=eps_rms[:, :]).then_inc(aux_free, 1)
                act.wait_ge(aux_free, use + 1)
                act.activation(rr[:, e, :], rr[:, e, :], ACT.Exp, scale=-0.5).then_inc(rms_ready, 1)

            def sigmoid(t, g, steps):
                tile_done(t, GATE_TILE[g])
                use = (1, 2, 4, 5)[g]
                gate_in(t, use)
                buf = gin[:, use % 2, :]
                steps.mark(act.activation(buf, main[GATE_TILE[g] % 4][:, :], ACT.Exp, scale=-1.0))
                steps.settle()
                steps.mark(act.activation(buf, buf, ACT.Ln, bias=ones[:, 0:1]))
                steps.settle()
                act.activation(buf, buf, ACT.Exp, scale=-1.0).then_inc(gin_ready, 1)

            def conv_c(t, ch):
                j = (J_C0, J_C1)[ch]
                tile_done(t, j)
                gate_in(t, 3 * ch)
                act.activation(gin[:, ch, :], main[j % 4][:, :], ACT.Copy).then_inc(main_free[j % 4], 1)

            def copy_tile(t, j, dst, scale=1.0):
                tile_done(t, j)
                act.activation(dst, main[j % 4][:, :], ACT.Copy, scale=scale).then_inc(main_free[j % 4], 1)

            def normalise(t, c, steps):
                act.wait_ge(ln_stats, 4 * (t - 1) + c + 1)
                steps.mark(act.activation(rstd[:, c:c + 1], mvar[:, c, 1:2], ACT.Ln, bias=eps_ln[:, :]))
                steps.settle()
                steps.mark(act.activation(rstd[:, c:c + 1], rstd[:, c:c + 1], ACT.Exp, scale=-0.5))
                steps.settle()
                steps.mark(act.activation(nmean[:, c:c + 1], nmean[:, c:c + 1], ACT.Copy, scale=rstd[:, c:c + 1]))
                steps.settle()
                act.activation(rows[:, c, :], rows[:, c, :], ACT.Identity, scale=rstd[:, c:c + 1],
                               bias=nmean[:, c:c + 1]).then_inc(ln_out, 1)

            def mixer_block(t, with_out, steps):
                for j in range(4):
                    for b in range(2):
                        xT_part(8 * t + 4 + 2 * j + b, SC_USES * t + 2 + SC_XT + j, b, j)
                    if with_out and j > 0:
                        next_split(t, J_OUT_A + j - 1)
                    elif not with_out and j in (0, 2):
                        split(0, J_XQ + j)
                        split(0, J_XQ + j + 1)
                if with_out:
                    next_split(t, J_OUT_A + 3)
                act.wait_ge(aux_done, AUX_USES * t + AUX_LOW + 1)
                act.wait_ge(y_ready, 8 * t)
                act.activation(lowT, aux[0:RANK, :], ACT.Copy).then_inc(aux_free, 1)
                for i in range(2):
                    copy_tile(t, J_XQ + i, xqT[:, i, :], DK ** -0.5)
                    gate_copy(t, i, steps)
                    next_split(t, J_XQ + i)
                copy_tile(t, J_Q, qT[:, 0, :], DK ** -0.5)
                next_split(t, J_Q)
                for j in range(4):
                    act.wait_ge(xmax_ready, 4 * t + j + 1)
                    for e in range(2):
                        act.wait_ge(sc_done[e], SC_USES * t + 2 + SC_XA + 2 * j + 1)
                        for i in range(2):
                            ins = act.activation(xp[:, 2 * i + e, :], sc[e][:, M * i:M * i + M], ACT.Exp,
                                                 bias=xnmax[:, 2 * e + i:2 * e + i + 1],
                                                 accum_out=xsum[:, 2 * i + e:2 * i + e + 1])
                        ins.then_inc(sc_free[e], 1)
                    act.wait_ge(sc_done[0], SC_USES * t + 2 + SC_XA + 2 * j + 2)
                    act.activation(xpT[:, 0, :], sc[0][:, :], ACT.Copy).then_inc(sc_free[0], 1)
                    if j == 0:
                        copy_tile(t, J_Q + 1, qT[:, 1, :], DK ** -0.5)
                        next_split(t, J_Q + 1)
                    elif with_out:
                        next_split(t, J_OUT_B + j - 1)
                    if j == 1:
                        exponentials(t, 0)
                    act.wait_ge(ob_done, OB_USES * t + OB_XA + j + 1)
                    for e in range(2):
                        r = slice(64 * e, 64 * e + 64)
                        src = ob[r, :].rearrange("p (i e n) -> p i e n", i=2, e=2)[:, :, e, :]
                        ins = act.activation(xy_raw[r, :, P * j:P * j + P], src, ACT.Copy)
                        if e == 0:
                            ins.then_inc(xy_copied, 1)
                        else:
                            ins.then_inc(ob_free, 1)
                if with_out:
                    next_split(t, J_OUT_B + 3)
                copy_tile(t, J_K, kT[:, 0, :])
                next_split(t, J_K)
                y_part(t, 0)
                y_part(t, 1)
                copy_tile(t, J_K + 1, kT[:, 1, :])
                next_split(t, J_K + 1)
                conv_c(t, 0)
                next_split(t, J_C0)
                next_split(t, J_H0)
                if with_out:
                    for c in range(4):
                        normalise(t, c, steps)
                copy_k_dec(t, 0)
                for i in range(3):
                    next_split(t, J_V + i)
                for i in range(4):
                    copy_tile(t, J_V + i, v_rows[:, i, :])
                next_split(t, J_V + 3)
                copy_o(t, 0, 0)
                copy_o(t, 0, 1)
                next_split(t, J_B0)
                copy_o(t, 0, 2)
                sigmoid(t, 0, steps)
                copy_o(t, 0, 3)
                next_split(t, J_G0)
                square(t, 0)
                exponentials(t, 1)
                inverse_rms(t, 0, 0)
                sigmoid(t, 1, steps)
                next_split(t, J_G1)
                y_part(t, 2)
                inverse_rms(t, 0, 1)
                next_split(t, J_C1)
                copy_k_dec(t, 1)
                y_part(t, 3)
                conv_c(t, 1)
                y_part(t, 4)
                copy_o(t, 1, 0)
                next_split(t, J_H1)
                copy_o(t, 1, 1)
                next_split(t, J_B1)
                copy_o(t, 1, 2)
                sigmoid(t, 2, steps)
                next_split(t, J_G2)
                copy_o(t, 1, 3)
                square(t, 1)
                y_part(t, 5)
                inverse_rms(t, 1, 0)
                inverse_rms(t, 1, 1)
                sigmoid(t, 3, steps)
                next_split(t, J_G3)
                y_part(t, 6)
                y_part(t, 7)

            nc.scalar.preload_act_table_set("natural_log_exp_and_others")
            split(0, 0)
            split(0, 1)
            for m in range(2):
                for b in range(2):
                    xT_part(0, m, b, m)
            split(0, 2)
            split(0, 3)
            act.wait_ge(small_landed, 16 * 6)
            act.wait_ge(const_done, 2)
            act.activation(low_hi[:, :, :], low_raw, ACT.Copy).then_inc(low_hi_done, 1)
            for i in range(4):
                act.wait_ge(main_done, i + 1)
                if i < 2:
                    act.activation(mkT[:, i, :], main[i][:, 0:M], ACT.Copy).then_inc(main_free[i], 1)
                else:
                    act.activation(mv[:, i - 2, :], main[i][:, 0:256], ACT.Copy).then_inc(main_free[i], 1)
            act.wait_ge(const_done, 8)
            steps = Steps(act, act_step, 0)
            mixer_block(0, False, steps)
            assert steps.count == ACT_STEPS_FIRST, steps.count
            with act.Fori(1, NBLK) as t:
                steps = Steps(act, act_step, ACT_STEPS_FIRST + ACT_STEPS * (t - 1))
                mixer_block(t, True, steps)
                assert steps.count == ACT_STEPS, steps.count
            steps = Steps(act, act_step, ACT_STEPS_FIRST + ACT_STEPS * (NBLK - 1))
            for i in range(4):
                split(NBLK, 4 + i)
            for c in range(4):
                normalise(NBLK, c, steps)

        @block.vector
        def _(dve):
            def split(t, j):
                dve.wait_ge(hi_done, slot_n(t, j) + 1)
                dve.tensor_tensor(w_lo[:, j % RING, :], raw[:, j % RAW, :], w_hi[:, j % RING, :].bitcast(F32),
                                  ALU.subtract).then_inc(lo_done, 1)

            def next_split(t, j):
                split(*following(t, j))

            def tile_done(t, j):
                dve.wait_ge(main_done, slot_n(t, j) + 1)

            def xT_part(n, b, j):
                dve.wait_ge(xt_hi_done, n + 1)
                dst = (slice(None), slice(4 * b, 4 * b + 4), slice(P * j, P * j + P))
                dve.tensor_tensor(xT_lo[dst], sc[b][:, :].rearrange("p (k n) -> p k n", k=4), xT_hi[dst].bitcast(F32),
                                  ALU.subtract).then_inc(sc_free[b], 1)

            def log_decays(t, hp, steps):
                dve.wait_ge(soft_ready, 2 * t + hp + 1)
                steps.mark(dve.scalar_tensor_tensor(out=gate[:, hp, :], in0=gate[:, hp, :], scalar=0.0,
                                                    in1=rr[:, hp, :], op0=ALU.min, op1=ALU.subtract))
                steps.settle()
                for c in range(NCH):
                    steps.mark(dve.tensor_tensor_scan(gate[:, hp, CH * c:CH * c + CH], ones[:, :],
                                                      gate[:, hp, CH * c:CH * c + CH], 0.0, ALU.mult, ALU.add))
                steps.settle()
                steps.mark(dve.tensor_copy(b_last[:, hp, :], gate[:, hp, CH - 1:BLK:CH]))
                steps.settle()

            def exponents_q(t, hp):
                for l, s in enumerate(LEVELS):
                    b = level_view(gate[:, hp, :], s)
                    ref = b[:, :, s - 1:s].to_broadcast([P, BLK // (2 * s), s])
                    ins = dve.tensor_tensor(q_lev[:, l, :].rearrange("p (n w) -> p n w", w=s), b[:, :, s:2 * s], ref,
                                            ALU.subtract)
                ins.then_inc(expo_ready, 1)

            def k_side(l):
                s = LEVELS[l]
                return k_top[:, :, :] if l == 6 else level_view(k_lev[:, l - 1, :], s)[:, :, 0:s]

            def exponents_k(t, hp):
                for l in range(1, 7):
                    s = LEVELS[l]
                    b = level_view(gate[:, hp, :], s)
                    ref = b[:, :, s - 1:s].to_broadcast([P, BLK // (2 * s), s])
                    dve.tensor_tensor(k_side(l), ref, b[:, :, 0:s], ALU.subtract)
                dve.tensor_tensor(k_dec[:, :].rearrange("p (c w) -> p c w", w=CH),
                                  b_last[:, hp, :].unsqueeze(2).to_broadcast([P, NCH, CH]),
                                  gate[:, hp, :].rearrange("p (c w) -> p c w", w=CH), ALU.subtract
                                  ).then_inc(expo_ready, 1)

            def decayed(t, hp):
                for j in (J_Q + hp, J_K + hp):
                    dve.wait_ge(main_free[j % 4], turn(t, j) + 1)
                dve.wait_ge(exp_ready, 4 * t + 2 * hp + 1)
                for l, s in enumerate(LEVELS):
                    dst = q_lev[:, l, :].rearrange("p (n w) -> p n w", w=s)
                    dve.tensor_tensor(dst, dst, level_view(qT[:, hp, :], s)[:, :, s:2 * s], ALU.mult)
                dve.wait_ge(exp_ready, 4 * t + 2 * hp + 2)
                dve.tensor_tensor(gate[:, hp, :], qT[:, hp, :], kT[:, hp, :], ALU.mult)
                for l, s in enumerate(LEVELS[1:], 1):
                    dve.tensor_tensor(k_side(l), k_side(l), level_view(kT[:, hp, :], s)[:, :, 0:s], ALU.mult)
                dve.tensor_tensor(q_dec[:, :], q_dec[:, :], qT[:, hp, :], ALU.mult)
                dve.tensor_tensor(k_dec[:, :], k_dec[:, :], kT[:, hp, :], ALU.mult).then_inc(prep_ready, 1)

            def mask_scores(t, hp, c, steps):
                for e in range(2):
                    dve.wait_ge(sc_done[e], SC_USES * t + 2 + SC_GLA + 4 * hp + c + 1)
                    steps.mark(dve.tensor_scalar(probs[:, e, :], ident[:, :], sc[e][:, 448:449], None, ALU.mult))
                steps.settle()
                for e in range(2):
                    steps.mark(dve.tensor_copy(probs[0:64, e, 64:128], sc[e][0:64, 384:448]))
                for l, s in enumerate(LEVELS[:6]):
                    steps.settle()
                    dve.nop(nofuse=True)
                    for e in range(2):
                        ins = dve.copy_predicated(level_view(probs[:, e, :], s)[:, :, s:2 * s],
                                                  masks[:, l, :].rearrange("p (n w) -> p n w", w=s),
                                                  sc[e][:, 64 * l:64 * l + 64].rearrange("p (n w) -> p n w", w=s))
                        if l == 5:
                            ins.then_inc(sc_free[e], 1)
                        else:
                            steps.mark(ins)

            def update_state(t, hp, c):
                dve.wait_ge(aux_done, AUX_USES * t + AUX_GLA + AUX_PAIR * hp + 1 + c + 1)
                for e in range(2):
                    r = slice(64 * e, 64 * e + 64)
                    ins = dve.scalar_tensor_tensor(out=state[r, hp, e, :], in0=state[r, hp, e, :],
                                                   scalar=decay_last[r, c:c + 1], in1=aux[r, DV * e:DV * e + DV],
                                                   op0=ALU.mult, op1=ALU.add)
                ins.then_inc(aux_free, 1)

            def normalise_o(t, hp):
                for e in range(2):
                    dve.wait_ge(rms_ready, 4 * t + 2 * hp + e + 1)
                    dve.scalar_tensor_tensor(out=oT[:, e, :], in0=oT[:, e, :], scalar=rms_g[:, 0:1], in1=rr[:, e, :],
                                             op0=ALU.mult, op1=ALU.mult).then_inc(on_ready, 1)

            def silu(t, g):
                j, use = GATE_TILE[g], (1, 2, 4, 5)[g]
                buf = gin[:, use % 2, :]
                dve.wait_ge(gin_ready, 4 * t + g + 1)
                dve.tensor_tensor(buf, buf, main[j % 4][:, :], ALU.mult).then_inc(main_free[j % 4], 1)

            def y_place(t, i):
                dve.wait_ge(y_ready, 8 * t + max(i - 1, 2))

            def gated(t, g):
                j, use, i = GATE_TILE[g], (1, 2, 4, 5)[g], (3, 4, 6, 7)[g]
                dve.wait_ge(on_ready, 4 * t + g + 1)
                dve.wait_ge(main_free[j % 4], turn(t, j) + 1)
                y_place(t, i)
                dve.tensor_tensor(y_raw[:, i % 2, :], oT[:, g % 2, :], gin[:, use % 2, :], ALU.mult
                                  ).then_inc(yraw_ready, 1)

            def conv_input(t, ch, j, steps):
                steps.mark(dve.tensor_copy(u[:, ch, 0:2], u[:, ch, BLK:BLK + 2]))
                steps.settle()
                tile_done(t, j)
                c_tile = J_C0 if ch == 0 else J_C1
                dve.wait_ge(main_free[c_tile % 4], turn(t, c_tile) + 1)
                dve.tensor_tensor(u[:, ch, 2:BLK + 2], gin[:, ch, :], main[j % 4][:, :], ALU.mult
                                  ).then_inc(main_free[j % 4], 1)

            def conv(t, ch, j, steps):
                acc = y_raw[:, ch, :]
                h_tile = J_H0 if ch == 0 else J_H1
                dve.wait_ge(main_free[h_tile % 4], turn(t, h_tile) + 1)
                y_place(t, 2 + 3 * ch)
                steps.mark(dve.tensor_scalar(acc, u[:, ch, 0:BLK], taps[:, ch, 0:1], None, ALU.mult))
                for w in (1, 2):
                    steps.settle()
                    steps.mark(dve.scalar_tensor_tensor(out=acc, in0=u[:, ch, w:w + BLK], scalar=taps[:, ch, w:w + 1],
                                                        in1=acc, op0=ALU.mult, op1=ALU.add))
                steps.settle()
                tile_done(t, j)
                dve.tensor_tensor(acc, acc, main[j % 4][:, :], ALU.mult).then_inc(yraw_ready, 1)
                dve.wait_ge(yraw_ready, 6 * t + 3 * ch + 1)
                dve.tensor_copy(xmax[:, 0:1], main[j % 4][:, 0:1]).then_inc(main_free[j % 4], 1)

            def output_tile(t, j0, half, c):
                tile_done(t, j0 + c)
                if half == 0:
                    dve.wait_ge(res_landed[c], 16 * t)
                dst = rows[:, c, 512 * half:512 * half + 512]
                dve.scalar_tensor_tensor(out=dst, in0=dst, scalar=ALPHA, in1=main[c][:, :],
                                         op0=ALU.mult, op1=ALU.add).then_inc(main_free[c], 1)

            def statistics(t, j0, c, steps):
                dve.wait_ge(main_free[c], turn(t, j0) + 1)
                for i in range(2):
                    steps.mark(dve.bn_stats(stats[:, c, i, :], rows[:, c, 512 * i:512 * i + 512]))
                steps.settle()
                dve.nop(nofuse=True)
                steps.mark(dve.bn_aggr(mvar[:, c, :], stats[:, c, :, :]))
                steps.settle()
                dve.tensor_scalar(nmean[:, c:c + 1], mvar[:, c, 0:1], -1.0, None, ALU.mult).then_inc(ln_stats, 1)

            def softmax_max(t, j, steps):
                for e in range(2):
                    dve.wait_ge(sc_done[e], SC_USES * t + 2 + SC_XA + 2 * j + 1)
                    steps.mark(dve.tensor_reduce(xmax[:, 2 * e:2 * e + 2],
                                                 sc[e][:, :].rearrange("p (i m) -> p i m", i=2), AX_X, ALU.max))
                steps.settle()
                dve.tensor_scalar(xnmax[:, :], xmax[:, :], -1.0, None, ALU.mult).then_inc(xmax_ready, 1)

            def softmax_norm(t, j, steps):
                for e in range(2):
                    dve.wait_ge(sc_free[e], SC_USES * t + 2 + SC_XA + 2 * j + 1)
                steps.mark(dve.reciprocal(xrec[:, :], xsum[:, :]))
                steps.settle()
                for h in range(4):
                    ins = dve.tensor_scalar(xp[:, h, :], xp[:, h, :], xrec[:, h:h + 1], None, ALU.mult)
                ins.then_inc(xp_ready, 1)

            def mixer_block(t, with_out, steps):
                for j in range(4):
                    for b in range(2):
                        xT_part(8 * t + 4 + 2 * j + b, b, j)
                    if with_out and j > 0:
                        next_split(t, J_OUT_A + j - 1)
                    elif not with_out and j in (0, 2):
                        split(0, J_XQ + j)
                        split(0, J_XQ + j + 1)
                if with_out:
                    next_split(t, J_OUT_A + 3)
                    for c in range(4):
                        output_tile(t, J_OUT_A, 0, c)
                for i in range(2):
                    next_split(t, J_XQ + i)
                    log_decays(t, i, steps)
                next_split(t, J_Q)
                for j in range(4):
                    softmax_max(t, j, steps)
                    if j == 0:
                        exponents_q(t, 0)
                    if j == 3 and with_out:
                        output_tile(t, J_OUT_B, 1, 0)
                        output_tile(t, J_OUT_B, 1, 1)
                    softmax_norm(t, j, steps)
                    if j == 3 and with_out:
                        output_tile(t, J_OUT_B, 1, 2)
                        output_tile(t, J_OUT_B, 1, 3)
                    dve.wait_ge(sc_done[1], SC_USES * t + 2 + SC_XA + 2 * j + 2)
                    dve.tensor_copy(xpT[:, 1, :], sc[1][:, :]).then_inc(sc_free[1], 1)
                    if j == 0:
                        exponents_k(t, 0)
                        next_split(t, J_Q + 1)
                    elif with_out:
                        next_split(t, J_OUT_B + j - 1)
                if with_out:
                    next_split(t, J_OUT_B + 3)
                decayed(t, 0)
                next_split(t, J_K)
                next_split(t, J_K + 1)
                if with_out:
                    statistics(t, J_OUT_B, 0, steps)
                    statistics(t, J_OUT_B, 1, steps)
                next_split(t, J_C0)
                conv_input(t, 0, J_H0, steps)
                next_split(t, J_H0)
                if with_out:
                    statistics(t, J_OUT_B, 2, steps)
                    statistics(t, J_OUT_B, 3, steps)
                for i in range(3):
                    next_split(t, J_V + i)
                mask_scores(t, 0, 0, steps)
                next_split(t, J_V + 3)
                update_state(t, 0, 0)
                mask_scores(t, 0, 1, steps)
                update_state(t, 0, 1)
                mask_scores(t, 0, 2, steps)
                next_split(t, J_B0)
                update_state(t, 0, 2)
                mask_scores(t, 0, 3, steps)
                silu(t, 0)
                exponents_q(t, 1)
                update_state(t, 0, 3)
                exponents_k(t, 1)
                next_split(t, J_G0)
                conv(t, 0, J_B0, steps)
                decayed(t, 1)
                next_split(t, J_G1)
                mask_scores(t, 1, 0, steps)
                normalise_o(t, 0)
                gated(t, 0)
                silu(t, 1)
                gated(t, 1)
                update_state(t, 1, 0)
                next_split(t, J_C1)
                mask_scores(t, 1, 1, steps)
                conv_input(t, 1, J_H1, steps)
                update_state(t, 1, 1)
                next_split(t, J_H1)
                mask_scores(t, 1, 2, steps)
                update_state(t, 1, 2)
                next_split(t, J_B1)
                mask_scores(t, 1, 3, steps)
                conv(t, 1, J_B1, steps)
                update_state(t, 1, 3)
                silu(t, 2)
                next_split(t, J_G2)
                normalise_o(t, 1)
                gated(t, 2)
                silu(t, 3)
                gated(t, 3)
                next_split(t, J_G3)

            split(0, 0)
            split(0, 1)
            for m in range(2):
                for b in range(2):
                    xT_part(2 * m + b, b, m)
            split(0, 2)
            split(0, 3)
            dve.wait_ge(low_hi_done, 1)
            dve.tensor_tensor(low_lo[:, :, :], low_raw, low_hi[:, :, :].bitcast(F32), ALU.subtract
                              ).then_inc(low_split, 1)
            dve.wait_ge(const_done, 8)
            steps = Steps(dve, dve_step, 0)
            mixer_block(0, False, steps)
            assert steps.count == DVE_STEPS_FIRST, steps.count
            with dve.Fori(1, NBLK) as t:
                steps = Steps(dve, dve_step, DVE_STEPS_FIRST + DVE_STEPS * (t - 1))
                mixer_block(t, True, steps)
                assert steps.count == DVE_STEPS, steps.count
            steps = Steps(dve, dve_step, DVE_STEPS_FIRST + DVE_STEPS * (NBLK - 1))
            for i in range(4):
                split(NBLK, 4 + i)
            for half in range(2):
                for c in range(4):
                    output_tile(NBLK, 4 * half, half, c)
            for c in range(4):
                statistics(NBLK, 4, c, steps)

    feed_forward(nc, normed, ln1_g, ln1_b, w1_v, w2_rows, ln2_g, ln2_b, out_rows, KT, HALF, NT, NFB)


def feed_forward(nc, normed, ln1_g, ln1_b, w1_v, w2_rows, ln2_g, ln2_b, out_rows, KT, HALF, NT, NFB):
    D = KT * P
    with ExitStack() as ctx:
        def sb(name, shape, dt=F32):
            return ctx.enter_context(nc.sbuf_tensor(name, shape, dt))

        def sem(name):
            return ctx.enter_context(nc.semaphore(name))

        raw = sb("f_raw", [P, 2, 1024])
        w_hi = sb("f_w_hi", [P, 4, 1024], F32R)
        w_lo = sb("f_w_lo", [P, 4, 1024], F32R)
        xT_hi = sb("f_xT_hi", [P, KT, HALF], F32R)
        xT_lo = sb("f_xT_lo", [P, KT, HALF], F32R)
        h_hi = sb("h_hi", [P, 2, HALF], F32R)
        h_lo = sb("h_lo", [P, 2, HALF], F32R)
        acc = sb("acc", [P, 2, NT, D])
        relu = sb("relu", [P, 2, 512])
        h_raw = sb("h_raw", [P, 2, 512])
        g1_row = sb("g1_row", [P, D])
        b1_row = sb("b1_row", [P, D])
        g2_row = sb("g2_row", [P, D])
        b2_row = sb("b2_row", [P, D])
        g1_col = sb("g1_col", [P, KT])
        b1_col = sb("b1_col", [P, KT])
        ident = sb("f_ident", [P, P])
        eps_ln = sb("f_eps_ln", [P, 1])
        stats = sb("f_stats", [P, NT, 2, 6])
        mvar = sb("f_mvar", [P, NT, 2])
        rstd = sb("f_rstd", [P, NT])
        nmean = sb("f_nmean", [P, NT])
        fm = [ctx.enter_context(nc.psum_tensor(f"fm{i}", [P, 512], F32)) for i in range(4)]
        fo = [ctx.enter_context(nc.psum_tensor(f"fo{i}", [P, 512], F32)) for i in range(4)]

        raw_landed = [sem(f"f_raw_landed{i}") for i in range(2)]
        hi_done, lo_done = sem("f_hi_done"), sem("f_lo_done")
        fm_done, fo_done = sem("fm_done"), sem("fo_done")
        fm_free = [sem(f"fm_free{i}") for i in range(4)]
        fo_free = [sem(f"fo_free{i}") for i in range(4)]
        n_landed = [[sem(f"n_landed{hf}_{c}") for c in range(NT)] for hf in range(2)]
        out_stored = [sem(f"out_stored{c}") for c in range(NT)]
        col_landed, row_landed = sem("col_landed"), sem("row_landed")
        const_step, const_done = sem("f_const_step"), sem("f_const_done")
        x_hi_ready, x_lo_ready = sem("x_hi_ready"), sem("x_lo_ready")
        init_step, init_done = sem("init_step"), sem("init_done")
        relu_ready, hraw_ready, h_hi_ready, h_lo_ready = (
            sem("relu_ready"), sem("hraw_ready"), sem("h_hi_ready"), sem("h_lo_ready"))
        stats_step, ln_stats, ln_step, ln_rstd, ln_out = (
            sem("f_stats_step"), sem("f_ln_stats"), sem("f_ln_step"), sem("f_ln_rstd"), sem("f_ln_out"))
        scale_step, out_ready = sem("scale_step"), sem("out_ready")
        tail_step, tail_ready, tail_stored = sem("tail_step"), sem("tail_ready"), sem("tail_stored")
        block = ctx.enter_context(nc.Block())

        def slot_n(hf, fb, s):
            return 4 * NFB * hf + 4 * fb + s

        def fm_turn(hf, fb):
            return (4 + NFB) * hf + 4 + fb

        def fm_n(hf, fb, i):
            return 4 * fm_turn(hf, fb) + i

        def fo_n(hf, fb, i):
            return 16 * NFB * hf + 16 * fb + i

        def h_n(hf, fb, i):
            return 4 * NFB * hf + 4 * fb + i

        POOL_TAIL = 5

        @block.sync
        def _(sp):
            def load(hf, fb, first=False):
                for s in range(4):
                    if not (first and s < 2):
                        sp.wait_ge(lo_done, slot_n(hf, fb, s) - 1)
                    if s < 2:
                        src = w1_v[:, :, bass.ds(2 * P * fb + P * s, P)]
                        dst = raw[:, s, :].rearrange("p (k n) -> p k n", k=KT)
                    else:
                        src = w2_rows[bass.ds(2 * P * fb + P * (s - 2), P), :]
                        dst = raw[:, s - 2, :]
                    sp.dma_start(dst, src).then_inc(raw_landed[s % 2], 16)

            load(0, 0, True)
            with sp.Fori(1, NFB) as fb:
                load(0, fb)
            with sp.Fori(0, NFB) as fb:
                load(1, fb)
            for i, c in enumerate(range(POOL_TAIL, NT)):
                sp.wait_ge(tail_ready, i + 1)
                sp.dma_start(out_rows[HALF + P * c:HALF + P * c + P, :], acc[:, 1, c, :]).then_inc(tail_stored, 16)
            sp.wait_ge(tail_stored, 16 * (NT - POOL_TAIL))

        @block.gpsimd
        def _(pool):
            for c in range(NT):
                pool.dma_start(acc[:, 0, c, :], normed[P * c:P * c + P, :]).then_inc(n_landed[0][c], 16)
            for dst, src in ((g1_col, ln1_g), (b1_col, ln1_b)):
                with nc.allow_non_contiguous_dma(reason="one value a partition, once"):
                    pool.dma_start(dst[:, :], src[0].rearrange("(k p) -> p k", p=P)).then_inc(col_landed, 16)
            pool.memset(ident[:, :], 0.0).then_inc(const_step, 1)
            pool.wait_ge(const_step, 1)
            pool.affine_select(out=ident[:, :], in_=ident[:, :], compare_op=ALU.not_equal, fill=1.0, base=0,
                               pattern=[[-1, P]], channel_multiplier=1).then_inc(const_done, 1)
            pool.memset(eps_ln[:, :], LN_EPS).then_inc(const_done, 1)
            for dst, src in ((g1_row, ln1_g), (b1_row, ln1_b), (g2_row, ln2_g), (b2_row, ln2_b)):
                pool.dma_start(dst[:, :], src.to_broadcast([P, D])).then_inc(row_landed, 16)
            for c in range(NT):
                pool.dma_start(acc[:, 1, c, :], normed[HALF + P * c:HALF + P * c + P, :]).then_inc(n_landed[1][c], 16)
            pool.wait_ge(row_landed, 16 * 4)
            pool.tensor_scalar(g1_row[:, :], g1_row[:, :], ALPHA, None, ALU.mult).then_inc(init_step, 1)
            pool.tensor_scalar(b1_row[:, :], b1_row[:, :], ALPHA, None, ALU.mult).then_inc(init_step, 1)
            for hf in range(2):
                for c in range(NT):
                    pool.wait_ge(fm_done, fm_n(hf, -4, 8 * (c // 4) + 8))
                    pool.wait_ge(init_step, 2 + NT * hf + c)
                    pool.tensor_tensor(acc[:, hf, c, :], acc[:, hf, c, :], g1_row[:, :], ALU.mult
                                       ).then_inc(init_step, 1)
                    pool.wait_ge(init_step, 2 + NT * hf + c + 1)
                    pool.tensor_tensor(acc[:, hf, c, :], acc[:, hf, c, :], b1_row[:, :], ALU.add
                                       ).then_inc(init_done, 1)
            for hf in range(2):
                for c in range(NT if hf == 0 else POOL_TAIL):
                    pool.wait_ge(ln_out, NT * hf + c + 1)
                    pool.tensor_tensor(acc[:, hf, c, :], acc[:, hf, c, :], g2_row[:, :], ALU.mult
                                       ).then_inc(scale_step, 1)
                    pool.wait_ge(scale_step, NT * hf + c + 1)
                    pool.tensor_tensor(acc[:, hf, c, :], acc[:, hf, c, :], b2_row[:, :], ALU.add
                                       ).then_inc(out_ready, 1)
                    pool.wait_ge(out_ready, NT * hf + c + 1)
                    pool.dma_start(out_rows[HALF * hf + P * c:HALF * hf + P * c + P, :], acc[:, hf, c, :]
                                   ).then_inc(out_stored[c], 16)
            for c in range(NT):
                pool.wait_ge(out_stored[c], 32 if c < POOL_TAIL else 16)

        @block.tensor
        def _(pe):
            three = three_products(pe)

            def hidden(hf, fb):
                for i in range(4):
                    f, sb_ = i % 2, i // 2
                    if i < 2:
                        pe.wait_ge(lo_done, slot_n(hf, fb, f) + 1)
                    pe.wait_ge(hraw_ready, h_n(hf, fb, 0))
                    tok = slice(512 * sb_, 512 * sb_ + 512)
                    for k in range(KT):
                        col = slice(P * k, P * k + P)
                        ins = three(fm[i][:, :], w_hi[:, f, col], w_lo[:, f, col], xT_hi[:, k, tok], xT_lo[:, k, tok],
                                    k == 0, k == KT - 1)
                    ins.then_inc(fm_done, 1)

            def project(hf, fb, i):
                c, d = i // 2, i % 2
                if i == 0:
                    pe.wait_ge(lo_done, slot_n(hf, fb, 3) + 1)
                if i % 8 == 0:
                    pe.wait_ge(h_lo_ready, h_n(hf, fb, 2 + i // 4))
                pe.wait_ge(fo_free[i % 4], 4 * NFB * hf + 4 * fb + i // 4)
                tok = slice(P * c, P * c + P)
                for f in range(2):
                    ins = three(fo[i % 4][:, :], h_hi[:, f, tok], h_lo[:, f, tok],
                                w_hi[:, 2 + f, 512 * d:512 * d + 512], w_lo[:, 2 + f, 512 * d:512 * d + 512],
                                f == 0, f == 1)
                ins.then_inc(fo_done, 1)

            def transposes(hf, i):
                sb_, k = i // 8, i % 8
                pe.wait_ge(fm_free[i % 4], 4 * hf + i // 4)
                if hf == 1 and i == 0:
                    pe.wait_ge(hraw_ready, h_n(1, 0, 0))
                for c in range(4):
                    if k == 0:
                        pe.wait_ge(n_landed[hf][4 * sb_ + c], 16)
                    ins = pe.transpose(fm[i % 4][:, P * c:P * c + P], acc[:, hf, 4 * sb_ + c, P * k:P * k + P],
                                       ident[:, :])
                ins.then_inc(fm_done, 1)

            def both(hf, fb):
                hidden(hf, fb)
                for i in range(16):
                    project(hf, fb, i)

            pe.wait_ge(const_done, 1)
            for i in range(16):
                transposes(0, i)
            pe.wait_ge(x_lo_ready, 16)
            both(0, 0)
            with pe.Fori(1, NFB - 1) as fb:
                both(0, fb)
            hidden(0, NFB - 1)
            for i in range(16):
                project(0, NFB - 1, i)
                transposes(1, i)
            pe.wait_ge(x_lo_ready, 32)
            both(1, 0)
            with pe.Fori(1, NFB) as fb:
                both(1, fb)

        @block.scalar
        def _(act):
            def split(hf, fb, s):
                act.wait_ge(raw_landed[s % 2], 16 * (2 * NFB * hf + 2 * fb + s // 2 + 1))
                first = isinstance(fb, int) and hf == 0 and fb == 0
                if s < 2 and isinstance(fb, int) and fb == 0:
                    if hf == 1:
                        act.wait_ge(fm_done, fm_n(0, NFB - 1, s + 3))
                elif s < 2:
                    act.wait_ge(fm_done, fm_n(hf, fb - 1, s + 3))
                elif not first:
                    act.wait_ge(fo_done, fo_n(hf, fb, 0))
                act.activation(w_hi[:, s, :], raw[:, s % 2, :], ACT.Copy).then_inc(hi_done, 1)

            def hidden(hf, fb):
                for i in range(4):
                    f, sb_ = i % 2, i // 2
                    act.wait_ge(fm_done, fm_n(hf, fb, i) + 1)
                    act.activation(relu[:, i % 2, :], fm[i][:, :], ACT.Relu).then_inc(relu_ready, 1)
                    act.wait_ge(hraw_ready, h_n(hf, fb, i) + 1)
                    act.activation(h_hi[:, f, 512 * sb_:512 * sb_ + 512], h_raw[:, i % 2, :], ACT.Copy
                                   ).then_inc(h_hi_ready, 1)

            def x_part(hf, i):
                sb_, k = i // 8, i % 8
                act.wait_ge(fm_done, fm_n(hf, -4, i) + 1)
                if i >= 2:
                    act.wait_ge(x_lo_ready, 16 * hf + i - 1)
                elif hf == 1:
                    act.wait_ge(hraw_ready, h_n(1, 0, 0))
                act.activation(relu[:, i % 2, :], fm[i % 4][:, :], ACT.Identity, scale=g1_col[:, k:k + 1],
                               bias=b1_col[:, k:k + 1]).then_inc(fm_free[i % 4], 1)
                act.wait_ge(fm_free[i % 4], 4 * hf + i // 4 + 1)
                act.activation(xT_hi[:, k, 512 * sb_:512 * sb_ + 512], relu[:, i % 2, :], ACT.Copy
                               ).then_inc(x_hi_ready, 1)

            def normalise(hf, c):
                act.wait_ge(ln_stats, NT * hf + c + 1)
                act.activation(rstd[:, c:c + 1], mvar[:, c, 1:2], ACT.Ln, bias=eps_ln[:, :]).then_inc(ln_step, 1)
                act.wait_ge(ln_step, 3 * (NT * hf + c) + 1)
                act.activation(rstd[:, c:c + 1], rstd[:, c:c + 1], ACT.Exp, scale=-0.5).then_inc(ln_step, 1)
                act.wait_ge(ln_step, 3 * (NT * hf + c) + 2)
                act.activation(nmean[:, c:c + 1], nmean[:, c:c + 1], ACT.Copy, scale=rstd[:, c:c + 1]
                               ).then_inc(ln_step, 1)
                act.wait_ge(ln_step, 3 * (NT * hf + c) + 3)
                act.activation(acc[:, hf, c, :], acc[:, hf, c, :], ACT.Identity, scale=rstd[:, c:c + 1],
                               bias=nmean[:, c:c + 1]).then_inc(ln_out, 1)

            def block_but_last(hf, fb):
                split(hf, fb, 2)
                split(hf, fb, 3)
                hidden(hf, fb)
                split(hf, fb + 1, 0)
                split(hf, fb + 1, 1)

            act.wait_ge(col_landed, 32)
            act.wait_ge(const_done, 2)
            split(0, 0, 0)
            split(0, 0, 1)
            for i in range(16):
                x_part(0, i)
            for hf in range(2):
                block_but_last(hf, 0)
                if hf == 1:
                    for c in range(NT):
                        normalise(0, c)
                with act.Fori(1, NFB - 1) as fb:
                    block_but_last(hf, fb)
                split(hf, NFB - 1, 2)
                split(hf, NFB - 1, 3)
                hidden(hf, NFB - 1)
                if hf == 0:
                    split(1, 0, 0)
                    split(1, 0, 1)
                    for i in range(16):
                        x_part(1, i)
            for c in range(NT):
                normalise(1, c)

        @block.vector
        def _(dve):
            def split(hf, fb, s):
                dve.wait_ge(hi_done, slot_n(hf, fb, s) + 1)
                dve.tensor_tensor(w_lo[:, s, :], raw[:, s % 2, :], w_hi[:, s, :].bitcast(F32), ALU.subtract
                                  ).then_inc(lo_done, 1)

            def hidden_tile(hf, fb, i):
                f, sb_ = i % 2, i // 2
                tok = slice(512 * sb_, 512 * sb_ + 512)
                dve.wait_ge(relu_ready, h_n(hf, fb, i) + 1)
                if not (isinstance(fb, int) and hf == 0 and fb == 0 and i < 2):
                    dve.wait_ge(h_lo_ready, h_n(hf, fb, i) - 1)
                dve.scalar_tensor_tensor(out=h_raw[:, i % 2, :], in0=fm[i][:, :], scalar=0.0,
                                         in1=relu[:, i % 2, :], op0=ALU.max, op1=ALU.mult
                                         ).then_inc(hraw_ready, 1)
                dve.wait_ge(h_hi_ready, h_n(hf, fb, i) + 1)
                dve.tensor_tensor(h_lo[:, f, tok], h_raw[:, i % 2, :], h_hi[:, f, tok].bitcast(F32),
                                  ALU.subtract).then_inc(h_lo_ready, 1)

            def add(hf, fb, i):
                c, d = i // 2, i % 2
                dve.wait_ge(fo_done, fo_n(hf, fb, i) + 1)
                if isinstance(fb, int) and fb == 0 and d == 0:
                    dve.wait_ge(init_done, NT * hf + c + 1)
                dst = acc[:, hf, c, 512 * d:512 * d + 512]
                dve.tensor_tensor(dst, dst, fo[i % 4][:, :], ALU.add).then_inc(fo_free[i % 4], 1)

            def x_part(hf, i):
                sb_, k = i // 8, i % 8
                tok = slice(512 * sb_, 512 * sb_ + 512)
                dve.wait_ge(x_hi_ready, 16 * hf + i + 1)
                dve.tensor_tensor(xT_lo[:, k, tok], relu[:, i % 2, :], xT_hi[:, k, tok].bitcast(F32), ALU.subtract
                                  ).then_inc(x_lo_ready, 1)

            def statistics(hf, c):
                for d in range(2):
                    i = 2 * c + d
                    dve.wait_ge(fo_free[i % 4], 4 * NFB * (hf + 1) - 4 + i // 4 + 1)
                    dve.bn_stats(stats[:, c, d, :], acc[:, hf, c, 512 * d:512 * d + 512]).then_inc(stats_step, 1)
                dve.wait_ge(stats_step, 3 * (NT * hf + c) + 2)
                dve.bn_aggr(mvar[:, c, :], stats[:, c, :, :]).then_inc(stats_step, 1)
                dve.wait_ge(stats_step, 3 * (NT * hf + c) + 3)
                dve.tensor_scalar(nmean[:, c:c + 1], mvar[:, c, 0:1], -1.0, None, ALU.mult).then_inc(ln_stats, 1)

            def block_but_last(hf, fb):
                split(hf, fb, 2)
                split(hf, fb, 3)
                for i in range(4):
                    hidden_tile(hf, fb, i)
                    if hf == 1 and isinstance(fb, int):
                        statistics(0, 2 * i)
                        statistics(0, 2 * i + 1)
                for i in range(16):
                    add(hf, fb, i)
                    if i == 3:
                        split(hf, fb + 1, 0)
                    if i == 5:
                        split(hf, fb + 1, 1)

            split(0, 0, 0)
            split(0, 0, 1)
            for i in range(16):
                x_part(0, i)
            for hf in range(2):
                block_but_last(hf, 0)
                with dve.Fori(1, NFB - 1) as fb:
                    block_but_last(hf, fb)
                split(hf, NFB - 1, 2)
                split(hf, NFB - 1, 3)
                for i in range(4):
                    hidden_tile(hf, NFB - 1, i)
                if hf == 0:
                    split(1, 0, 0)
                    split(1, 0, 1)
                    for i in range(16):
                        add(0, NFB - 1, i)
                        x_part(1, i)
            for c in range(NT):
                add(1, NFB - 1, 2 * c)
                add(1, NFB - 1, 2 * c + 1)
                statistics(1, c)
            dve.wait_ge(row_landed, 16 * 4)
            for i, c in enumerate(range(POOL_TAIL, NT)):
                dve.wait_ge(ln_out, NT + c + 1)
                dve.tensor_tensor(acc[:, 1, c, :], acc[:, 1, c, :], g2_row[:, :], ALU.mult).then_inc(tail_step, 1)
                dve.wait_ge(tail_step, i + 1)
                dve.tensor_tensor(acc[:, 1, c, :], acc[:, 1, c, :], b2_row[:, :], ALU.add).then_inc(tail_ready, 1)


_INS = ["x", "mem", "w_in", "w_gate_up", "b_gate", "conv_w", "gla_norm_g", "w_mem_kv", "w_out",
        "ln1_g", "ln1_b", "w_ff1", "w_ff2", "ln2_g", "ln2_b"]


def kernel(**inputs):
    import numpy as _np
    import concourse.bacc as _bacc
    from concourse import mybir as _mybir
    from concourse.bass_utils import run_bass_kernel_spmd as _run

    nc = _bacc.Bacc("TRN2", target_bir_lowering=False, num_devices=1,
                    dynamic_dma_scratch_size=8192)
    arrays, args = {}, []
    for name in _INS:
        a = _np.ascontiguousarray(inputs[name])
        arrays[f"in_{name}_dram"] = a
        args.append(nc.dram_tensor(f"in_{name}_dram", a.shape, _mybir.dt.from_np(a.dtype), kind="ExternalInput").ap())
    B, S, D = inputs["x"].shape
    args.append(nc.dram_tensor("normed_dram", (S, D), _mybir.dt.float32, kind="Internal").ap())
    args.append(nc.dram_tensor("out_0_dram", (B, S, D), _mybir.dt.float32, kind="ExternalOutput").ap())
    hybrid_layer(nc, *args)
    r = _run(nc, [arrays], core_ids=[0])
    return r.results[0]["out_0_dram"]
```

```python
from contextlib import ExitStack

import concourse.bass as bass
from concourse import mybir

F32 = mybir.dt.float32
F32R = mybir.dt.float32r
U8 = mybir.dt.uint8
ALU = mybir.AluOpType
ACT = mybir.ActivationFunctionType
AX_X = mybir.AxisListType.X

P = 128
BLK = 512
CH = 128
NCH = BLK // CH
LEVELS = [1, 2, 4, 8, 16, 32, 64]
DK, DV, HEADS = 64, 128, 4
RANK = 16
LN_EPS, RMS_EPS = 1e-5, 1e-6
ALPHA = 2.0 ** 0.25
TAU = 16.0
RAW = 2
RING = 4

J_OUT_A, J_XQ, J_Q, J_OUT_B, J_K, J_C0, J_H0, J_V = 0, 4, 6, 8, 12, 14, 15, 16
J_B0, J_G0, J_G1, J_C1, J_H1, J_B1, J_G2, J_G3 = range(20, 28)
GATE_TILE = [J_G0, J_G1, J_G2, J_G3]
SC_XT, SC_XA, SC_GLA, SC_USES = 0, 4, 12, 20
OB_XA, OB_GLA, OB_USES = 0, 4, 12
AUX_LOW, AUX_GATE, AUX_GLA, AUX_PAIR, AUX_USES = 0, 1, 3, 7, 17
ACT_STEPS_FIRST, ACT_STEPS = 12, 24
DVE_STEPS_FIRST, DVE_STEPS = 88, 100
K_ORDER = [3, 0, 2, 1]
K_READY = [2, 5, 6, 8]
Y_TILE = [6, 7, 4, 0, 1, 5, 2, 3]


class Shared:
    pass


def three_products(pe):
    def three(dst, a_hi, a_lo, b_hi, b_lo, first, last):
        pe.matmul(dst, a_hi, b_lo, start=first, stop=False)
        pe.matmul(dst, a_lo, b_hi, start=False, stop=False)
        return pe.matmul(dst, a_hi, b_hi, start=False, stop=last)
    return three


def hybrid_layer(nc, x, mem, w_in, w_gate_up, b_gate, conv_w, gla_norm_g, w_mem_kv, w_out,
                 ln1_g, ln1_b, w_ff1, w_ff2, ln2_g, ln2_b, normed, out):
    S, D = x.shape[1], x.shape[2]
    KT = D // P
    NBLK = S // BLK
    DFF = w_ff1.shape[2]
    M = mem.shape[1]
    HALF = S // 2
    NT = HALF // P
    NFB = DFF // (2 * P)
    assert (KT, NBLK, M) == (8, 4, 256)

    x_rows = x[0]
    out_rows = out[0]
    win_v = w_in[0].rearrange("(k p) n -> p k n", p=P)
    wout_v = w_out[0].rearrange("(k p) n -> p k n", p=P)
    wkv_v = w_mem_kv[0].rearrange("(k p) n -> p k n", p=P)
    w1_v = w_ff1[0].rearrange("(k p) n -> p k n", p=P)
    w2_rows = w_ff2[0]
    COL_Q, COL_V, COL_G = 0, 512, 1024
    COL_LOW = 1536
    COL_B, COL_C, COL_H, COL_XQ = 1552, 1808, 2064, 2320
    SLOT_COL = {J_Q: 0, J_Q + 1: 128, J_K: 256, J_K + 1: 384, J_XQ: COL_XQ, J_XQ + 1: COL_XQ + 128,
                J_C0: COL_C, J_H0: COL_H, J_B0: COL_B, J_C1: COL_C + 128, J_H1: COL_H + 128, J_B1: COL_B + 128,
                J_G0: COL_G, J_G1: COL_G + 128, J_G2: COL_G + 256, J_G3: COL_G + 384}

    def slot_source(j):
        for half, j0 in ((0, J_OUT_A), (1, J_OUT_B)):
            if j0 <= j < j0 + 4:
                k = 2 * K_ORDER[j - j0]
                return wout_v[:, k:k + 2, 512 * half:512 * half + 512]
        if J_V <= j < J_V + 4:
            return win_v[:, 2 * (j - J_V):2 * (j - J_V) + 2, COL_V:COL_V + 512]
        return win_v[:, :, SLOT_COL[j]:SLOT_COL[j] + P]

    with ExitStack() as ctx:
        def sb(name, shape, dt=F32):
            return ctx.enter_context(nc.sbuf_tensor(name, shape, dt))

        def sem(name):
            return ctx.enter_context(nc.semaphore(name))

        raw = sb("raw", [P, RAW, 1024])
        w_hi = sb("w_hi", [P, RING, 1024], F32R)
        w_lo = sb("w_lo", [P, RING, 1024], F32R)
        ident = sb("ident", [P, P])
        eps_ln = sb("eps_ln", [P, 1])
        stats = sb("stats", [P, 4, 2, 6])
        mvar = sb("mvar", [P, 4, 2])
        rstd = sb("rstd", [P, 4])
        nmean = sb("nmean", [P, 4])
        ff = Shared()
        ff.g1_col = sb("g1_col", [P, KT])
        ff.b1_col = sb("b1_col", [P, KT])
        ff.stats = sb("f_stats", [P, NT, 2, 6])
        ff.mvar = sb("f_mvar", [P, NT, 2])
        ff.rstd = sb("f_rstd", [P, NT])
        ff.nmean = sb("f_nmean", [P, NT])

        with ExitStack() as shared:
            def shared_sb(name, shape, dt=F32):
                return shared.enter_context(nc.sbuf_tensor(name, shape, dt))

            acc1 = shared_sb("acc1", [P, NT, D])
            ff.h_hi = shared_sb("h_hi", [P, 2, HALF], F32R)
            ff.h_lo = shared_sb("h_lo", [P, 2, HALF], F32R)
            ff.acc = [shared_sb("acc0", [P, NT, D]), acc1]
            ff.xT_hi = shared_sb("f_xT_hi", [P, KT, HALF], F32R)
            ff.xT_lo = shared_sb("f_xT_lo", [P, KT, HALF], F32R)
            ff.relu = shared_sb("relu", [P, 2, 512])
            ff.h_raw = shared_sb("h_raw", [P, 2, 512])
            ff.g1_row = shared_sb("g1_row", [P, D])
            ff.b1_row = shared_sb("b1_row", [P, D])
            ff.g2_row = shared_sb("g2_row", [P, D])
            ff.b2_row = shared_sb("b2_row", [P, D])

        rows = sb("rows", [P, 4, D])
        y_hi = sb("y_hi", [P, KT, BLK], F32R)
        y_lo = sb("y_lo", [P, KT, BLK], F32R)
        xT_hi = sb("xT_hi", [P, KT, BLK], F32R)
        xT_lo = sb("xT_lo", [P, KT, BLK], F32R)
        qT = sb("qT", [P, 2, BLK])
        kT = sb("kT", [P, 2, BLK])
        v_rows = sb("v_rows", [P, NCH, HEADS * DV])
        xqT = sb("xqT", [P, 2, BLK])
        u = sb("u", [P, 2, BLK + 2])
        gate = sb("gate", [P, 2, BLK])
        k_dec = sb("k_dec", [P, BLK])
        b_last = sb("b_last", [P, 2, NCH])
        decay_last = sb("decay_last", [P, NCH])
        k_lev = sb("k_lev", [P, 5, BLK])
        k_top = sb("k_top", [P, NCH, 64])
        q_lev = sb("q_lev", [P, 7, 2, BLK // 2])
        q_dec = sb("q_dec", [P, BLK])
        state = sb("state", [P, 2, 2, DV])
        oT = sb("oT", [P, 2, BLK])
        rr = sb("rr", [P, 2, BLK])
        gin = sb("gin", [P, 2, BLK])
        y_raw = sb("y_raw", [P, 2, BLK])
        xy_raw = sb("xy_raw", [P, 2, BLK])
        xp = sb("xp", [P, 4, M])
        xpT = sb("xpT", [P, 2, 4 * P])
        k_dec_rows = xp[:, 0:2, :].rearrange("p a (b n) -> p (a b) n", n=P)
        probs = xpT[:, 0, 0:2 * CH]
        mkT = sb("mkT", [P, 2, M])
        mv = sb("mv", [P, 2, 256])
        masks = sb("masks", [P, 6, 2 * 64], U8)
        ones = sb("ones", [P, P])
        low = sb("low", [P, KT, 2 * RANK], F32R)
        w_gate = sb("w_gate", [2 * RANK, 256])
        few = sb("few", [P, 28])
        xmax, xnmax, xsum, xrec = (few[:, 4 * i:4 * i + 4] for i in range(4))
        taps = few[:, 16:22].rearrange("p (c w) -> p c w", c=2)
        gate_bias = few[:, 22:24]
        head_sum = few[:, 24:26]
        rms_g = few[:, 26:27]
        eps_rms = few[:, 27:28]
        lowT = y_raw[0:2 * RANK, 1, :]
        low_raw = gin[:, 0, 0:KT * RANK].rearrange("p (k n) -> p k n", k=KT)
        mask_f = gin[:, 1, 0:384].rearrange("p (l n) -> p l n", l=6)

        main = [ctx.enter_context(nc.psum_tensor(f"main{i}", [P, 512], F32)) for i in range(RING)]
        sc = [ctx.enter_context(nc.psum_tensor(f"sc{i}", [P, 512], F32)) for i in range(2)]
        ob = ctx.enter_context(nc.psum_tensor("ob", [P, 512], F32))
        aux = ctx.enter_context(nc.psum_tensor("aux", [P, 512], F32))

        raw_landed = [sem(f"raw_landed{i}") for i in range(RAW)]
        hi_done, lo_done, row_used = sem("hi_done"), sem("lo_done"), sem("row_used")
        main_done = sem("main_done")
        main_free = [sem(f"main_free{i}") for i in range(RING)]
        sc_done = [sem(f"sc_done{i}") for i in range(2)]
        sc_free = [sem(f"sc_free{i}") for i in range(2)]
        ob_done, ob_free = sem("ob_done"), sem("ob_free")
        aux_done, aux_free = sem("aux_done"), sem("aux_free")
        x_landed = [sem(f"x_landed{i}") for i in range(4)]
        res_landed = [sem(f"res_landed{i}") for i in range(4)]
        stored = [sem(f"stored{i}") for i in range(4)]
        mem_landed = [sem(f"mem_landed{i}") for i in range(2)]
        small_landed, const_done, const_step = sem("small_landed"), sem("const_done"), sem("const_step")
        xt_hi_done = sem("xt_hi_done")
        low_hi_done, low_split = sem("low_hi_done"), sem("low_split")
        ln_stats, ln_rstd, ln_out = sem("ln_stats"), sem("ln_rstd"), sem("ln_out")
        soft_ready = sem("soft_ready")
        expo_ready, exp_ready, prep_ready = sem("expo_ready"), sem("exp_ready"), sem("prep_ready")
        high_step, high_ready = sem("high_step"), sem("high_ready")
        sq_ready, rms_ready, on_ready = sem("sq_ready"), sem("rms_ready"), sem("on_ready")
        gin_ready, yraw_ready, yhi_ready, y_ready = sem("gin_ready"), sem("yraw_ready"), sem("yhi_ready"), sem("y_ready")
        xmax_ready, xp_ready = sem("xmax_ready"), sem("xp_ready")
        act_step, dve_step, xy_copied = sem("act_step"), sem("dve_step"), sem("xy_copied")
        ff.fm = [sc[0], sc[1], ob, aux]
        ff.fo = main
        ff.n_landed = [[sem(f"n_landed{hf}_{c}") for c in range(NT)] for hf in range(2)]
        ff.fm_done, ff.col_landed = sem("fm_done"), sem("col_landed")
        ff.fm_free = [sem(f"fm_free{i}") for i in range(4)]
        ff.row_landed, ff.init_step, ff.init_done = sem("row_landed"), sem("init_step"), sem("init_done")
        ff.x_hi_ready, ff.x_lo_ready = sem("x_hi_ready"), sem("x_lo_ready")
        ff.sem, ff.raw, ff.w_hi, ff.w_lo, ff.ident, ff.eps_ln = sem, raw, w_hi, w_lo, ident, eps_ln
        ff.raw_landed, ff.hi_done, ff.lo_done = raw_landed, hi_done, lo_done
        ff.main_free, ff.main_done, ff.stored = main_free, main_done, stored
        ff.first_slot = 28 * NBLK + 4
        block = ctx.enter_context(nc.Block())

        def mixer_blocks_over(eng):
            eng.wait_ge(lo_done, 28 * NBLK)
            eng.wait_ge(yhi_ready, 8 * NBLK)
            eng.wait_ge(y_ready, 8 * NBLK)
            eng.wait_ge(main_done, 28 * NBLK - 4)
            eng.wait_ge(aux_done, AUX_USES * NBLK)

        def slot_n(t, j):
            if isinstance(t, int) and t == 0 and j < 8:
                return j
            return 28 * t - 4 + j

        def turn(t, j):
            if isinstance(t, int) and t == 0 and j < 8:
                return j // 4
            return 7 * t - 1 + j // 4

        def raw_turn(t, j):
            if isinstance(t, int) and t == 0 and j < 8:
                return j // RAW
            return (4 // RAW) * (7 * t - 1) + j // RAW

        def following(t, j):
            if isinstance(t, int) and t == 0 and j < 8:
                return 0, j + 8
            return (t, j + 4) if j + 4 < 28 else (t + 1, j + 4 - 28)

        def level_view(tile, s):
            return tile.rearrange("p (n w) -> p n w", w=2 * s)

        class Steps:

            def __init__(self, eng, semaphore, base):
                self.eng, self.semaphore, self.base, self.count = eng, semaphore, base, 0

            def mark(self, ins):
                ins.then_inc(self.semaphore, 1)
                self.count += 1

            def settle(self):
                self.eng.wait_ge(self.semaphore, self.base + self.count)

        @block.sync
        def _(sp):
            def load(t, j, source):
                if not (isinstance(t, int) and slot_n(t, j) < RAW):
                    sp.wait_ge(lo_done, slot_n(t, j) - RAW + 1)
                shape = source.shape
                dst = raw[:, j % RAW, :].rearrange("p (k n) -> p k n", k=shape[1])
                sp.dma_start(dst, source).then_inc(raw_landed[j % RAW], 16)

            for i in range(4):
                src = wkv_v[:, :, P * i:P * i + P] if i < 2 else wkv_v[:, 4 * (i - 2):4 * (i - 2) + 4, 256:512]
                load(0, i, src)
            for j in range(J_XQ, 28):
                if not J_OUT_B <= j < J_OUT_B + 4:
                    load(0, j, slot_source(j))
            with sp.Fori(1, NBLK) as t:
                for j in range(28):
                    load(t, j, slot_source(j))
            for i in range(4):
                load(NBLK, i, slot_source(J_OUT_A + i))
            load(NBLK, 4, slot_source(J_OUT_B))
            load(NBLK, 5, slot_source(J_OUT_B + 1))
            mixer_blocks_over(sp)
            for j in range(4):
                sp.wait_ge(stored[j], 32)
            for i in range(2):
                for c in range(4 * i, 4 * i + 4):
                    sp.dma_start(ff.acc[0][:, c, :], normed[P * c:P * c + P, :]).then_inc(ff.n_landed[0][c], 16)
                load(NBLK, 6 + i, slot_source(J_OUT_B + 2 + i))

        @block.gpsimd
        def _(pool):
            pool.memset(ident[:, :], 0.0).then_inc(const_step, 1)
            pool.dma_start(rows[:, 2, :], mem[0, 0:P, :]).then_inc(mem_landed[0], 16)
            pool.wait_ge(const_step, 1)
            pool.affine_select(out=ident[:, :], in_=ident[:, :], compare_op=ALU.not_equal, fill=1.0, base=0,
                               pattern=[[-1, P]], channel_multiplier=1).then_inc(const_done, 1)
            pool.dma_start(rows[:, 3, :], mem[0, P:2 * P, :]).then_inc(mem_landed[1], 16)
            for j in range(2):
                pool.dma_start(rows[:, j, :], x_rows[P * j:P * j + P, :]).then_inc(x_landed[j], 16)
            pool.memset(ones[:, :], 1.0)
            pool.memset(eps_rms[:, :], RMS_EPS)
            pool.memset(eps_ln[:, :], LN_EPS).then_inc(const_done, 1)
            for dst, src in ((low_raw, win_v[:, :, COL_LOW:COL_LOW + RANK]),
                             (w_gate[0:RANK, :], w_gate_up[0]),
                             (w_gate[RANK:2 * RANK, :], w_gate_up[0]),
                             (gate_bias[:, :], b_gate[0].rearrange("(c p) -> p c", p=P)),
                             (rms_g[:, :], gla_norm_g[0].rearrange("(c p) -> p c", p=P))):
                with nc.allow_non_contiguous_dma(reason="a few short rows, once"):
                    pool.dma_start(dst, src).then_inc(small_landed, 16)
            for c in range(2):
                with nc.allow_non_contiguous_dma(reason="a few short rows, once"):
                    pool.dma_start(taps[:, c, :], conv_w[0, :, P * c:P * c + P].rearrange("w p -> p w")).then_inc(
                        small_landed, 16)
            for dst, src in ((ff.g1_col, ln1_g), (ff.b1_col, ln1_b)):
                with nc.allow_non_contiguous_dma(reason="one value a partition, once"):
                    pool.dma_start(dst[:, :], src[0].rearrange("(k p) -> p k", p=P)).then_inc(ff.col_landed, 16)
            pool.memset(mask_f, 1.0).then_inc(const_step, 1)
            for m in range(2):
                pool.wait_ge(sc_done[0], m + 1)
                pool.wait_ge(sc_done[1], m + 1)
                pool.dma_start(rows[:, 2 + m, :], x_rows[P * (2 + m):P * (3 + m), :]).then_inc(x_landed[2 + m], 16)
            pool.wait_ge(const_step, 2)
            for l, s in enumerate(LEVELS[:6]):
                m = mask_f[:, l, :].rearrange("p (n w) -> p n w", w=s)
                pool.affine_select(out=m, in_=m, compare_op=ALU.is_ge, fill=0.0, base=0,
                                   pattern=[[-2 * s, 64 // s], [0, s]], channel_multiplier=1).then_inc(const_step, 1)
            pool.wait_ge(const_step, 8)
            for l, s in enumerate(LEVELS[:6]):
                m = mask_f[:, l, :].rearrange("p (n w) -> p n w", w=s)
                pool.affine_select(out=m, in_=m, compare_op=ALU.is_ge, fill=0.0, base=s - 1,
                                   pattern=[[2 * s, 64 // s], [0, s]], channel_multiplier=-1).then_inc(const_step, 1)
            pool.wait_ge(const_step, 14)
            pool.tensor_copy(masks[:, :, 0:64], mask_f)
            pool.tensor_copy(masks[:, :, 64:128], mask_f).then_inc(const_done, 1)

            def load_rows(t, j, landed):
                pool.nop(nofuse=True)
                pool.dma_start(rows[:, j, :], x_rows[bass.ds(BLK * t + P * j, P), :]).then_inc(landed[j], 16)

            def transposed(t, j):
                pool.wait_ge(sc_done[0], SC_USES * t + 2 + SC_XT + j + 1)
                pool.wait_ge(sc_done[1], SC_USES * t + 2 + SC_XT + j + 1)

            def store_normed(t, j):
                pool.wait_ge(ln_out, 4 * (t - 1) + j + 1)
                pool.nop(nofuse=True)
                pool.dma_start(normed[bass.ds(BLK * (t - 1) + P * j, P), :], rows[:, j, :]).then_inc(stored[j], 16)

            def decayed_high(t, hp):
                if isinstance(t, int) and t == 0 and hp == 0:
                    pool.wait_ge(const_done, 3)
                else:
                    pool.wait_ge(y_ready, 8 * t + 2 * hp)
                pool.wait_ge(main_free[(J_Q + hp) % 4], turn(t, J_Q + hp) + 1)
                pool.wait_ge(exp_ready, 4 * t + 2 * hp + 1)
                pool.nop(nofuse=True)
                r = slice(64, P)
                for l, s in enumerate(LEVELS):
                    pool.tensor_tensor(q_lev[r, l, 1, :].rearrange("p (n w) -> p n w", w=s),
                                       q_lev[r, l, 0, :].rearrange("p (n w) -> p n w", w=s),
                                       level_view(qT[r, hp, :], s)[:, :, s:2 * s], ALU.mult).then_inc(high_step, 1)
                pool.wait_ge(high_step, 14 * t + 7 * hp + 7)
                pool.nop(nofuse=True)
                pool.memset(q_lev[r, :, 0, :], 0.0).then_inc(high_ready, 1)
                pool.wait_ge(high_ready, 2 * t + hp + 1)

            def y_low(t, i):
                src = xy_raw[:, i, :] if i < 2 else y_raw[:, i % 2, :]
                pool.wait_ge(yhi_ready, 8 * t + i + 1)
                pool.nop(nofuse=True)
                pool.tensor_tensor(y_lo[:, Y_TILE[i], :], src, y_hi[:, Y_TILE[i], :].bitcast(F32), ALU.subtract
                                   ).then_inc(y_ready, 1)

            for j in range(4):
                transposed(0, j)
                load_rows(1, j, x_landed)
            decayed_high(0, 0)
            y_low(0, 0)
            y_low(0, 1)
            decayed_high(0, 1)
            for i in range(2, 8):
                y_low(0, i)

            def mixer_block(t, next_t, landed):
                for j in range(4):
                    transposed(t, j)
                    load_rows(t - 1, j, res_landed)
                decayed_high(t, 0)
                y_low(t, 0)
                y_low(t, 1)
                for j in range(4):
                    store_normed(t, j)
                for j in range(4):
                    pool.wait_ge(stored[j], 16 * t)
                    load_rows(next_t, j, landed)
                decayed_high(t, 1)
                for i in range(2, 8):
                    y_low(t, i)

            with pool.Fori(1, NBLK - 1) as t:
                mixer_block(t, t + 1, x_landed)
            mixer_block(NBLK - 1, NBLK - 1, res_landed)
            mixer_blocks_over(pool)
            pool_first_rows(pool, ff, ln1_g, ln1_b, ln2_g, ln2_b)
            for j in range(4):
                store_normed(NBLK, j)
            for j in range(4):
                pool.wait_ge(stored[j], 16 * NBLK)
            pool.wait_ge(main_done, 28 * NBLK + 4)
            for c in range(NT):
                pool.dma_start(ff.acc[1][:, c, :], normed[HALF + P * c:HALF + P * c + P, :]
                               ).then_inc(ff.n_landed[1][c], 16)

        @block.tensor
        def _(pe):
            three = three_products(pe)

            def transposes(u_sc, j):
                for b in range(2):
                    pe.wait_ge(sc_free[b], u_sc)
                    for k in range(4):
                        src = rows[:, j, P * (4 * b + k):P * (4 * b + k) + P]
                        ins = pe.transpose(sc[b][:, P * k:P * k + P], src, ident[:, :])
                    ins.then_inc(sc_done[b], 1)

            def column_quarter(t, j, q):
                if q == 0:
                    pe.wait_ge(lo_done, slot_n(t, j) + 1)
                    pe.wait_ge(main_free[j % 4], turn(t, j))
                hi = w_hi[:, j % RING, :].rearrange("p (k n) -> p k n", k=KT)
                lo = w_lo[:, j % RING, :].rearrange("p (k n) -> p k n", k=KT)
                for k in (2 * q, 2 * q + 1):
                    ins = three(main[j % 4][:, :], hi[:, k, :], lo[:, k, :], xT_hi[:, k, :], xT_lo[:, k, :],
                                k == 0, k == KT - 1)
                if q == 3:
                    ins.then_inc(main_done, 1)

            def column_tile(t, j):
                for q in range(4):
                    column_quarter(t, j, q)

            def row_piece(t, j0, i, c, a_hi, a_lo, kt0):
                j = j0 + i
                if c == 0:
                    pe.wait_ge(lo_done, slot_n(t, j) + 1)
                if i == 0:
                    pe.wait_ge(main_free[c], turn(t, j0))
                hi = w_hi[:, j % RING, :].rearrange("p (k n) -> p k n", k=2)
                lo = w_lo[:, j % RING, :].rearrange("p (k n) -> p k n", k=2)
                tok = slice(P * c, P * c + P)
                for k in range(2):
                    ins = three(main[c][:, :], a_hi[:, kt0 + k, tok], a_lo[:, kt0 + k, tok], hi[:, k, :],
                                lo[:, k, :], i == 0 and k == 0, i == 3 and k == 1)
                if i == 3:
                    ins.then_inc(main_done, 1)
                elif c == 3:
                    ins.then_inc(row_used, 1)

            def output_piece(t, j0, i, c):
                if j0 == J_OUT_A and c == 0:
                    pe.wait_ge(y_ready, 8 * (t - 1) + K_READY[i])
                row_piece(t, j0, i, c, y_hi, y_lo, 2 * K_ORDER[i])

            def aux_turn(t, use):
                pe.wait_ge(aux_free, AUX_USES * t + use)

            def transpose_k(t, hp):
                pe.wait_ge(prep_ready, 2 * t + hp + 1)
                aux_turn(t, AUX_GLA + AUX_PAIR * hp)
                for c in range(NCH):
                    ins = pe.transpose(aux[:, P * c:P * c + P], k_dec[:, CH * c:CH * c + CH], ident[:, :])
                ins.then_inc(aux_done, 1)

            def score(t, hp, c):
                tok = slice(CH * c, CH * c + CH)
                if c == 0:
                    pe.wait_ge(prep_ready, 2 * t + hp + 1)
                    pe.wait_ge(high_ready, 2 * t + hp + 1)
                for l in range(7):
                    if l % 4 == 0:
                        pe.wait_ge(sc_free[l // 4], SC_USES * t + 2 + SC_GLA + 4 * hp + c)
                    if l == 0:
                        k_side = kT[:, hp, tok]
                    elif l < 6:
                        k_side = k_lev[:, l - 1, tok]
                    else:
                        k_side = k_top[:, c, :]
                    rows_out = P if l < 6 else 64
                    ins = pe.matmul(sc[l // 4][0:rows_out, P * (l % 4):P * (l % 4) + P], k_side,
                                    q_lev[:, l, :, 64 * c:64 * c + 64], start=True, stop=True)
                    if l == 3:
                        ins.then_inc(sc_done[0], 1)
                pe.matmul(sc[1][:, 384:386], gate[:, hp, tok], head_sum[:, :], start=True, stop=True
                          ).then_inc(sc_done[1], 1)

            def attend(t, hp, c):
                tok = slice(CH * c, CH * c + CH)
                for e in range(2):
                    pe.wait_ge(sc_free[e], SC_USES * t + 2 + SC_GLA + 4 * hp + c + 1)
                pe.wait_ge(ob_free, OB_USES * t + OB_GLA + 4 * hp + c)
                aux_turn(t, AUX_GLA + AUX_PAIR * hp + 1 + c)
                if hp == 0:
                    pe.wait_ge(main_free[c], turn(t, J_V) + 1)
                for e in range(2):
                    vh = v_rows[:, c, DV * (2 * hp + e):DV * (2 * hp + e) + DV]
                    pe.matmul(ob[:, DV * e:DV * e + CH], vh, probs[:, CH * e:CH * e + CH], start=True, stop=False)
                    ins = pe.matmul(ob[:, DV * e:DV * e + CH], state[:, hp, e, :], q_dec[:, tok],
                                    start=False, stop=True)
                ins.then_inc(ob_done, 1)
                ins = pe.matmul(aux[:, 0:2 * DV], k_dec_rows[:, c, :], v_rows[:, c, 2 * DV * hp:2 * DV * hp + 2 * DV],
                                start=True, stop=True)
                ins.then_inc(aux_done, 1)

            def mean_square(t, hp, e):
                aux_turn(t, AUX_GLA + AUX_PAIR * hp + 5 + e)
                pe.wait_ge(sq_ready, 4 * t + 2 * hp + e + 1)
                pe.matmul(aux[:, :], ones[:, :], rr[:, e, :], start=True, stop=True).then_inc(aux_done, 1)

            def xattn_score(t, j):
                if j == 0:
                    for i in range(2):
                        pe.wait_ge(main_free[i], turn(t, J_XQ) + 1)
                for e in range(2):
                    pe.wait_ge(sc_free[e], SC_USES * t + 2 + SC_XA + 2 * j)
                    for i in range(2):
                        ins = pe.matmul(sc[e][:, M * i:M * i + M], xqT[64 * e:64 * e + 64, i, P * j:P * j + P],
                                        mkT[64 * e:64 * e + 64, i, :], start=True, stop=True)
                    ins.then_inc(sc_done[e], 1)

            def xattn_transpose(t, j):
                pe.wait_ge(xp_ready, 4 * t + j + 1)
                for m in range(2):
                    pe.wait_ge(sc_free[m], SC_USES * t + 2 + SC_XA + 2 * j + 1)
                    for h in range(4):
                        ins = pe.transpose(sc[m][:, P * h:P * h + P], xp[:, h, P * m:P * m + P], ident[:, :])
                    ins.then_inc(sc_done[m], 1)

            def xattn_attend(t, j):
                pe.wait_ge(sc_free[0], SC_USES * t + 2 + SC_XA + 2 * j + 2)
                pe.wait_ge(sc_free[1], SC_USES * t + 2 + SC_XA + 2 * j + 2)
                pe.wait_ge(ob_free, OB_USES * t + OB_XA + j)
                for i in range(2):
                    for m in range(2):
                        ins = pe.matmul(ob[:, 2 * P * i:2 * P * i + 2 * P], mv[:, m, P * i:P * i + P],
                                        xpT[:, m, 2 * P * i:2 * P * i + 2 * P], start=(m == 0), stop=(m == 1))
                ins.then_inc(ob_done, 1)

            def mixer_block(t, with_out):
                def x_transposes(j):
                    pe.wait_ge(x_landed[j], 16 * (t + 1))
                    transposes(SC_USES * t + 2 + SC_XT + j, j)

                for j in range(4):
                    x_transposes(j)
                    if with_out:
                        for c in range(4):
                            output_piece(t, J_OUT_A, j, c)
                pe.wait_ge(sc_free[0], SC_USES * t + 2 + 4)
                pe.wait_ge(sc_free[1], SC_USES * t + 2 + 4)
                aux_turn(t, AUX_LOW)
                for k in range(KT):
                    pe.matmul(aux[0:2 * RANK, :], low[:, k, :], xT_lo[:, k, :], start=k == 0, stop=False)
                    ins = pe.matmul(aux[0:2 * RANK, :], low[:, k, :], xT_hi[:, k, :], start=False, stop=k == KT - 1)
                ins.then_inc(aux_done, 1)
                for i in range(2):
                    column_tile(t, J_XQ + i)
                    aux_turn(t, AUX_GATE + i)
                    pe.matmul(aux[:, :], w_gate[:, P * i:P * i + P], lowT, start=True, stop=True
                              ).then_inc(aux_done, 1)
                column_tile(t, J_Q)

                q_fill = [lambda q=q: column_quarter(t, J_Q + 1, q) for q in range(4)]
                out_fill = [lambda i=i, c=c: output_piece(t, J_OUT_B, i, c) for i in range(4) for c in range(4)]
                k_fill = [lambda q=q: column_quarter(t, J_K, q) for q in range(4)]
                if with_out:
                    fill = q_fill + out_fill + k_fill
                    parts = [(fill[6 * j:6 * j + 4], fill[6 * j + 4:6 * j + 6]) for j in range(4)]
                else:
                    fill = q_fill + k_fill + [lambda j=j, q=q: column_quarter(t, j, q)
                                              for j in (J_K + 1, J_C0) for q in range(4)]
                    parts = [(fill[4 * j:4 * j + 3], fill[4 * j + 3:4 * j + 4]) for j in range(4)]
                for j in range(4):
                    xattn_score(t, j)
                    for piece in parts[j][0]:
                        piece()
                    xattn_transpose(t, j)
                    for piece in parts[j][1]:
                        piece()
                    xattn_attend(t, j)

                for j in (J_K + 1, J_C0, J_H0) if with_out else (J_H0,):
                    column_tile(t, j)
                for i in range(4):
                    for c in range(4):
                        row_piece(t, J_V, i, c, xT_hi, xT_lo, 2 * i)
                    if i == 0:
                        transpose_k(t, 0)
                    if i == 2:
                        score(t, 0, 0)
                attend(t, 0, 0)

                done = 0

                def quarters(n):
                    nonlocal done
                    for i in range(done, done + n):
                        column_quarter(t, J_B0 + i // 4, i % 4)
                    done += n

                for c in range(1, NCH):
                    score(t, 0, c)
                    quarters(3)
                    attend(t, 0, c)
                quarters(3)
                mean_square(t, 0, 0)
                quarters(5)
                mean_square(t, 0, 1)
                quarters(1)
                for c in range(NCH):
                    score(t, 1, c)
                    if c == 0:
                        transpose_k(t, 1)
                    quarters(3)
                    attend(t, 1, c)
                quarters(1)
                mean_square(t, 1, 0)
                quarters(1)
                mean_square(t, 1, 1)
                assert done == 32

            pe.wait_ge(const_done, 1)
            for m in range(2):
                pe.wait_ge(mem_landed[m], 16)
                transposes(m, 2 + m)
            pe.wait_ge(sc_free[0], 2)
            pe.wait_ge(sc_free[1], 2)
            for i in range(2):
                pe.wait_ge(lo_done, i + 1)
                for k in range(KT):
                    hi = w_hi[:, i, P * k:P * k + P]
                    lo = w_lo[:, i, P * k:P * k + P]
                    ins = three(main[i][:, 0:M], hi, lo, xT_hi[:, k, 0:M], xT_lo[:, k, 0:M], k == 0, k == KT - 1)
                ins.then_inc(main_done, 1)
            for i in range(2):
                pe.wait_ge(lo_done, 3 + i)
                for m in range(2):
                    for k in range(4):
                        tok = slice(P * m, P * m + P)
                        ins = three(main[2 + m][:, 0:256], xT_hi[:, 4 * i + k, tok], xT_lo[:, 4 * i + k, tok],
                                    w_hi[:, 2 + i, 256 * k:256 * k + 256], w_lo[:, 2 + i, 256 * k:256 * k + 256],
                                    i == 0 and k == 0, i == 1 and k == 3)
                    if i == 1:
                        ins.then_inc(main_done, 1)
            pe.wait_ge(const_done, 2)
            pe.wait_ge(low_split, 1)
            mixer_block(0, False)
            with pe.Fori(1, NBLK) as t:
                mixer_block(t, True)
            pe.wait_ge(sc_free[0], SC_USES * NBLK + 2)
            pe.wait_ge(sc_free[1], SC_USES * NBLK + 2)
            pe.wait_ge(ob_free, OB_USES * NBLK)
            pe.wait_ge(aux_free, AUX_USES * NBLK)
            for piece in range(32):
                half, i, c = piece // 16, piece // 4 % 4, piece % 4
                if half == 0 and c == 0:
                    pe.wait_ge(y_ready, 8 * (NBLK - 1) + K_READY[i])
                row_piece(NBLK, 4 * half, i, c, y_hi, y_lo, 2 * K_ORDER[i])
                if 8 <= piece < 24:
                    transpose_rows(pe, ff, 0, piece - 8)

        def reuse(eng, t, j):
            if isinstance(t, int) and t == 0 and j < 16:
                if 4 <= j < 8:
                    eng.wait_ge(main_done, j - 3 if j < 6 else 4)
                elif j >= 12:
                    eng.wait_ge(main_done, slot_n(0, j - 8) + 1)
                return
            p = j - 4
            group = {0: 0, 8: 1, 16: 2}.get(p - p % 4)
            if isinstance(t, int) and t == NBLK and p >= 4:
                group = 1
            if p < 0 or group is None or p % 4 == 3:
                eng.wait_ge(main_done, slot_n(t, p) + 1)
            else:
                eng.wait_ge(row_used, 9 * t - 6 + 3 * group + p % 4 + 1)

        @block.scalar
        def _(act):
            def split(t, j):
                act.wait_ge(raw_landed[j % RAW], 16 * (raw_turn(t, j) + 1))
                reuse(act, t, j)
                act.activation(w_hi[:, j % RING, :], raw[:, j % RAW, :], ACT.Copy).then_inc(hi_done, 1)

            def next_split(t, j):
                split(*following(t, j))

            def tile_done(t, j):
                act.wait_ge(main_done, slot_n(t, j) + 1)

            def xT_part(n, uses, b, j):
                act.wait_ge(sc_done[b], uses + 1)
                act.activation(xT_hi[:, 4 * b:4 * b + 4, P * j:P * j + P],
                               sc[b][:, :].rearrange("p (k n) -> p k n", k=4), ACT.Copy).then_inc(xt_hi_done, 1)

            def gate_in(t, i):
                if i < 2 and isinstance(t, int) and t == 0:
                    act.wait_ge(const_done, 3)
                    return
                if i in (2, 5):
                    j = J_H0 if i == 2 else J_H1
                    act.wait_ge(main_free[j % 4], turn(t, j) + 1)
                else:
                    act.wait_ge(yraw_ready, 6 * t + {0: -1, 1: 0, 3: 2, 4: 3}[i])

            def y_part(t, i):
                if i < 2:
                    if not (isinstance(t, int) and t == 0):
                        tile_done(t, J_OUT_B + 3)
                    src = xy_raw[:, i, :]
                    act.wait_ge(xy_copied, 4 * t + 4)
                    act.wait_ge(ob_free, OB_USES * t + OB_XA + 4)
                else:
                    act.wait_ge(yraw_ready, 6 * t + i - 2 + 1)
                    src = y_raw[:, i % 2, :]
                act.activation(y_hi[:, Y_TILE[i], :], src, ACT.Copy).then_inc(yhi_ready, 1)

            def gate_copy(t, h, steps):
                act.wait_ge(aux_done, AUX_USES * t + AUX_GATE + h + 1)
                act.activation(gate[:, h, :], aux[:, :], ACT.Identity, bias=gate_bias[:, h:h + 1]
                               ).then_inc(aux_free, 1)
                act.wait_ge(aux_free, AUX_USES * t + AUX_GATE + h + 1)
                act.wait_ge(on_ready, 4 * t)
                steps.mark(act.activation(rr[:, h, :], gate[:, h, :], ACT.Abs))
                steps.settle()
                steps.mark(act.activation(rr[:, h, :], rr[:, h, :], ACT.Exp, scale=-1.0))
                steps.settle()
                act.activation(rr[:, h, :], rr[:, h, :], ACT.Ln, bias=ones[:, 0:1]).then_inc(soft_ready, 1)

            def exponentials(t, hp):
                act.wait_ge(expo_ready, 4 * t + 2 * hp + 1)
                act.activation(q_lev[:, :, 0, :], q_lev[:, :, 0, :], ACT.Exp, scale=1.0 / TAU).then_inc(exp_ready, 1)
                act.wait_ge(expo_ready, 4 * t + 2 * hp + 2)
                for l in range(1, 6):
                    view = level_view(k_lev[:, l - 1, :], LEVELS[l])[:, :, 0:LEVELS[l]]
                    act.activation(view, view, ACT.Exp, scale=1.0 / TAU)
                act.activation(k_top[:, :, :], k_top[:, :, :], ACT.Exp, scale=1.0 / TAU)
                act.activation(k_dec[:, :], k_dec[:, :], ACT.Exp, scale=1.0 / TAU)
                if hp == 1:
                    act.wait_ge(ob_done, OB_USES * t + OB_GLA + 4)
                act.activation(q_dec[:, :], gate[:, hp, :], ACT.Exp, scale=1.0 / TAU)
                act.activation(decay_last[:, :], b_last[:, hp, :], ACT.Exp, scale=1.0 / TAU).then_inc(exp_ready, 1)

            def copy_k_dec(t, hp):
                act.wait_ge(aux_done, AUX_USES * t + AUX_GLA + AUX_PAIR * hp + 1)
                act.activation(k_dec_rows[:, :, :], aux[:, :].rearrange("p (c n) -> p c n", c=NCH), ACT.Copy
                               ).then_inc(aux_free, 1)

            def copy_o(t, hp, c):
                act.wait_ge(ob_done, OB_USES * t + OB_GLA + 4 * hp + c + 1)
                if c == 0:
                    act.wait_ge(yraw_ready, 6 * t + 3 * hp)
                act.activation(oT[:, :, CH * c:CH * c + CH], ob[:, 0:2 * CH].rearrange("p (e n) -> p e n", e=2),
                               ACT.Copy).then_inc(ob_free, 1)

            def square(t, hp):
                act.wait_ge(on_ready, 4 * t + 2 * hp)
                act.wait_ge(ob_free, OB_USES * t + OB_GLA + 4 * hp + 4)
                for e in range(2):
                    act.activation(rr[:, e, :], oT[:, e, :], ACT.Square).then_inc(sq_ready, 1)

            def inverse_rms(t, hp, e):
                use = AUX_USES * t + AUX_GLA + AUX_PAIR * hp + 5 + e
                act.wait_ge(aux_done, use + 1)
                act.activation(rr[:, e, :], aux[:, :], ACT.Ln, scale=1.0 / DV, bias=eps_rms[:, :]).then_inc(aux_free, 1)
                act.wait_ge(aux_free, use + 1)
                act.activation(rr[:, e, :], rr[:, e, :], ACT.Exp, scale=-0.5).then_inc(rms_ready, 1)

            def sigmoid(t, g, steps):
                tile_done(t, GATE_TILE[g])
                use = (1, 2, 4, 5)[g]
                gate_in(t, use)
                buf = gin[:, use % 2, :]
                steps.mark(act.activation(buf, main[GATE_TILE[g] % 4][:, :], ACT.Exp, scale=-1.0))
                steps.settle()
                steps.mark(act.activation(buf, buf, ACT.Ln, bias=ones[:, 0:1]))
                steps.settle()
                act.activation(buf, buf, ACT.Exp, scale=-1.0).then_inc(gin_ready, 1)

            def conv_c(t, ch):
                j = (J_C0, J_C1)[ch]
                tile_done(t, j)
                gate_in(t, 3 * ch)
                act.activation(gin[:, ch, :], main[j % 4][:, :], ACT.Copy).then_inc(main_free[j % 4], 1)

            def copy_tile(t, j, dst, scale=1.0):
                tile_done(t, j)
                act.activation(dst, main[j % 4][:, :], ACT.Copy, scale=scale).then_inc(main_free[j % 4], 1)

            def normalise(t, c, steps):
                act.wait_ge(ln_stats, 4 * (t - 1) + c + 1)
                steps.mark(act.activation(rstd[:, c:c + 1], mvar[:, c, 1:2], ACT.Ln, bias=eps_ln[:, :]))
                steps.settle()
                steps.mark(act.activation(rstd[:, c:c + 1], rstd[:, c:c + 1], ACT.Exp, scale=-0.5))
                steps.settle()
                steps.mark(act.activation(nmean[:, c:c + 1], nmean[:, c:c + 1], ACT.Copy, scale=rstd[:, c:c + 1]))
                steps.settle()
                act.activation(rows[:, c, :], rows[:, c, :], ACT.Identity, scale=rstd[:, c:c + 1],
                               bias=nmean[:, c:c + 1]).then_inc(ln_out, 1)

            def mixer_block(t, with_out, steps):
                for j in range(4):
                    for b in range(2):
                        xT_part(8 * t + 4 + 2 * j + b, SC_USES * t + 2 + SC_XT + j, b, j)
                    if with_out and j > 0:
                        next_split(t, J_OUT_A + j - 1)
                    elif not with_out and j in (1, 2):
                        split(0, J_Q + j - 1)
                if with_out:
                    next_split(t, J_OUT_A + 3)
                act.wait_ge(aux_done, AUX_USES * t + AUX_LOW + 1)
                act.wait_ge(y_ready, 8 * t)
                act.activation(lowT, aux[0:2 * RANK, :], ACT.Copy).then_inc(aux_free, 1)
                for i in range(2):
                    copy_tile(t, J_XQ + i, xqT[:, i, :], DK ** -0.5)
                    gate_copy(t, i, steps)
                    next_split(t, J_XQ + i)
                copy_tile(t, J_Q, qT[:, 0, :], DK ** -0.5)
                next_split(t, J_Q)
                for j in range(4):
                    act.wait_ge(xmax_ready, 4 * t + j + 1)
                    for e in range(2):
                        act.wait_ge(sc_done[e], SC_USES * t + 2 + SC_XA + 2 * j + 1)
                        for i in range(2):
                            ins = act.activation(xp[:, 2 * i + e, :], sc[e][:, M * i:M * i + M], ACT.Exp,
                                                 bias=xnmax[:, 2 * e + i:2 * e + i + 1],
                                                 accum_out=xsum[:, 2 * i + e:2 * i + e + 1])
                        ins.then_inc(sc_free[e], 1)
                    act.wait_ge(sc_done[0], SC_USES * t + 2 + SC_XA + 2 * j + 2)
                    act.activation(xpT[:, 0, :], sc[0][:, :], ACT.Copy).then_inc(sc_free[0], 1)
                    if j == 0:
                        copy_tile(t, J_Q + 1, qT[:, 1, :], DK ** -0.5)
                        next_split(t, J_Q + 1)
                    elif with_out:
                        next_split(t, J_OUT_B + j - 1)
                    elif j >= 2:
                        copy_tile(t, J_K + j - 2, kT[:, j - 2, :])
                        next_split(t, J_K + j - 2)
                    if j == 1:
                        exponentials(t, 0)
                    act.wait_ge(ob_done, OB_USES * t + OB_XA + j + 1)
                    for e in range(2):
                        r = slice(64 * e, 64 * e + 64)
                        src = ob[r, :].rearrange("p (i e n) -> p i e n", i=2, e=2)[:, :, e, :]
                        ins = act.activation(xy_raw[r, :, P * j:P * j + P], src, ACT.Copy)
                        if e == 0:
                            ins.then_inc(xy_copied, 1)
                        else:
                            ins.then_inc(ob_free, 1)
                if with_out:
                    next_split(t, J_OUT_B + 3)
                    copy_tile(t, J_K, kT[:, 0, :])
                    next_split(t, J_K)
                y_part(t, 0)
                y_part(t, 1)
                if with_out:
                    copy_tile(t, J_K + 1, kT[:, 1, :])
                    next_split(t, J_K + 1)
                conv_c(t, 0)
                next_split(t, J_C0)
                next_split(t, J_H0)
                if with_out:
                    for c in range(4):
                        normalise(t, c, steps)
                copy_k_dec(t, 0)
                for i in range(3):
                    next_split(t, J_V + i)
                for i in range(4):
                    copy_tile(t, J_V + i, v_rows[:, i, :])
                next_split(t, J_V + 3)
                copy_o(t, 0, 0)
                copy_o(t, 0, 1)
                next_split(t, J_B0)
                copy_o(t, 0, 2)
                sigmoid(t, 0, steps)
                copy_o(t, 0, 3)
                next_split(t, J_G0)
                square(t, 0)
                exponentials(t, 1)
                inverse_rms(t, 0, 0)
                sigmoid(t, 1, steps)
                next_split(t, J_G1)
                y_part(t, 2)
                inverse_rms(t, 0, 1)
                next_split(t, J_C1)
                copy_k_dec(t, 1)
                y_part(t, 3)
                conv_c(t, 1)
                y_part(t, 4)
                copy_o(t, 1, 0)
                next_split(t, J_H1)
                copy_o(t, 1, 1)
                next_split(t, J_B1)
                copy_o(t, 1, 2)
                sigmoid(t, 2, steps)
                next_split(t, J_G2)
                copy_o(t, 1, 3)
                square(t, 1)
                inverse_rms(t, 1, 0)
                inverse_rms(t, 1, 1)
                y_part(t, 5)
                sigmoid(t, 3, steps)
                next_split(t, J_G3)
                y_part(t, 6)
                y_part(t, 7)

            nc.scalar.preload_act_table_set("natural_log_exp_and_others")
            split(0, 0)
            split(0, 1)
            for m in range(2):
                for b in range(2):
                    xT_part(0, m, b, m)
            split(0, 2)
            split(0, 3)
            act.wait_ge(small_landed, 16 * 7)
            act.activation(low[:, :, 0:RANK], low_raw, ACT.Copy).then_inc(low_hi_done, 1)
            for i in range(4):
                act.wait_ge(main_done, i + 1)
                if i < 2:
                    act.activation(mkT[:, i, :], main[i][:, 0:M], ACT.Copy).then_inc(main_free[i], 1)
                    split(0, 4 + i)
                else:
                    act.activation(mv[:, i - 2, :], main[i][:, 0:256], ACT.Copy).then_inc(main_free[i], 1)
            act.wait_ge(const_done, 2)
            steps = Steps(act, act_step, 0)
            mixer_block(0, False, steps)
            assert steps.count == ACT_STEPS_FIRST, steps.count
            with act.Fori(1, NBLK) as t:
                steps = Steps(act, act_step, ACT_STEPS_FIRST + ACT_STEPS * (t - 1))
                mixer_block(t, True, steps)
                assert steps.count == ACT_STEPS, steps.count
            steps = Steps(act, act_step, ACT_STEPS_FIRST + ACT_STEPS * (NBLK - 1))
            act.wait_ge(ff.col_landed, 32)
            split(NBLK, 4)
            for i in range(4):
                split(NBLK, 5 + i)
                for k in range(4):
                    x_high(act, ff, 0, 4 * i + k)
            for i in range(9, 12):
                split(NBLK, i)
            for c in range(4):
                normalise(NBLK, c, steps)

        @block.vector
        def _(dve):
            def split(t, j):
                dve.wait_ge(hi_done, slot_n(t, j) + 1)
                dve.tensor_tensor(w_lo[:, j % RING, :], raw[:, j % RAW, :], w_hi[:, j % RING, :].bitcast(F32),
                                  ALU.subtract).then_inc(lo_done, 1)

            def next_split(t, j):
                split(*following(t, j))

            def tile_done(t, j):
                dve.wait_ge(main_done, slot_n(t, j) + 1)

            def xT_part(n, b, j):
                dve.wait_ge(xt_hi_done, n + 1)
                dst = (slice(None), slice(4 * b, 4 * b + 4), slice(P * j, P * j + P))
                dve.tensor_tensor(xT_lo[dst], sc[b][:, :].rearrange("p (k n) -> p k n", k=4), xT_hi[dst].bitcast(F32),
                                  ALU.subtract).then_inc(sc_free[b], 1)

            def log_decays(t, hp, steps):
                dve.wait_ge(soft_ready, 2 * t + hp + 1)
                steps.mark(dve.scalar_tensor_tensor(out=gate[:, hp, :], in0=gate[:, hp, :], scalar=0.0,
                                                    in1=rr[:, hp, :], op0=ALU.min, op1=ALU.subtract))
                steps.settle()
                for c in range(NCH):
                    steps.mark(dve.tensor_tensor_scan(gate[:, hp, CH * c:CH * c + CH], ones[:, :],
                                                      gate[:, hp, CH * c:CH * c + CH], 0.0, ALU.mult, ALU.add))
                steps.settle()
                steps.mark(dve.tensor_copy(b_last[:, hp, :], gate[:, hp, CH - 1:BLK:CH]))
                steps.settle()

            def exponents_q(t, hp):
                for l, s in enumerate(LEVELS):
                    b = level_view(gate[:, hp, :], s)
                    ref = b[:, :, s - 1:s].to_broadcast([P, BLK // (2 * s), s])
                    ins = dve.tensor_tensor(q_lev[:, l, 0, :].rearrange("p (n w) -> p n w", w=s), b[:, :, s:2 * s], ref,
                                            ALU.subtract)
                ins.then_inc(expo_ready, 1)

            def k_side(l):
                s = LEVELS[l]
                return k_top[:, :, :] if l == 6 else level_view(k_lev[:, l - 1, :], s)[:, :, 0:s]

            def exponents_k(t, hp):
                for l in range(1, 7):
                    s = LEVELS[l]
                    b = level_view(gate[:, hp, :], s)
                    ref = b[:, :, s - 1:s].to_broadcast([P, BLK // (2 * s), s])
                    dve.tensor_tensor(k_side(l), ref, b[:, :, 0:s], ALU.subtract)
                dve.tensor_tensor(k_dec[:, :].rearrange("p (c w) -> p c w", w=CH),
                                  b_last[:, hp, :].unsqueeze(2).to_broadcast([P, NCH, CH]),
                                  gate[:, hp, :].rearrange("p (c w) -> p c w", w=CH), ALU.subtract
                                  ).then_inc(expo_ready, 1)

            def decayed(t, hp):
                for j in (J_Q + hp, J_K + hp):
                    dve.wait_ge(main_free[j % 4], turn(t, j) + 1)
                dve.wait_ge(exp_ready, 4 * t + 2 * hp + 1)
                for l, s in enumerate(LEVELS):
                    dst = q_lev[0:64, l, 0, :].rearrange("p (n w) -> p n w", w=s)
                    dve.tensor_tensor(dst, dst, level_view(qT[0:64, hp, :], s)[:, :, s:2 * s], ALU.mult)
                dve.wait_ge(exp_ready, 4 * t + 2 * hp + 2)
                dve.tensor_tensor(gate[:, hp, :], qT[:, hp, :], kT[:, hp, :], ALU.mult)
                for l, s in enumerate(LEVELS[1:], 1):
                    dve.tensor_tensor(k_side(l), k_side(l), level_view(kT[:, hp, :], s)[:, :, 0:s], ALU.mult)
                dve.tensor_tensor(q_dec[:, :], q_dec[:, :], qT[:, hp, :], ALU.mult)
                dve.tensor_tensor(k_dec[:, :], k_dec[:, :], kT[:, hp, :], ALU.mult).then_inc(prep_ready, 1)

            def mask_scores(t, hp, c, steps):
                use = SC_USES * t + 2 + SC_GLA + 4 * hp + c + 1
                if isinstance(t, int) and t == 0 and hp == 0 and c == 0:
                    dve.wait_ge(const_done, 3)
                dve.wait_ge(sc_done[1], use)
                for e in range(2):
                    steps.mark(dve.tensor_scalar(probs[:, CH * e:CH * e + CH], ident[:, :], sc[1][:, 384 + e:385 + e],
                                                 None, ALU.mult))
                steps.settle()
                steps.mark(dve.tensor_copy(level_view(probs[0:64, :], 64)[:, :, 64:128],
                                           sc[1][0:64, 256:384].rearrange("p (e n) -> p e n", e=2)))
                dve.wait_ge(sc_done[0], use)
                for l, s in enumerate(LEVELS[:6]):
                    if l == 4:
                        dve.wait_ge(sc_free[0], use)
                    else:
                        steps.settle()
                    dve.nop(nofuse=True)
                    ins = dve.copy_predicated(level_view(probs, s)[:, :, s:2 * s],
                                              masks[:, l, :].rearrange("p (n w) -> p n w", w=s),
                                              sc[l // 4][:, P * (l % 4):P * (l % 4) + P].rearrange(
                                                  "p (n w) -> p n w", w=s))
                    if l == 3:
                        ins.then_inc(sc_free[0], 1)
                    elif l == 5:
                        ins.then_inc(sc_free[1], 1)
                    else:
                        steps.mark(ins)

            def update_state(t, hp, c):
                dve.wait_ge(aux_done, AUX_USES * t + AUX_GLA + AUX_PAIR * hp + 1 + c + 1)
                for e in range(2):
                    r = slice(64 * e, 64 * e + 64)
                    ins = dve.scalar_tensor_tensor(out=state[r, hp, e, :], in0=state[r, hp, e, :],
                                                   scalar=decay_last[r, c:c + 1], in1=aux[r, DV * e:DV * e + DV],
                                                   op0=ALU.mult, op1=ALU.add)
                ins.then_inc(aux_free, 1)

            def normalise_o(t, hp):
                for e in range(2):
                    dve.wait_ge(rms_ready, 4 * t + 2 * hp + e + 1)
                    dve.scalar_tensor_tensor(out=oT[:, e, :], in0=oT[:, e, :], scalar=rms_g[:, 0:1], in1=rr[:, e, :],
                                             op0=ALU.mult, op1=ALU.mult).then_inc(on_ready, 1)

            def silu(t, g):
                j, use = GATE_TILE[g], (1, 2, 4, 5)[g]
                buf = gin[:, use % 2, :]
                dve.wait_ge(gin_ready, 4 * t + g + 1)
                dve.tensor_tensor(buf, buf, main[j % 4][:, :], ALU.mult).then_inc(main_free[j % 4], 1)

            def y_place(t, i):
                dve.wait_ge(y_ready, 8 * t + max(i - 1, 2))

            def gated(t, g):
                j, use, i = GATE_TILE[g], (1, 2, 4, 5)[g], (3, 4, 6, 7)[g]
                dve.wait_ge(on_ready, 4 * t + g + 1)
                dve.wait_ge(main_free[j % 4], turn(t, j) + 1)
                y_place(t, i)
                dve.tensor_tensor(y_raw[:, i % 2, :], oT[:, g % 2, :], gin[:, use % 2, :], ALU.mult
                                  ).then_inc(yraw_ready, 1)

            def conv_input(t, ch, j, steps):
                steps.mark(dve.tensor_copy(u[:, ch, 0:2], u[:, ch, BLK:BLK + 2]))
                steps.settle()
                tile_done(t, j)
                c_tile = J_C0 if ch == 0 else J_C1
                dve.wait_ge(main_free[c_tile % 4], turn(t, c_tile) + 1)
                dve.tensor_tensor(u[:, ch, 2:BLK + 2], gin[:, ch, :], main[j % 4][:, :], ALU.mult
                                  ).then_inc(main_free[j % 4], 1)

            def conv(t, ch, j, steps):
                acc = y_raw[:, ch, :]
                h_tile = J_H0 if ch == 0 else J_H1
                dve.wait_ge(main_free[h_tile % 4], turn(t, h_tile) + 1)
                y_place(t, 2 + 3 * ch)
                steps.mark(dve.tensor_scalar(acc, u[:, ch, 0:BLK], taps[:, ch, 0:1], None, ALU.mult))
                for w in (1, 2):
                    steps.settle()
                    steps.mark(dve.scalar_tensor_tensor(out=acc, in0=u[:, ch, w:w + BLK], scalar=taps[:, ch, w:w + 1],
                                                        in1=acc, op0=ALU.mult, op1=ALU.add))
                steps.settle()
                tile_done(t, j)
                dve.tensor_tensor(acc, acc, main[j % 4][:, :], ALU.mult).then_inc(yraw_ready, 1)
                dve.wait_ge(yraw_ready, 6 * t + 3 * ch + 1)
                dve.tensor_copy(xmax[:, 0:1], main[j % 4][:, 0:1]).then_inc(main_free[j % 4], 1)

            def output_tile(t, j0, half, c):
                tile_done(t, j0 + c)
                if half == 0:
                    dve.wait_ge(res_landed[c], 16 * t)
                dst = rows[:, c, 512 * half:512 * half + 512]
                dve.scalar_tensor_tensor(out=dst, in0=dst, scalar=ALPHA, in1=main[c][:, :],
                                         op0=ALU.mult, op1=ALU.add).then_inc(main_free[c], 1)

            def statistics(t, j0, c, steps):
                dve.wait_ge(main_free[c], turn(t, j0) + 1)
                for i in range(2):
                    steps.mark(dve.bn_stats(stats[:, c, i, :], rows[:, c, 512 * i:512 * i + 512]))
                steps.settle()
                dve.nop(nofuse=True)
                steps.mark(dve.bn_aggr(mvar[:, c, :], stats[:, c, :, :]))
                steps.settle()
                dve.tensor_scalar(nmean[:, c:c + 1], mvar[:, c, 0:1], -1.0, None, ALU.mult).then_inc(ln_stats, 1)

            def softmax_max(t, j, steps):
                for e in range(2):
                    dve.wait_ge(sc_done[e], SC_USES * t + 2 + SC_XA + 2 * j + 1)
                    steps.mark(dve.tensor_reduce(xmax[:, 2 * e:2 * e + 2],
                                                 sc[e][:, :].rearrange("p (i m) -> p i m", i=2), AX_X, ALU.max))
                steps.settle()
                dve.tensor_scalar(xnmax[:, :], xmax[:, :], -1.0, None, ALU.mult).then_inc(xmax_ready, 1)

            def softmax_norm(t, j, steps):
                for e in range(2):
                    dve.wait_ge(sc_free[e], SC_USES * t + 2 + SC_XA + 2 * j + 1)
                steps.mark(dve.reciprocal(xrec[:, :], xsum[:, :]))
                steps.settle()
                for h in range(4):
                    ins = dve.tensor_scalar(xp[:, h, :], xp[:, h, :], xrec[:, h:h + 1], None, ALU.mult)
                ins.then_inc(xp_ready, 1)

            def mixer_block(t, with_out, steps):
                for j in range(4):
                    for b in range(2):
                        xT_part(8 * t + 4 + 2 * j + b, b, j)
                    if with_out and j > 0:
                        next_split(t, J_OUT_A + j - 1)
                    elif not with_out and j in (1, 2):
                        split(0, J_Q + j - 1)
                if with_out:
                    next_split(t, J_OUT_A + 3)
                    for c in range(4):
                        output_tile(t, J_OUT_A, 0, c)
                for i in range(2):
                    next_split(t, J_XQ + i)
                    log_decays(t, i, steps)
                for j in range(4):
                    softmax_max(t, j, steps)
                    if j == 0:
                        exponents_q(t, 0)
                    if j == 3 and with_out:
                        output_tile(t, J_OUT_B, 1, 0)
                        output_tile(t, J_OUT_B, 1, 1)
                    softmax_norm(t, j, steps)
                    if j == 0:
                        next_split(t, J_Q)
                    if j == 3 and with_out:
                        output_tile(t, J_OUT_B, 1, 2)
                        output_tile(t, J_OUT_B, 1, 3)
                    dve.wait_ge(sc_done[1], SC_USES * t + 2 + SC_XA + 2 * j + 2)
                    dve.tensor_copy(xpT[:, 1, :], sc[1][:, :]).then_inc(sc_free[1], 1)
                    if j == 0:
                        exponents_k(t, 0)
                        next_split(t, J_Q + 1)
                    elif with_out:
                        next_split(t, J_OUT_B + j - 1)
                    elif j >= 2:
                        next_split(t, J_K + j - 2)
                if with_out:
                    next_split(t, J_OUT_B + 3)
                decayed(t, 0)
                if with_out:
                    next_split(t, J_K)
                    next_split(t, J_K + 1)
                    statistics(t, J_OUT_B, 0, steps)
                    statistics(t, J_OUT_B, 1, steps)
                next_split(t, J_C0)
                conv_input(t, 0, J_H0, steps)
                next_split(t, J_H0)
                if with_out:
                    statistics(t, J_OUT_B, 2, steps)
                    statistics(t, J_OUT_B, 3, steps)
                for i in range(3):
                    next_split(t, J_V + i)
                mask_scores(t, 0, 0, steps)
                next_split(t, J_V + 3)
                update_state(t, 0, 0)
                mask_scores(t, 0, 1, steps)
                update_state(t, 0, 1)
                mask_scores(t, 0, 2, steps)
                conv(t, 0, J_B0, steps)
                update_state(t, 0, 2)
                mask_scores(t, 0, 3, steps)
                silu(t, 0)
                exponents_q(t, 1)
                update_state(t, 0, 3)
                exponents_k(t, 1)
                next_split(t, J_B0)
                decayed(t, 1)
                next_split(t, J_G0)
                next_split(t, J_G1)
                mask_scores(t, 1, 0, steps)
                normalise_o(t, 0)
                gated(t, 0)
                silu(t, 1)
                gated(t, 1)
                update_state(t, 1, 0)
                mask_scores(t, 1, 1, steps)
                next_split(t, J_C1)
                conv_input(t, 1, J_H1, steps)
                update_state(t, 1, 1)
                mask_scores(t, 1, 2, steps)
                next_split(t, J_H1)
                update_state(t, 1, 2)
                mask_scores(t, 1, 3, steps)
                conv(t, 1, J_B1, steps)
                update_state(t, 1, 3)
                next_split(t, J_B1)
                silu(t, 2)
                next_split(t, J_G2)
                normalise_o(t, 1)
                gated(t, 2)
                silu(t, 3)
                gated(t, 3)
                next_split(t, J_G3)

            dve.memset(q_lev[:, :, 1, :], 0.0)
            dve.memset(k_lev[:, :, :], 0.0)
            dve.memset(state[:, :, :, :], 0.0)
            dve.memset(u[:, :, :], 0.0)
            for e in range(2):
                for h in range(2):
                    dve.memset(head_sum[64 * e:64 * e + 64, h:h + 1], float(e == h))
            split(0, 0)
            split(0, 1)
            for m in range(2):
                for b in range(2):
                    xT_part(2 * m + b, b, m)
            split(0, 2)
            split(0, 3)
            dve.wait_ge(low_hi_done, 1)
            dve.tensor_tensor(low[:, :, RANK:2 * RANK], low_raw, low[:, :, 0:RANK].bitcast(F32), ALU.subtract
                              ).then_inc(low_split, 1)
            split(0, 4)
            split(0, 5)
            dve.wait_ge(const_done, 2)
            steps = Steps(dve, dve_step, 0)
            mixer_block(0, False, steps)
            assert steps.count == DVE_STEPS_FIRST, steps.count
            with dve.Fori(1, NBLK) as t:
                steps = Steps(dve, dve_step, DVE_STEPS_FIRST + DVE_STEPS * (t - 1))
                mixer_block(t, True, steps)
                assert steps.count == DVE_STEPS, steps.count
            steps = Steps(dve, dve_step, DVE_STEPS_FIRST + DVE_STEPS * (NBLK - 1))
            split(NBLK, 4)
            for i in range(4):
                split(NBLK, 5 + i)
                for k in range(4):
                    if i == 1:
                        output_tile(NBLK, 0, 0, k)
                    x_low(dve, ff, 0, 4 * i + k)
            split(NBLK, 9)
            split(NBLK, 10)
            for c in range(4):
                output_tile(NBLK, 4, 1, c)
            split(NBLK, 11)
            for c in range(4):
                statistics(NBLK, 4, c, steps)

        feed_forward(nc, block, ff, w1_v, w2_rows, out_rows, KT, HALF, NT, NFB)


def transpose_rows(pe, ff, hf, i):
    group, k = i // 8, i % 8
    pe.wait_ge(ff.fm_free[i % 4], 4 * hf + i // 4)
    for c in range(4):
        if k == 0:
            pe.wait_ge(ff.n_landed[hf][4 * group + c], 16)
        ins = pe.transpose(ff.fm[i % 4][:, P * c:P * c + P], ff.acc[hf][:, 4 * group + c, P * k:P * k + P],
                           ff.ident[:, :])
    ins.then_inc(ff.fm_done, 1)


def transposes_before(hf, i):
    return 80 * hf + i


def x_high(act, ff, hf, i):
    group, k = i // 8, i % 8
    act.wait_ge(ff.fm_done, transposes_before(hf, i) + 1)
    if i >= 2:
        act.wait_ge(ff.x_lo_ready, 16 * hf + i - 1)
    act.activation(ff.relu[:, i % 2, :], ff.fm[i % 4][:, :], ACT.Identity, scale=ff.g1_col[:, k:k + 1],
                   bias=ff.b1_col[:, k:k + 1]).then_inc(ff.fm_free[i % 4], 1)
    act.wait_ge(ff.fm_free[i % 4], 4 * hf + i // 4 + 1)
    act.activation(ff.xT_hi[:, k, 512 * group:512 * group + 512], ff.relu[:, i % 2, :], ACT.Copy
                   ).then_inc(ff.x_hi_ready, 1)


def x_low(dve, ff, hf, i):
    group, k = i // 8, i % 8
    tok = slice(512 * group, 512 * group + 512)
    dve.wait_ge(ff.x_hi_ready, 16 * hf + i + 1)
    dve.tensor_tensor(ff.xT_lo[:, k, tok], ff.relu[:, i % 2, :], ff.xT_hi[:, k, tok].bitcast(F32), ALU.subtract
                      ).then_inc(ff.x_lo_ready, 1)


def init_rows(pool, ff, hf):
    rows = ff.acc[hf]
    count = rows.shape[1]
    for c in range(count):
        pool.wait_ge(ff.fm_done, transposes_before(hf, 8 * (c // 4) + 8))
        pool.wait_ge(ff.init_step, 2 + count * hf + c)
        pool.tensor_tensor(rows[:, c, :], rows[:, c, :], ff.g1_row[:, :], ALU.mult).then_inc(ff.init_step, 1)
        pool.wait_ge(ff.init_step, 2 + count * hf + c + 1)
        pool.tensor_tensor(rows[:, c, :], rows[:, c, :], ff.b1_row[:, :], ALU.add).then_inc(ff.init_done, 1)


def pool_first_rows(pool, ff, ln1_g, ln1_b, ln2_g, ln2_b):
    for dst, src in ((ff.g1_row, ln1_g), (ff.b1_row, ln1_b), (ff.g2_row, ln2_g), (ff.b2_row, ln2_b)):
        pool.dma_start(dst[:, :], src.to_broadcast([P, dst.shape[1]])).then_inc(ff.row_landed, 16)
    pool.wait_ge(ff.row_landed, 16 * 4)
    for row in (ff.g1_row, ff.b1_row):
        pool.tensor_scalar(row[:, :], row[:, :], ALPHA, None, ALU.mult).then_inc(ff.init_step, 1)
    init_rows(pool, ff, 0)


def feed_forward(nc, block, ff, w1_v, w2_rows, out_rows, KT, HALF, NT, NFB):
    sem, fm, fo, acc = ff.sem, ff.fm, ff.fo, ff.acc
    raw, w_hi, w_lo, ident, eps_ln = ff.raw, ff.w_hi, ff.w_lo, ff.ident, ff.eps_ln
    xT_hi, xT_lo, h_hi, h_lo, relu, h_raw = ff.xT_hi, ff.xT_lo, ff.h_hi, ff.h_lo, ff.relu, ff.h_raw
    g2_row, b2_row = ff.g2_row, ff.b2_row
    stats, mvar, rstd, nmean = ff.stats, ff.mvar, ff.rstd, ff.nmean
    raw_landed, hi_done, lo_done, fm_done = ff.raw_landed, ff.hi_done, ff.lo_done, ff.fm_done
    row_landed, init_done, x_lo_ready = ff.row_landed, ff.init_done, ff.x_lo_ready
    fo_done = sem("fo_done")
    fo_free = [sem(f"fo_free{i}") for i in range(4)]
    out_stored = [sem(f"out_stored{c}") for c in range(NT)]
    relu_ready, hraw_ready, h_hi_ready, h_lo_ready = (
        sem("relu_ready"), sem("hraw_ready"), sem("h_hi_ready"), sem("h_lo_ready"))
    stats_step, ln_stats, ln_step, ln_out = sem("f_stats_step"), sem("f_ln_stats"), sem("f_ln_step"), sem("f_ln_out")
    scale_step, out_ready = sem("scale_step"), sem("out_ready")
    tail_step, tail_ready, tail_stored = sem("tail_step"), sem("tail_ready"), sem("tail_stored")

    def slot_n(hf, fb, s):
        return ff.first_slot + 4 * NFB * hf + 4 * fb + s

    def fm_turn(hf, fb):
        return (4 + NFB) * hf + 4 + fb

    def fm_n(hf, fb, i):
        return 4 * fm_turn(hf, fb) + i

    def fo_n(hf, fb, i):
        return 16 * NFB * hf + 16 * fb + i

    def h_n(hf, fb, i):
        return 4 * NFB * hf + 4 * fb + i

    POOL_TAIL = 4

    @block.sync
    def _(sp):
        def load(hf, fb):
            for s in range(4):
                sp.wait_ge(lo_done, slot_n(hf, fb, s) - 1)
                if s < 2:
                    src = w1_v[:, :, bass.ds(2 * P * fb + P * s, P)]
                    dst = raw[:, s, :].rearrange("p (k n) -> p k n", k=KT)
                else:
                    src = w2_rows[bass.ds(2 * P * fb + P * (s - 2), P), :]
                    dst = raw[:, s - 2, :]
                sp.dma_start(dst, src).then_inc(raw_landed[s % 2], 16)

        with sp.Fori(0, NFB) as fb:
            load(0, fb)
        with sp.Fori(0, NFB) as fb:
            load(1, fb)
        for i, c in enumerate(range(POOL_TAIL, NT)):
            sp.wait_ge(tail_ready, i + 1)
            sp.dma_start(out_rows[HALF + P * c:HALF + P * c + P, :], acc[1][:, c, :]).then_inc(tail_stored, 16)
        sp.wait_ge(tail_stored, 16 * (NT - POOL_TAIL))

    @block.gpsimd
    def _(pool):
        init_rows(pool, ff, 1)
        for hf in range(2):
            for c in range(NT if hf == 0 else POOL_TAIL):
                pool.wait_ge(ln_out, NT * hf + c + 1)
                pool.tensor_tensor(acc[hf][:, c, :], acc[hf][:, c, :], g2_row[:, :], ALU.mult
                                   ).then_inc(scale_step, 1)
                pool.wait_ge(scale_step, NT * hf + c + 1)
                pool.tensor_tensor(acc[hf][:, c, :], acc[hf][:, c, :], b2_row[:, :], ALU.add
                                   ).then_inc(out_ready, 1)
                pool.wait_ge(out_ready, NT * hf + c + 1)
                pool.dma_start(out_rows[HALF * hf + P * c:HALF * hf + P * c + P, :], acc[hf][:, c, :]
                               ).then_inc(out_stored[c], 16)
        for c in range(NT):
            pool.wait_ge(out_stored[c], 32 if c < POOL_TAIL else 16)

    @block.tensor
    def _(pe):
        three = three_products(pe)

        def hidden(hf, fb):
            for i in range(4):
                f, sb_ = i % 2, i // 2
                if i < 2:
                    pe.wait_ge(lo_done, slot_n(hf, fb, f) + 1)
                pe.wait_ge(hraw_ready, h_n(hf, fb, 0))
                tok = slice(512 * sb_, 512 * sb_ + 512)
                for k in range(KT):
                    col = slice(P * k, P * k + P)
                    ins = three(fm[i][:, :], w_hi[:, f, col], w_lo[:, f, col], xT_hi[:, k, tok], xT_lo[:, k, tok],
                                k == 0, k == KT - 1)
                ins.then_inc(fm_done, 1)

        def project(hf, fb, i):
            c, d = i // 2, i % 2
            if i == 0:
                pe.wait_ge(lo_done, slot_n(hf, fb, 3) + 1)
            if i % 8 == 0:
                pe.wait_ge(h_lo_ready, h_n(hf, fb, 2 + i // 4))
            if isinstance(fb, int) and hf == 0 and fb == 0 and i < 4:
                pe.wait_ge(ff.main_free[i], ff.first_slot // 4)
            pe.wait_ge(fo_free[i % 4], 4 * NFB * hf + 4 * fb + i // 4)
            tok = slice(P * c, P * c + P)
            for f in range(2):
                ins = three(fo[i % 4][:, :], h_hi[:, f, tok], h_lo[:, f, tok],
                            w_hi[:, 2 + f, 512 * d:512 * d + 512], w_lo[:, 2 + f, 512 * d:512 * d + 512],
                            f == 0, f == 1)
            ins.then_inc(fo_done, 1)

        def both(hf, fb):
            hidden(hf, fb)
            for i in range(16):
                project(hf, fb, i)

        pe.wait_ge(x_lo_ready, 16)
        both(0, 0)
        with pe.Fori(1, NFB - 1) as fb:
            both(0, fb)
        hidden(0, NFB - 1)
        for i in range(16):
            project(0, NFB - 1, i)
            if i == 0:
                pe.wait_ge(hraw_ready, h_n(1, 0, 0))
            transpose_rows(pe, ff, 1, i)
        pe.wait_ge(x_lo_ready, 32)
        both(1, 0)
        with pe.Fori(1, NFB) as fb:
            both(1, fb)

    @block.scalar
    def _(act):
        def split(hf, fb, s):
            act.wait_ge(raw_landed[s % 2], 16 * (ff.first_slot // 2 + 2 * NFB * hf + 2 * fb + s // 2 + 1))
            if s < 2 and isinstance(fb, int) and fb == 0:
                act.wait_ge(fm_done, fm_n(0, NFB - 1, s + 3))
            elif s < 2:
                act.wait_ge(fm_done, fm_n(hf, fb - 1, s + 3))
            else:
                act.wait_ge(fo_done, fo_n(hf, fb, 0))
            act.activation(w_hi[:, s, :], raw[:, s % 2, :], ACT.Copy).then_inc(hi_done, 1)

        def hidden(hf, fb):
            for i in range(4):
                f, sb_ = i % 2, i // 2
                act.wait_ge(fm_done, fm_n(hf, fb, i) + 1)
                act.activation(relu[:, i % 2, :], fm[i][:, :], ACT.Relu).then_inc(relu_ready, 1)
                act.wait_ge(hraw_ready, h_n(hf, fb, i) + 1)
                act.activation(h_hi[:, f, 512 * sb_:512 * sb_ + 512], h_raw[:, i % 2, :], ACT.Copy
                               ).then_inc(h_hi_ready, 1)

        def normalise(hf, c):
            act.wait_ge(ln_stats, NT * hf + c + 1)
            act.activation(rstd[:, c:c + 1], mvar[:, c, 1:2], ACT.Ln, bias=eps_ln[:, :]).then_inc(ln_step, 1)
            act.wait_ge(ln_step, 3 * (NT * hf + c) + 1)
            act.activation(rstd[:, c:c + 1], rstd[:, c:c + 1], ACT.Exp, scale=-0.5).then_inc(ln_step, 1)
            act.wait_ge(ln_step, 3 * (NT * hf + c) + 2)
            act.activation(nmean[:, c:c + 1], nmean[:, c:c + 1], ACT.Copy, scale=rstd[:, c:c + 1]
                           ).then_inc(ln_step, 1)
            act.wait_ge(ln_step, 3 * (NT * hf + c) + 3)
            act.activation(acc[hf][:, c, :], acc[hf][:, c, :], ACT.Identity, scale=rstd[:, c:c + 1],
                           bias=nmean[:, c:c + 1]).then_inc(ln_out, 1)

        def block_but_last(hf, fb):
            if not (isinstance(fb, int) and hf == 0):
                split(hf, fb, 2)
                split(hf, fb, 3)
            hidden(hf, fb)
            split(hf, fb + 1, 0)
            split(hf, fb + 1, 1)

        for hf in range(2):
            block_but_last(hf, 0)
            if hf == 1:
                for c in range(NT):
                    normalise(0, c)
            with act.Fori(1, NFB - 1) as fb:
                block_but_last(hf, fb)
            split(hf, NFB - 1, 2)
            split(hf, NFB - 1, 3)
            hidden(hf, NFB - 1)
            if hf == 0:
                split(1, 0, 0)
                split(1, 0, 1)
                act.wait_ge(hraw_ready, h_n(1, 0, 0))
                for i in range(16):
                    x_high(act, ff, 1, i)
        for c in range(NT):
            normalise(1, c)

    @block.vector
    def _(dve):
        def split(hf, fb, s):
            dve.wait_ge(hi_done, slot_n(hf, fb, s) + 1)
            dve.tensor_tensor(w_lo[:, s, :], raw[:, s % 2, :], w_hi[:, s, :].bitcast(F32), ALU.subtract
                              ).then_inc(lo_done, 1)

        def hidden_tile(hf, fb, i):
            f, sb_ = i % 2, i // 2
            tok = slice(512 * sb_, 512 * sb_ + 512)
            dve.wait_ge(relu_ready, h_n(hf, fb, i) + 1)
            if not (isinstance(fb, int) and hf == 0 and fb == 0 and i < 2):
                dve.wait_ge(h_lo_ready, h_n(hf, fb, i) - 1)
            dve.scalar_tensor_tensor(out=h_raw[:, i % 2, :], in0=fm[i][:, :], scalar=0.0,
                                     in1=relu[:, i % 2, :], op0=ALU.max, op1=ALU.mult
                                     ).then_inc(hraw_ready, 1)
            dve.wait_ge(h_hi_ready, h_n(hf, fb, i) + 1)
            dve.tensor_tensor(h_lo[:, f, tok], h_raw[:, i % 2, :], h_hi[:, f, tok].bitcast(F32),
                              ALU.subtract).then_inc(h_lo_ready, 1)

        def add(hf, fb, i):
            c, d = i // 2, i % 2
            dve.wait_ge(fo_done, fo_n(hf, fb, i) + 1)
            if isinstance(fb, int) and fb == 0 and d == 0:
                dve.wait_ge(init_done, NT * hf + c + 1)
            dst = acc[hf][:, c, 512 * d:512 * d + 512]
            dve.tensor_tensor(dst, dst, fo[i % 4][:, :], ALU.add).then_inc(fo_free[i % 4], 1)

        def statistics(hf, c):
            for d in range(2):
                i = 2 * c + d
                dve.wait_ge(fo_free[i % 4], 4 * NFB * (hf + 1) - 4 + i // 4 + 1)
                dve.bn_stats(stats[:, c, d, :], acc[hf][:, c, 512 * d:512 * d + 512]).then_inc(stats_step, 1)
            dve.wait_ge(stats_step, 3 * (NT * hf + c) + 2)
            dve.bn_aggr(mvar[:, c, :], stats[:, c, :, :]).then_inc(stats_step, 1)
            dve.wait_ge(stats_step, 3 * (NT * hf + c) + 3)
            dve.tensor_scalar(nmean[:, c:c + 1], mvar[:, c, 0:1], -1.0, None, ALU.mult).then_inc(ln_stats, 1)

        def block_but_last(hf, fb):
            if not (isinstance(fb, int) and hf == 0):
                split(hf, fb, 2)
                split(hf, fb, 3)
            for i in range(4):
                hidden_tile(hf, fb, i)
                if hf == 1 and isinstance(fb, int):
                    statistics(0, 2 * i)
                    statistics(0, 2 * i + 1)
            for i in range(16):
                add(hf, fb, i)
                if i == 3:
                    split(hf, fb + 1, 0)
                if i == 5:
                    split(hf, fb + 1, 1)

        for hf in range(2):
            block_but_last(hf, 0)
            with dve.Fori(1, NFB - 1) as fb:
                block_but_last(hf, fb)
            split(hf, NFB - 1, 2)
            split(hf, NFB - 1, 3)
            for i in range(4):
                hidden_tile(hf, NFB - 1, i)
            if hf == 0:
                split(1, 0, 0)
                split(1, 0, 1)
                for i in range(16):
                    add(0, NFB - 1, i)
                    x_low(dve, ff, 1, i)
        for c in range(NT):
            add(1, NFB - 1, 2 * c)
            add(1, NFB - 1, 2 * c + 1)
            statistics(1, c)
        dve.wait_ge(row_landed, 16 * 4)
        for i, c in enumerate(range(POOL_TAIL, NT)):
            dve.wait_ge(ln_out, NT + c + 1)
            dve.tensor_tensor(acc[1][:, c, :], acc[1][:, c, :], g2_row[:, :], ALU.mult).then_inc(tail_step, 1)
            dve.wait_ge(tail_step, i + 1)
            dve.tensor_tensor(acc[1][:, c, :], acc[1][:, c, :], b2_row[:, :], ALU.add).then_inc(tail_ready, 1)


_INS = ["x", "mem", "w_in", "w_gate_up", "b_gate", "conv_w", "gla_norm_g", "w_mem_kv", "w_out",
        "ln1_g", "ln1_b", "w_ff1", "w_ff2", "ln2_g", "ln2_b"]


def kernel(**inputs):
    import numpy as _np
    import concourse.bacc as _bacc
    from concourse import mybir as _mybir
    from concourse.bass_utils import run_bass_kernel_spmd as _run

    nc = _bacc.Bacc("TRN2", target_bir_lowering=False, num_devices=1,
                    dynamic_dma_scratch_size=8192)
    arrays, args = {}, []
    for name in _INS:
        a = _np.ascontiguousarray(inputs[name])
        arrays[f"in_{name}_dram"] = a
        args.append(nc.dram_tensor(f"in_{name}_dram", a.shape, _mybir.dt.from_np(a.dtype), kind="ExternalInput").ap())
    B, S, D = inputs["x"].shape
    args.append(nc.dram_tensor("normed_dram", (S, D), _mybir.dt.float32, kind="Internal").ap())
    args.append(nc.dram_tensor("out_0_dram", (B, S, D), _mybir.dt.float32, kind="ExternalOutput").ap())
    hybrid_layer(nc, *args)
    r = _run(nc, [arrays], core_ids=[0])
    return r.results[0]["out_0_dram"]
```
